# Optimizing a Trainium2 kernel written in Bass

```python
import jax, jax.numpy as jnp
from jax import lax
import numpy as np

D_MODEL = 1024
BATCH = 1
SEQ = 256
DEPTH = 1

D_MIX = D_MODEL
D_CONV = D_MIX // 2
D_RET = D_MIX - D_CONV
N_RET_HEADS = 4
RET_HEAD_DIM = D_RET // N_RET_HEADS
CONV_WIDTH = 31
CHUNK = 128
D_FF = ((8 * D_MODEL // 3 + 255) // 256) * 256
D_PLE = 256
ROPE_BASE = 10000.0
EPS = 1e-6
D_IN = 2 * D_CONV + 4 * D_RET


def rmsnorm(x, w):
    xf = x.astype(jnp.float32)
    y = xf * lax.rsqrt(jnp.mean(xf * xf, axis=-1, keepdims=True) + EPS)
    return (y * w.astype(jnp.float32)).astype(x.dtype)

def layernorm(x, w, b):
    xf = x.astype(jnp.float32)
    mu = jnp.mean(xf, axis=-1, keepdims=True)
    var = jnp.mean(jnp.square(xf - mu), axis=-1, keepdims=True)
    y = (xf - mu) * lax.rsqrt(var + EPS)
    return (y * w.astype(jnp.float32) + b.astype(jnp.float32)).astype(x.dtype)

def rotary(t, pos):
    half = t.shape[-1] // 2
    freqs = ROPE_BASE ** (-jnp.arange(half, dtype=jnp.float32) / half)
    ang = pos[:, None] * freqs[None, :]
    cos = jnp.cos(ang)[None, :, None, :]
    sin = jnp.sin(ang)[None, :, None, :]
    t1, t2 = t[..., :half], t[..., half:]
    return jnp.concatenate([t1 * cos - t2 * sin, t1 * sin + t2 * cos], axis=-1)

def conformer_conv(u_a, u_b, dw_w, dw_b, ln_w, ln_b):
    u = u_a * jax.nn.sigmoid(u_b)
    y = lax.conv_general_dilated(
        u, dw_w[:, None, :].astype(u.dtype), window_strides=(1,),
        padding=[(CONV_WIDTH - 1, 0)],
        dimension_numbers=("NWC", "WIO", "NWC"),
        feature_group_count=D_CONV)
    y = y + dw_b
    y = layernorm(y, ln_w, ln_b)
    return jax.nn.silu(y)

def chunkwise_retention(q, k, v):
    b, s, h, dh = q.shape
    nc = s // CHUNK
    log_g = jnp.log(1.0 - 2.0 ** (-5.0 - jnp.arange(h, dtype=jnp.float32)))
    idx = jnp.arange(CHUNK, dtype=jnp.float32)
    rel = idx[:, None] - idx[None, :]
    decay_in = jnp.where(rel >= 0, jnp.exp(log_g[:, None, None] * jnp.maximum(rel, 0.0)), 0.0)
    q_decay = jnp.exp(log_g[:, None] * (idx + 1.0))[None, :, :, None]
    k_decay = jnp.exp(log_g[:, None] * (CHUNK - 1.0 - idx))[None, :, :, None]
    chunk_decay = jnp.exp(log_g * CHUNK)[None, :, None, None]

    def to_chunks(t):
        return t.reshape(b, nc, CHUNK, h, dh).transpose(1, 0, 3, 2, 4)

    def step(state, qkv):
        qc, kc, vc = qkv
        scores = jnp.einsum("bhid,bhjd->bhij", qc, kc) * decay_in[None]
        inner = jnp.einsum("bhij,bhjd->bhid", scores, vc)
        cross = jnp.einsum("bhid,bhde->bhie", qc, state) * q_decay
        new_state = state * chunk_decay + jnp.einsum("bhjd,bhje->bhde", kc * k_decay, vc)
        return new_state, inner + cross

    state0 = jnp.zeros((b, h, dh, dh), jnp.float32)
    _, out = lax.scan(step, state0, (to_chunks(q), to_chunks(k), to_chunks(v)))
    return out.transpose(1, 0, 3, 2, 4).reshape(b, s, h, dh)

def retention_group(hq, hk, hv, hg):
    b, s, _ = hq.shape
    shp = (b, s, N_RET_HEADS, RET_HEAD_DIM)
    pos = jnp.arange(s, dtype=jnp.float32)
    q = rotary(hq.reshape(shp).astype(jnp.float32), pos)
    k = rotary(hk.reshape(shp).astype(jnp.float32), pos) * (RET_HEAD_DIM ** -0.5)
    v = hv.reshape(shp).astype(jnp.float32)
    o = chunkwise_retention(q, k, v)
    o = o * lax.rsqrt(jnp.mean(o * o, axis=-1, keepdims=True) + EPS)
    o = o.reshape(b, s, D_RET).astype(hg.dtype)
    return jax.nn.silu(hg) * o

def first_inputs(seed: int = 0) -> dict:
    key = jax.random.key(seed)
    ks = jax.random.split(key, 20)
    f32 = jnp.float32

    def nrm(k, shape, scale):
        return jax.random.normal(k, shape, f32) * scale

    def gain(k, shape):
        return 1.0 + 0.01 * jax.random.normal(k, shape, f32)

    L = DEPTH
    return {
        "x": nrm(ks[0], (BATCH, SEQ, D_MODEL), 1.0),
        "p": nrm(ks[1], (DEPTH, BATCH, SEQ, D_PLE), 1.0),
        "mix_pre_norm": gain(ks[2], (L, D_MODEL)),
        "w_in": nrm(ks[3], (L, D_MODEL, D_IN), D_MODEL ** -0.5),
        "conv_dw_w": nrm(ks[4], (L, CONV_WIDTH, D_CONV), CONV_WIDTH ** -0.5),
        "conv_dw_b": nrm(ks[5], (L, D_CONV), 0.01),
        "conv_ln_w": gain(ks[6], (L, D_CONV)),
        "conv_ln_b": nrm(ks[7], (L, D_CONV), 0.01),
        "w_out": nrm(ks[8], (L, D_MIX, D_MODEL), D_MIX ** -0.5),
        "mix_post_norm": gain(ks[9], (L, D_MODEL)),
        "ffn_pre_norm": gain(ks[10], (L, D_MODEL)),
        "w_ffn_gate": nrm(ks[11], (L, D_MODEL, D_FF), D_MODEL ** -0.5),
        "w_ffn_up": nrm(ks[12], (L, D_MODEL, D_FF), D_MODEL ** -0.5),
        "w_ffn_down": nrm(ks[13], (L, D_FF, D_MODEL), D_FF ** -0.5),
        "ffn_post_norm": gain(ks[14], (L, D_MODEL)),
        "w_ple_gate": nrm(ks[15], (L, D_MODEL, D_MODEL), D_MODEL ** -0.5),
        "w_ple_proj": nrm(ks[16], (L, D_PLE, D_MODEL), D_PLE ** -0.5),
        "ple_post_norm": gain(ks[17], (L, D_MODEL)),
    }

def first_block(x, p, mix_pre_norm, w_in, conv_dw_w, conv_dw_b, conv_ln_w, conv_ln_b,
              w_out, mix_post_norm, ffn_pre_norm, w_ffn_gate, w_ffn_up, w_ffn_down,
              ffn_post_norm, w_ple_gate, w_ple_proj, ple_post_norm):
    for i in range(DEPTH):
        h = rmsnorm(x, mix_pre_norm[i])
        u = h @ w_in[i]
        c0, c1 = D_CONV, 2 * D_CONV
        u_a, u_b = u[..., :c0], u[..., c0:c1]
        hq = u[..., c1:c1 + D_RET]
        hk = u[..., c1 + D_RET:c1 + 2 * D_RET]
        hv = u[..., c1 + 2 * D_RET:c1 + 3 * D_RET]
        hg = u[..., c1 + 3 * D_RET:]
        y_conv = conformer_conv(u_a, u_b, conv_dw_w[i], conv_dw_b[i], conv_ln_w[i], conv_ln_b[i])
        y_ret = retention_group(hq, hk, hv, hg)
        y = jnp.concatenate([y_conv, y_ret], axis=-1) @ w_out[i]
        x = x + rmsnorm(y, mix_post_norm[i])
        h = rmsnorm(x, ffn_pre_norm[i])
        f = (jax.nn.silu(h @ w_ffn_gate[i]) * (h @ w_ffn_up[i])) @ w_ffn_down[i]
        x = x + rmsnorm(f, ffn_post_norm[i])
        e = jax.nn.sigmoid(x @ w_ple_gate[i]) * (p[i].astype(x.dtype) @ w_ple_proj[i])
        x = x + rmsnorm(e, ple_post_norm[i])
    return x


GRID_W = 64
MEM_LEN = 256
HG_HEADS = 8
HG_DIM = 128
HG_WIDTH = HG_HEADS * HG_DIM
HG_CHUNK = 64
NA_HEADS = 8
NA_DIM = 64
NA_WIDTH = NA_HEADS * NA_DIM
NA_KH = 8
NA_KW = 16
CA_HEADS = 4
CA_DIM = 128
CA_WIDTH = CA_HEADS * CA_DIM
N_BRANCH = 3
D_FF_2 = 2816
CONV_W = 3
F_FLOOR = 1e-12
MASK_NEG = -1e30
IN_SIZES = (HG_WIDTH,) * 5 + (NA_WIDTH,) * 3 + (CA_WIDTH,) + (D_MODEL,) * N_BRANCH
IN_COLS = sum(IN_SIZES)


def rmsnorm_2(x, g):
    xf = x.astype(jnp.float32)
    y = xf * lax.rsqrt(jnp.mean(xf * xf, axis=-1, keepdims=True) + EPS)
    return (y * g.astype(jnp.float32)).astype(x.dtype)

def to_heads(a, n):
    b, t, w = a.shape
    return a.reshape(b, t, n, w // n).transpose(0, 2, 1, 3)

def split_cols(a):
    return jnp.split(a, np.cumsum(IN_SIZES)[:-1].tolist(), axis=-1)

def gla_chunk_scan(q, k, v, log_f):
    b, h, t, dk = q.shape
    dv = v.shape[-1]
    n = t // HG_CHUNK

    def chunks(a):
        return jnp.moveaxis(a.reshape(b, h, n, HG_CHUNK, a.shape[-1]), 2, 0)

    tri = jnp.tril(jnp.ones((HG_CHUNK, HG_CHUNK), dtype=bool))[:, :, None]

    def step(S, inp):
        qc, kc, vc, gc = inp
        cum = jnp.cumsum(gc, axis=2)
        diff = cum[:, :, :, None, :] - cum[:, :, None, :, :]
        decay = jnp.where(tri, jnp.exp(jnp.where(tri, diff, 0.0)), 0.0)
        scores = jnp.einsum('bhtk,bhsk,bhtsk->bhts', qc, kc, decay)
        o = jnp.einsum('bhts,bhsv->bhtv', scores, vc) + jnp.einsum('bhtk,bhkv->bhtv', qc * jnp.exp(cum), S)
        last = cum[:, :, -1:, :]
        S = jnp.exp(last[:, :, 0, :, None]) * S + jnp.einsum('bhsk,bhsv->bhkv', kc * jnp.exp(last - cum), vc)
        return S, o

    S0 = jnp.zeros((b, h, dk, dv), q.dtype)
    _, o = lax.scan(step, S0, (chunks(q), chunks(k), chunks(v), chunks(log_f)))
    return jnp.moveaxis(o, 0, 2).reshape(b, h, t, dv)

def hgrn2_branch(zq, zi, zf_fwd, zf_bwd, zg, lb, gnorm, w_o):
    f32 = jnp.float32
    dt = zq.dtype
    b, t = zq.shape[:2]
    q = to_heads(jax.nn.silu(zq.astype(f32)) * HG_DIM ** -0.5, HG_HEADS)
    v = to_heads(zi.astype(f32), HG_HEADS)

    def one_direction(zf, lb_d, reverse):
        zf = zf.astype(f32)
        f = lb_d + (1.0 - lb_d) * jax.nn.sigmoid(zf)
        log_f = jnp.log(jnp.maximum(f, F_FLOOR))
        k = (1.0 - lb_d) * jax.nn.sigmoid(-zf)
        ins = (q, to_heads(k, HG_HEADS), v, to_heads(log_f, HG_HEADS))
        if reverse:
            ins = tuple(jnp.flip(a, axis=2) for a in ins)
            return jnp.flip(gla_chunk_scan(*ins), axis=2)
        return gla_chunk_scan(*ins)

    o = one_direction(zf_fwd, lb[0], False) + one_direction(zf_bwd, lb[1], True)
    o = rmsnorm_2(o.transpose(0, 2, 1, 3), gnorm)
    gate = jax.nn.silu(zg.astype(f32)).reshape(o.shape)
    o = (o * gate).reshape(b, t, HG_WIDTH).astype(dt)
    return o @ w_o

def neighbourhood_attention(zq, zk, zv, rpb, w_o):
    b, t, _ = zq.shape
    rows = t // GRID_W
    kh = min(NA_KH, rows)
    r = np.arange(rows)
    row_idx = np.clip(r - kh // 2, 0, rows - kh)[:, None] + np.arange(kh)[None, :]
    c = np.arange(GRID_W)
    col_start = np.clip(c - NA_KW // 2, 0, GRID_W - NA_KW)
    col_mask = (c[None, :] >= col_start[:, None]) & (c[None, :] < col_start[:, None] + NA_KW)
    dr = row_idx - r[:, None] + (NA_KH - 1)
    dc = np.clip(c[None, :] - c[:, None], -(NA_KW - 1), NA_KW - 1) + (NA_KW - 1)
    bias = rpb[:, dr[:, None, :, None], dc[None, :, None, :]]

    def grid(a):
        return a.reshape(b, rows, GRID_W, NA_HEADS, NA_DIM)

    q = grid(zq) * NA_DIM ** -0.5
    k = grid(zk)[:, row_idx]
    v = grid(zv)[:, row_idx]
    s = jnp.einsum('brqhd,brkwhd->bhrqkw', q, k).astype(jnp.float32) + bias.astype(jnp.float32)
    s = jnp.where(col_mask[:, None, :], s, MASK_NEG)
    p = jax.nn.softmax(s.reshape(b, NA_HEADS, rows, GRID_W, kh * GRID_W), axis=-1)
    p = p.reshape(s.shape).astype(zv.dtype)
    o = jnp.einsum('bhrqkw,brkwhd->brqhd', p, v).reshape(b, t, NA_WIDTH)
    return o @ w_o

def memory_cross_attention(zq, mem_n, w_kv, w_o):
    b, t, _ = zq.shape
    m = mem_n.shape[1]
    q = zq.reshape(b, t, CA_HEADS, CA_DIM) * CA_DIM ** -0.5
    kv = (mem_n @ w_kv).reshape(b, m, 2, CA_HEADS, CA_DIM)
    s = jnp.einsum('bthd,bmhd->bhtm', q, kv[:, :, 0]).astype(jnp.float32)
    p = jax.nn.softmax(s, axis=-1).astype(zq.dtype)
    o = jnp.einsum('bhtm,bmhd->bthd', p, kv[:, :, 1]).reshape(b, t, CA_WIDTH)
    return o @ w_o

def conv_ffn(h, w_up, conv_w, conv_b, w_down):
    t = h.shape[1]
    u = h @ w_up
    up = jnp.pad(u, ((0, 0), (CONV_W // 2, CONV_W // 2), (0, 0)))
    u = sum(up[:, j:j + t] * conv_w[j] for j in range(CONV_W)) + conv_b
    a, g = jnp.split(u, 2, axis=-1)
    return (jax.nn.gelu(a) * g) @ w_down

def second_inputs(seed: int = 0) -> dict:
    key = jax.random.key(seed)
    ks = jax.random.split(key, 19)

    def nrm(k, shape, scale):
        return jax.random.normal(k, shape, jnp.float32) * scale

    return {
        'x': nrm(ks[0], (BATCH, SEQ, D_MODEL), 1.0),
        'mem': nrm(ks[1], (BATCH, MEM_LEN, D_MODEL), 1.0),
        'norm_mix': 1.0 + nrm(ks[2], (DEPTH, D_MODEL), 0.02),
        'w_in': nrm(ks[3], (DEPTH, D_MODEL, IN_COLS), D_MODEL ** -0.5),
        'hg_lb_logits': nrm(ks[4], (DEPTH, 2, HG_WIDTH), 1.0),
        'hg_gnorm': 1.0 + nrm(ks[5], (DEPTH, HG_DIM), 0.02),
        'w_hg_o': nrm(ks[6], (DEPTH, HG_WIDTH, D_MODEL), HG_WIDTH ** -0.5),
        'na_rpb': nrm(ks[7], (DEPTH, NA_HEADS, 2 * NA_KH - 1, 2 * NA_KW - 1), 0.1),
        'w_na_o': nrm(ks[8], (DEPTH, NA_WIDTH, D_MODEL), NA_WIDTH ** -0.5),
        'mem_norm': 1.0 + nrm(ks[9], (D_MODEL,), 0.02),
        'w_mem_kv': nrm(ks[10], (DEPTH, D_MODEL, 2 * CA_WIDTH), D_MODEL ** -0.5),
        'w_ca_o': nrm(ks[11], (DEPTH, CA_WIDTH, D_MODEL), CA_WIDTH ** -0.5),
        'w_out': nrm(ks[12], (DEPTH, D_MODEL, D_MODEL), D_MODEL ** -0.5),
        'norm_ffn': 1.0 + nrm(ks[13], (DEPTH, D_MODEL), 0.02),
        'w_up': nrm(ks[14], (DEPTH, D_MODEL, 2 * D_FF_2), D_MODEL ** -0.5),
        'conv_w': nrm(ks[15], (DEPTH, CONV_W, 2 * D_FF_2), CONV_W ** -0.5),
        'conv_b': nrm(ks[16], (DEPTH, 2 * D_FF_2), 0.01),
        'w_down': nrm(ks[17], (DEPTH, D_FF_2, D_MODEL), D_FF_2 ** -0.5),
        'norm_final': 1.0 + nrm(ks[18], (D_MODEL,), 0.02),
    }

def second_block(x, mem, norm_mix, w_in, hg_lb_logits, hg_gnorm, w_hg_o, na_rpb, w_na_o, mem_norm,
              w_mem_kv, w_ca_o, w_out, norm_ffn, w_up, conv_w, conv_b, w_down, norm_final):
    p_lb = jax.nn.softmax(hg_lb_logits.astype(jnp.float32), axis=0)
    lower_bounds = jnp.clip(jnp.cumsum(p_lb, axis=0) - p_lb[0], 0.0, 1.0)
    mem_n = rmsnorm_2(mem, mem_norm)
    for l in range(DEPTH):
        h = rmsnorm_2(x, norm_mix[l])
        (hq, hi, hff, hfb, hg, nq, nk, nv, cq, g_hg, g_na, g_ca) = split_cols(h @ w_in[l])
        y_hg = hgrn2_branch(hq, hi, hff, hfb, hg, lower_bounds[l], hg_gnorm[l], w_hg_o[l])
        y_na = neighbourhood_attention(nq, nk, nv, na_rpb[l], w_na_o[l])
        y_ca = memory_cross_attention(cq, mem_n, w_mem_kv[l], w_ca_o[l])
        merged = jax.nn.sigmoid(g_hg) * y_hg + jax.nn.sigmoid(g_na) * y_na + jax.nn.sigmoid(g_ca) * y_ca
        x = x + merged @ w_out[l]
        x = x + conv_ffn(rmsnorm_2(x, norm_ffn[l]), w_up[l], conv_w[l], conv_b[l], w_down[l])
    return rmsnorm_2(x, norm_final)


def setup_inputs(seed=0):
    out = dict(first_inputs(seed))
    for name, value in second_inputs(seed + 1).items():
        if name != "x":
            out[name + "_2"] = value
    return out


def reference(
    x, p, mix_pre_norm, w_in, conv_dw_w, conv_dw_b, conv_ln_w, conv_ln_b, w_out, mix_post_norm,
    ffn_pre_norm, w_ffn_gate, w_ffn_up, w_ffn_down, ffn_post_norm, w_ple_gate, w_ple_proj,
    ple_post_norm, mem_2, norm_mix_2, w_in_2, hg_lb_logits_2, hg_gnorm_2, w_hg_o_2, na_rpb_2,
    w_na_o_2, mem_norm_2, w_mem_kv_2, w_ca_o_2, w_out_2, norm_ffn_2, w_up_2, conv_w_2, conv_b_2,
    w_down_2, norm_final_2,
):
    x = first_block(
        x, p, mix_pre_norm, w_in, conv_dw_w, conv_dw_b, conv_ln_w, conv_ln_b, w_out,
        mix_post_norm, ffn_pre_norm, w_ffn_gate, w_ffn_up, w_ffn_down, ffn_post_norm,
        w_ple_gate, w_ple_proj, ple_post_norm,
    )
    return second_block(
        x, mem_2, norm_mix_2, w_in_2, hg_lb_logits_2, hg_gnorm_2, w_hg_o_2, na_rpb_2, w_na_o_2,
        mem_norm_2, w_mem_kv_2, w_ca_o_2, w_out_2, norm_ffn_2, w_up_2, conv_w_2, conv_b_2,
        w_down_2, norm_final_2,
    )


_drawn_inputs = setup_inputs


def setup_inputs(seed=0):
    import zlib

    import numpy as np

    out = dict(_drawn_inputs(seed))
    spreads = {}
    factors = {'mix_pre_norm': 4.206,
     'conv_dw_b': 4.367,
     'conv_ln_w': 7.924,
     'conv_ln_b': 8.0,
     'mix_post_norm': 7.139,
     'ffn_pre_norm': 7.204,
     'ffn_post_norm': 8.0,
     'ple_post_norm': 27.666,
     'norm_mix_2': 8.0,
     'hg_gnorm_2': 8.0,
     'na_rpb_2': 33.574,
     'mem_norm_2': 21.428,
     'norm_ffn_2': 19.438,
     'conv_b_2': 39.753,
     'norm_final_2': 21.562}
    for name, (base, spread) in spreads.items():
        noise = np.random.default_rng([zlib.crc32(name.encode()), seed]).standard_normal(out[name].shape)
        drawn = base * np.exp(spread * noise) if base else spread * noise
        out[name] = __import__('jax').numpy.asarray(drawn.astype(out[name].dtype))
    for name, factor in factors.items():
        out[name] = (out[name] * factor).astype(out[name].dtype)
    return out
```

```python
from contextlib import ExitStack

import numpy as np
import concourse.bass as bass
from concourse import mybir

P = 128
D = 1024
S = 256
KT = D // P
DC = 512
DFF = 2816
FT = DFF // P
CW = 31
EPS = 1e-6
HG = 8
NA = 8
CA = 4
RET = 4
RING = 5
PJ = 3
SLOT = 16 * P

ALU = mybir.AluOpType
ACT = mybir.ActivationFunctionType
F32 = mybir.dt.float32
I32 = mybir.dt.int32
AX = mybir.AxisListType

STAGES = [
    ("conv", 4, 16, "dve"), ("qk", 4, 16, "act"), ("v", 2, 16, "act"), ("g", 2, 16, "act"),
    ("memk", 2, 16, "act"), ("memv", 2, 16, "act"), ("wout", 4, 16, "act"),
    ("ff", 22, 16, "dve"), ("down", 4, 2 * FT, "act"), ("ple", 4, 16, "dve"),
    ("hq", 4, 16, "act"), ("hff", 4, 16, "act"), ("hfb", 4, 16, "act"), ("hi", 4, 16, "act"),
    ("nq", 2, 16, "act"), ("nk", 2, 16, "act"), ("nv", 2, 16, "act"), ("cq", 2, 16, "act"),
    ("hg", 4, 16, "act"), ("mhg", 8, 16, "dve"), ("mna", 8, 12, "dve"), ("mca", 8, 12, "dve"),
    ("wout2", 4, 16, "dve"), ("up", 22, 16, "dve"), ("down2", 4, 2 * FT, "dve"),
]
FILLS = [(name, j, nb, who) for name, n, nb, who in STAGES for j in range(n)]
INDEX = {(name, j): n for n, (name, j, _, _) in enumerate(FILLS)}
FIRST_BLOCK = [sum(f[2] for f in FILLS[:n]) for n in range(len(FILLS) + 1)]
NBLOCKS = FIRST_BLOCK[-1]
NSLOTS = NBLOCKS // 16

STATS = [("mix_pre", 2), ("mem", 2), ("ln_mean", 0), ("ln_var", 1), ("ret0", 1), ("ret1", 1),
         ("mix_post", 4), ("ffn_pre", 2), ("ffn_post", 4), ("ple_post", 4), ("mix2", 2),
         ("hg0", 1), ("hg1", 1), ("hg2", 1), ("hg3", 1), ("ffn2", 2), ("final", 2)]
STAT = {name: n for n, (name, _) in enumerate(STATS)}
ROOTS = [name for name, _ in STATS if name != "ln_mean"]
SQ_BEFORE = {name: sum(c for _, c in STATS[:n]) for n, (name, _) in enumerate(STATS)}

VEC_SIZES = [("mix_pre", 8), ("dw_w", 4 * CW), ("dw_b", 4), ("ln_w", 4), ("ln_b", 4), ("mix_post", 8),
             ("ffn_pre", 8), ("ffn_post", 8), ("ple_post", 8), ("norm_mix2", 8), ("lb", 16), ("gnorm", 1),
             ("mem_norm", 8), ("norm_ffn2", 8), ("conv_w", 3 * 44), ("conv_b", 44), ("norm_final", 8)]
VEC = {}
for _n, _c in VEC_SIZES:
    VEC[_n] = sum(c for n, c in VEC_SIZES[:len(VEC)])
NVEC = sum(c for _, c in VEC_SIZES)

CONST = {"m1024": 0, "m512": P, "m128": 2 * P, "ident": 3 * P, "mask": 4 * P}
LEVELS = [1, 2, 4, 8, 16, 32, 64]
NCONST = 4 * P + len(LEVELS) * P


def fill_of_last_block(slot):
    last = 16 * slot + 15
    return next(n for n in range(len(FILLS)) if FIRST_BLOCK[n + 1] > last)


def freed_count(n, who):
    return sum(1 for f in FILLS[:n + 1] if f[3] == who)


def program(nc, xt, memt, pt, wstream, wproj, vecs, consts, rope_tab, decay_tab, rpb, out, toep):
    ctx = ExitStack()
    with ctx:
        def sb(name, shape):
            return ctx.enter_context(nc.sbuf_tensor(name, [P] + shape, F32))

        def sem(name):
            return ctx.enter_context(nc.semaphore(name))

        ring = sb("ring", [RING, 16, P])
        x = sb("x", [KT, S])
        h = sb("h", [KT, S])
        y = sb("y", [KT, S])
        sq = sb("sq", [KT, S])
        vec = sb("vec", [NVEC])
        con = sb("con", [NCONST])
        rstd = sb("rstd", [2 * S])
        rstd_h = sb("rstd_h", [S])
        std = sb("std", [2 * S])
        eps = sb("eps", [1])
        gate_tmp = sb("gate_tmp", [2, 2, S])
        prod_tmp = sb("prod_tmp", [2, S])
        mem_k = sb("mem_k", [CA, S])
        mem_v = sb("mem_v", [2, DC])
        lb = sb("lb", [6, 16])
        arena = ctx.enter_context(nc.sbuf_tensor("arena", [P, 24576], F32))

        def part(start, *shape):
            size = int(np.prod(shape))
            v = arena[:, start:start + size]
            if len(shape) == 2:
                v = v.rearrange("p (a b) -> p a b", b=shape[1])
            return v, start + size

        at = 0
        ff, at = part(at, FT, S)
        conv_in, at = part(at, 4, CW - 1 + S)
        conv_y, at = part(at, 4, S)
        q_raw, at = part(at, RET, S)
        k_raw, at = part(at, RET, S)
        v_ret, at = part(at, 2, DC)
        g_ret, at = part(at, RET, S)
        o_ret, at = part(at, RET, S)
        mix, at = part(at, KT, S)
        mem_n, at = part(at, KT, S)
        p_in, at = part(at, 2, S)
        w_ple, at = part(at, 2, D)
        rope, at = part(at, 2, S)
        at1 = at
        s_ret = arena[:, 0:RET * 384].rearrange("p (a b) -> p a b", b=384)
        decay = arena[:, 1536:1536 + RET * 384].rearrange("p (a b) -> p a b", b=384)
        rope_a = arena[:, 3072:3072 + 1024].rearrange("p (a b) -> p a b", b=S)
        rope_b = arena[:, 4096:4096 + 1024].rearrange("p (a b) -> p a b", b=S)
        ple_p = arena[:, 0:KT * S].rearrange("p (a b) -> p a b", b=S)

        at = 0
        f_f, at = part(at, HG, S)
        f_b, at = part(at, HG, S)
        k_f, at = part(at, HG, S)
        k_b, at = part(at, HG, S)
        q_f, at = part(at, HG, S)
        q_b, at = part(at, HG, S)
        v_hg, at = part(at, 2, D)
        gate_hg, at = part(at, HG, S)
        st_hg, at = part(at, HG, 4 * P)
        q_na, at = part(at, 4, S)
        k_na, at = part(at, 4, S)
        v_na, at = part(at, 2, DC)
        q_ca, at = part(at, CA, S)
        at2 = at
        assert max(at1, at2) <= 24576, (at1, at2)
        toep_t = arena[:, 0:NA * 6 * 64].rearrange("p (a b) -> p a b", b=6 * 64)
        o_hg, _ = part(2 * HG * S, HG, S)
        merged, _ = part(3 * HG * S, HG, S)
        o_na, _ = part(4 * HG * S, 4, S)
        o_ca, _ = part(4 * HG * S + 1024, 4, S)
        probs, _ = part(5 * HG * S, 2, 2 * S)
        probs_t, _ = part(5 * HG * S + 1024, 2, 2 * S)
        soft = sb("soft", [2, 3, 2])
        ksum = sq
        q_s = y

        pj = [ctx.enter_context(nc.psum_tensor(f"pj{i}", [P, 2, S], F32)) for i in range(PJ)]
        sc = [ctx.enter_context(nc.psum_tensor(f"sc{i}", [P, 512], F32)) for i in range(4)]
        st = ctx.enter_context(nc.psum_tensor("st", [P, 512], F32))

        load_x = sem("load_x")
        load_params = sem("load_params")
        load_mem = sem("load_mem")
        load_side = sem("load_side")
        slot_ready = [sem(f"slot_ready{i}") for i in range(RING)]
        fill_done = sem("fill_done")
        freed = {"act": sem("freed_act"), "dve": sem("freed_dve")}
        gate_done = sem("gate_done")
        sq_ready = sem("sq_ready")
        stat_done = sem("stat_done")
        root_done = sem("root_done")
        eps_ready = sem("eps_ready")
        stat_read = sem("stat_read")
        h_ready = sem("h_ready")
        x_ready = sem("x_ready")
        mem_ready = sem("mem_ready")
        pad_ready = sem("pad_ready")
        conv_ready = sem("conv_ready")
        mix_conv = sem("mix_conv")
        rope_ready = sem("rope_ready")
        sc_done = sem("sc_done")
        s_ready = sem("s_ready")
        o_copied = sem("o_copied")
        mix_ret = sem("mix_ret")
        lb_exp = sem("lb_exp")
        lb_ready = sem("lb_ready")
        ple_proj = sem("ple_proj")
        ple_mul = sem("ple_mul")
        ff_ready = sem("ff_ready")
        gates_ready = sem("gates_ready")
        level_ready = sem("level_ready")
        st_diag = sem("st_diag")
        st_mask = sem("st_mask")
        st_cross = sem("st_cross")
        hg_out = sem("hg_out")
        toep_zero = sem("toep_zero")
        toep_row = sem("toep_row")
        toep_load = sem("toep_load")
        toep_sel = sem("toep_sel")
        zero_ready = sem("zero_ready")
        logits_ready = sem("logits_ready")
        exp_ready = sem("exp_ready")
        p_ready = sem("p_ready")
        turned = sem("turned")
        pt_ready = sem("pt_ready")
        scored = sem("scored")
        pv_done = sem("pv_done")
        o_att = sem("o_att")
        merge_ready = sem("merge_ready")
        up_lin = sem("up_lin")
        up_conv = sem("up_conv")
        gelu_done = sem("gelu_done")
        dve_chain = sem("dve_chain")
        act_chain = sem("act_chain")
        pool_chain = sem("pool_chain")
        out_ready = sem("out_ready")
        stored = sem("stored")

        def col(name, i=0):
            c = VEC[name] + i
            return vec[:, c:c + 1]

        def mat(name, i=0):
            c = CONST[name] + i * P
            return con[:, c:c + P]

        def fi(name, j=0):
            return INDEX[(name, j)]

        def bank(name, j):
            return pj[fi(name, j) % PJ]

        def gate_slot(name, j):
            return (freed_count(fi(name, j), "dve") - 1) % 2

        def wait_gate_slot(eng, name, j):
            d = freed_count(fi(name, j), "dve") - 1
            if d >= 2:
                eng.wait_ge(freed["dve"], d - 1)

        def wait_read(eng, name, j):
            n = fi(name, j)
            eng.wait_ge(freed[FILLS[n][3]], freed_count(n, FILLS[n][3]))

        H_TILES = {"mix_pre": 0, "ffn_pre": 8, "mix2": 16, "ffn2": 24}
        X_HALF = {"mix_post": 0, "ffn_post": 2, "ple_post": 4}
        SC_RET, SC_RO = 0, RET
        SC_LEVEL = 2 * RET
        SC_CROSS = SC_LEVEL + 4 * (1 + len(LEVELS))
        SC_HGO = SC_CROSS + 4

        def diag_view(g):
            v = st_hg[:, 2 * g:2 * g + 2].rearrange("p a (b c) -> p a b c", c=P)
            return v[:, :, 0:4:3]

        SIDE_FILLS = [(name, j) for name, j, _, _ in FILLS if name in ("hi", "nq", "nk", "nv", "cq", "hg")]
        MERGE_FILLS = [(name, j) for name, j, _, _ in FILLS if name in ("mhg", "mna", "mca")]

        block = ctx.enter_context(nc.Block())

        @block.sync
        def _(sp):
            sp.dma_start(x[:], xt).then_inc(load_x, 16)
            sp.dma_start(con[:], consts).then_inc(load_params, 16)
            sp.dma_start(vec[:], vecs).then_inc(load_params, 16)
            for n in range(NSLOTS):
                if n >= RING:
                    sp.wait_ge(fill_done, fill_of_last_block(n - RING) + 1)
                sp.dma_start(ring[:, n % RING], wstream[n]).then_inc(slot_ready[n % RING], 16)
                if n == 4:
                    sp.dma_start(mem_n, memt).then_inc(load_mem, 16)
                if n == 6:
                    sp.dma_start(rope, rope_tab).then_inc(load_side, 16)
                    sp.dma_start(decay, decay_tab).then_inc(load_side, 16)
                    sp.dma_start(p_in, pt).then_inc(load_side, 16)
                    sp.dma_start(w_ple, wproj).then_inc(load_side, 16)
            sp.wait_ge(out_ready, 2)
            sp.dma_start(out, y[:]).then_inc(stored, 16)
            sp.wait_ge(stored, 16)

        @block.gpsimd
        def _(pool):
            chain = [0]

            def link(ins):
                chain[0] += 1
                ins.then_inc(pool_chain, 1)
                return chain[0]

            nc.gpsimd.memset(conv_in[:, :, 0:CW - 1], 0.0).then_inc(pad_ready, 1)
            nc.gpsimd.memset(prod_tmp[:, 0, 0:P], 0.0).then_inc(zero_ready, 1)
            pool.wait_ge(zero_ready, 1)
            pool.dma_start(toep, prod_tmp[0:NA * 15, 0, 0:P]).then_inc(toep_zero, 16)
            pool.wait_ge(toep_zero, 16)
            pool.dma_start(toep[:, 48:79], rpb).then_inc(toep_row, 16)
            pool.wait_ge(toep_row, 16)
            pool.wait_ge(lb_ready, 1)
            for d, (stage, f, k) in enumerate((("hff", f_f, k_f), ("hfb", f_b, k_b))):
                for j in range(4):
                    wait_read(pool, stage, j)
                    for t in (2 * j, 2 * j + 1):
                        c = d * 8 + t
                        last = link(nc.gpsimd.tensor_scalar(f[:, t], f[:, t], lb[:, 5, c:c + 1],
                                                            lb[:, 4, c:c + 1], ALU.mult, ALU.add))
                        nc.gpsimd.tensor_scalar(k[:, t], k[:, t], lb[:, 5, c:c + 1], None, ALU.mult)
                    pool.wait_ge(pool_chain, last)
                    nc.gpsimd.tensor_scalar(f[:, 2 * j:2 * j + 2], f[:, 2 * j:2 * j + 2], 1e-12, None,
                                            ALU.max).then_inc(gates_ready, 1)
            pool.wait_ge(level_ready, 1 + len(LEVELS))
            for half in range(2):
                for hd in range(NA):
                    off = (hd * 15 + 5 - half) * P
                    src = bass.AP(tensor=toep.tensor, offset=toep.offset + off, ap=[[1, 64], [P, 6], [1, 64]])
                    pool.dma_start(toep_t[64 * half:64 * half + 64, hd].rearrange("p (d c) -> p d c", c=64),
                                   src).then_inc(toep_load, 16)
            pool.wait_ge(toep_load, 16 * 2 * NA)
            for half in range(2):
                v = toep_t[64 * half:64 * half + 64].rearrange("p a (d c) -> p (a d) c", c=64)
                lo, hi = v[:, :, 16:64], v[:, :, 0:48]
                a = link(nc.gpsimd.affine_select(out=lo, in_=lo, compare_op=ALU.is_ge, fill=-1e30, base=55,
                                                 pattern=[[0, NA * 6], [-1, 48]], channel_multiplier=-1))
                pool.wait_ge(pool_chain, a)
                nc.gpsimd.affine_select(out=hi, in_=hi, compare_op=ALU.is_ge, fill=-1e30, base=-56,
                                        pattern=[[0, NA * 6], [1, 48]], channel_multiplier=1
                                        ).then_inc(toep_sel, 1)

        @block.scalar
        def _(act):
            A = nc.scalar.activation
            chain = [0]

            def squares_of_x(stage):
                for i in range(2):
                    if stage in X_HALF:
                        act.wait_ge(x_ready, X_HALF[stage] + i + 1)
                    elif stage is not None:
                        wait_read(act, stage, 2 * i + 1)
                    A(sq[:, 4 * i:4 * i + 4], x[:, 4 * i:4 * i + 4], ACT.Square).then_inc(sq_ready, 1)

            def root(name, n=S):
                act.wait_ge(stat_done, STAT[name] + 1)
                if STAT[name]:
                    act.wait_ge(stat_read, STAT[name])
                A(std[:, 0:n], st[:, 0:n], ACT.Sqrt, bias=eps[:, 0:1]).then_inc(root_done, 1)

            def wait_fill(name, j):
                act.wait_ge(fill_done, fi(name, j) + 1)

            def post_norm_fill(name, j):
                wait_fill(name, j)
                A(sq[:, 2 * j:2 * j + 2], bank(name, j)[:], ACT.Square).then_inc(sq_ready, 1)
                nc.scalar.copy(y[:, 2 * j:2 * j + 2], bank(name, j)[:]).then_inc(freed["act"], 1)

            def copy_fill(name, j, dst, func=None, view=None):
                wait_fill(name, j)
                src = bank(name, j)[:]
                if func is None:
                    nc.scalar.copy(dst, src).then_inc(freed["act"], 1)
                else:
                    A(dst, src, func).then_inc(freed["act"], 1)

            act.wait_ge(load_x, 16)
            squares_of_x(None)
            act.wait_ge(eps_ready, 1)
            root("mix_pre")
            act.wait_ge(lb_exp, 1)
            A(lb[:, 1], lb[:, 0], ACT.Exp).then_inc(lb_exp, 1)
            act.wait_ge(load_mem, 16)
            act.wait_ge(stat_done, STAT["mix_pre"] + 1)
            for i in range(2):
                A(sq[:, 4 * i:4 * i + 4], mem_n[:, 4 * i:4 * i + 4], ACT.Square).then_inc(sq_ready, 1)
            root("mem")
            for j in range(4):
                wait_fill("conv", j)
                wait_gate_slot(act, "conv", j)
                A(gate_tmp[:, gate_slot("conv", j), 0], bank("conv", j)[:, 1], ACT.Sigmoid).then_inc(gate_done, 1)
            for j in range(2):
                copy_fill("qk", j, q_raw[:, 2 * j:2 * j + 2])
            for j in range(2):
                copy_fill("qk", 2 + j, k_raw[:, 2 * j:2 * j + 2])
            for j in range(2):
                copy_fill("v", j, v_ret[:, :, 256 * j:256 * j + 256])
            for j in range(2):
                copy_fill("g", j, g_ret[:, 2 * j:2 * j + 2], ACT.Silu)
            for j in range(2):
                copy_fill("memk", j, mem_k[:, 2 * j:2 * j + 2])
            for j in range(2):
                copy_fill("memv", j, mem_v[:, :, 256 * j:256 * j + 256])
            act.wait_ge(conv_ready, 2)
            act.wait_ge(stat_done, STAT["mem"] + 1)
            A(sq[:, 0:4], conv_y, ACT.Square).then_inc(sq_ready, 1)
            root("ln_var")
            for g in range(2):
                for hd in (2 * g, 2 * g + 1):
                    act.wait_ge(sc_done, SC_RO + hd + 1)
                    ins = A(sq[:, 4 + hd], sc[hd][:, 0:S], ACT.Square)
                    if hd % 2:
                        ins.then_inc(sq_ready, 1)
                    nc.scalar.copy(o_ret[:, hd], sc[hd][:, 0:S]).then_inc(o_copied, 1)
            root("ret0", 2 * S)
            root("ret1", 2 * S)
            act.wait_ge(conv_ready, 3)
            for j in range(4):
                A(mix[:, j], conv_y[:, j], ACT.Silu, bias=col("ln_b", j), scale=col("ln_w", j)).then_inc(mix_conv, 1)
            act.wait_ge(stat_done, STAT["ret1"] + 1)
            for j in range(4):
                post_norm_fill("wout", j)
            root("mix_post")
            squares_of_x("mix_post")
            root("ffn_pre")
            for j in range(22):
                wait_fill("ff", j)
                wait_gate_slot(act, "ff", j)
                A(gate_tmp[:, gate_slot("ff", j), 0], bank("ff", j)[:, 0], ACT.Silu).then_inc(gate_done, 1)
            for j in range(4):
                post_norm_fill("down", j)
            root("ffn_post")
            for j in range(4):
                act.wait_ge(sc_done, SC_LEVEL + j + 1)
                nc.scalar.copy(ple_p[:, 2 * j:2 * j + 2], sc[j][:]).then_inc(ple_proj, 1)
            for j in range(4):
                wait_fill("ple", j)
                wait_gate_slot(act, "ple", j)
                A(gate_tmp[:, gate_slot("ple", j)], bank("ple", j)[:], ACT.Sigmoid).then_inc(gate_done, 1)
                wait_read(act, "ple", j)
                A(sq[:, 2 * j:2 * j + 2], y[:, 2 * j:2 * j + 2], ACT.Square).then_inc(sq_ready, 1)
            root("ple_post")
            squares_of_x("ple_post")
            root("mix2")

            act.wait_ge(x_ready, X_HALF["ple_post"] + 2)
            for j in range(4):
                copy_fill("hq", j, q_s[:, 2 * j:2 * j + 2], ACT.Silu)
            for stage, f, k in (("hff", f_f, k_f), ("hfb", f_b, k_b)):
                for j in range(4):
                    wait_fill(stage, j)
                    A(f[:, 2 * j:2 * j + 2], bank(stage, j)[:], ACT.Sigmoid)
                    A(k[:, 2 * j:2 * j + 2], bank(stage, j)[:], ACT.Sigmoid, scale=-1.0).then_inc(freed["act"], 1)

            def diagonal():
                for g in range(4):
                    act.wait_ge(sc_done, SC_LEVEL + 4 + g + 1)
                    nc.scalar.copy(diag_view(g), sc[g][:].rearrange("p (a b c) -> p a b c", a=2, b=2)
                                   ).then_inc(st_diag, 1)

            def cross():
                for g in range(4):
                    act.wait_ge(sc_done, SC_CROSS + 4 + g + 1)
                    nc.scalar.copy(st_hg[:, 2 * g:2 * g + 2, P:3 * P],
                                   sc[g][:].rearrange("p (a b) -> p a b", a=2)).then_inc(st_cross, 1)

            def hg_outputs():
                for g in range(4):
                    act.wait_ge(sc_done, SC_HGO + 4 + g + 1)
                    o = sc[g][:].rearrange("p (a b) -> p a b", a=2)
                    A(sq[:, 2 * g:2 * g + 2], o, ACT.Square).then_inc(sq_ready, 1)
                    nc.scalar.copy(o_hg[:, 2 * g:2 * g + 2], o).then_inc(o_copied, 1)
                for g in range(4):
                    root(f"hg{g}", 2 * S)

            for e, (name, j) in enumerate(SIDE_FILLS):
                if name in ("hi", "nv"):
                    dst = (v_hg if name == "hi" else v_na)[:, :, 256 * j:256 * j + 256]
                    copy_fill(name, j, dst)
                elif name == "hg":
                    copy_fill(name, j, gate_hg[:, 2 * j:2 * j + 2], ACT.Silu)
                else:
                    copy_fill(name, j, {"nq": q_na, "nk": k_na, "cq": q_ca}[name][:, 2 * j:2 * j + 2])
                if e == 0:
                    diagonal()
            cross()
            hg_outputs()

            def att_exp(a):
                act.wait_ge(logits_ready, a + 1)
                for t in range(2):
                    if a < NA:
                        src, scale = probs[:, a % 2, t * S:t * S + S], 1.0
                    else:
                        src, scale = sc[a % 2][:, t * S:t * S + S], float(P) ** -0.5
                    ins = A(probs[:, a % 2, t * S:t * S + S], src, ACT.Exp, bias=soft[:, a % 2, 0, t:t + 1],
                            scale=scale, accum_out=soft[:, a % 2, 1, t:t + 1])
                ins.then_inc(exp_ready, 1)

            def att_turn(a):
                act.wait_ge(turned, a + 1)
                if a >= 2:
                    act.wait_ge(pv_done, a - 1)
                nc.scalar.copy(probs_t[:, a % 2], sc[2][:]).then_inc(pt_ready, 1)

            def att_out(a):
                act.wait_ge(pv_done, a + 1)
                if a < NA:
                    if a % 2:
                        nc.scalar.copy(o_na[:, a // 2], sc[3][:, 0:S]).then_inc(o_att, 1)
                else:
                    nc.scalar.copy(o_ca[:, a - NA], sc[3][:, 0:S]).then_inc(o_att, 1)

            def att_slot(i):
                if i < NA + CA:
                    att_exp(i)
                if 1 <= i <= NA + CA:
                    att_turn(i - 1)
                if 2 <= i < NA + CA + 2:
                    att_out(i - 2)

            att_slot(0)
            att_slot(1)
            for i, (name, j) in enumerate(MERGE_FILLS):
                wait_fill(name, j)
                wait_gate_slot(act, name, j)
                A(gate_tmp[:, gate_slot(name, j), 0], bank(name, j)[:, 0], ACT.Sigmoid).then_inc(gate_done, 1)
                att_slot(i + 2)
            act.wait_ge(stat_done, STAT["hg3"] + 1)
            squares_of_x("wout2")
            root("ffn2")
            for j in range(23):
                if j < 22:
                    wait_fill("up", j)
                    if j >= 2:
                        act.wait_ge(ff_ready, j - 1)
                    for i in range(2):
                        ins = A(gate_tmp[:, j % 2, i], bank("up", j)[:, i], ACT.Identity,
                                bias=col("conv_b", 22 * i + j), scale=col("conv_w", 44 + 22 * i + j))
                    ins.then_inc(up_lin, 1)
                if j >= 1:
                    i = j - 1
                    wait_read(act, "up", i)
                    A(gate_tmp[:, i % 2, 0], gate_tmp[:, i % 2, 0], ACT.Gelu_apprx_tanh).then_inc(gelu_done, 1)
            squares_of_x("down2")
            root("final")

        @block.vector
        def _(dve):
            V = nc.vector
            chain = [0]

            def link(ins):
                chain[0] += 1
                ins.then_inc(dve_chain, 1)
                return chain[0]

            def after(n):
                dve.wait_ge(dve_chain, n)

            def over(v, n):
                return v.unsqueeze(1).to_broadcast([P, n, S])

            def root(name, dst, n=S):
                dve.wait_ge(root_done, ROOTS.index(name) + 1)
                V.reciprocal(dst, std[:, 0:n]).then_inc(stat_read, 1)
                dve.wait_ge(stat_read, STAT[name] + 1)

            def norm_to_h(name, gain):
                root(name, rstd_h[:])
                for t in range(KT):
                    V.scalar_tensor_tensor(out=h[:, t], in0=x[:, t], scalar=col(gain, t), in1=rstd_h[:],
                                           op0=ALU.mult, op1=ALU.mult).then_inc(h_ready, 1)
                dve.wait_ge(h_ready, H_TILES[name] + KT)

            def post_norm(name, gain):
                root(name, rstd[:, 0:S])
                for i in range(2):
                    for t in range(4 * i, 4 * i + 4):
                        n = link(V.scalar_tensor_tensor(out=y[:, t], in0=y[:, t], scalar=col(gain, t),
                                                        in1=rstd[:, 0:S], op0=ALU.mult, op1=ALU.mult))
                    after(n)
                    V.tensor_tensor(x[:, 4 * i:4 * i + 4], x[:, 4 * i:4 * i + 4], y[:, 4 * i:4 * i + 4],
                                    ALU.add).then_inc(x_ready, 1)
                dve.wait_ge(x_ready, X_HALF[name] + 2)

            def wait_gate(count):
                dve.wait_ge(gate_done, count)

            gates = [0]

            V.memset(eps[:], EPS).then_inc(eps_ready, 1)
            dve.wait_ge(load_params, 32)
            logits = vec[:, VEC["lb"]:VEC["lb"] + 16]
            V.tensor_tensor(lb[:, 0], logits, logits, ALU.subtract).then_inc(lb_exp, 1)
            norm_to_h("mix_pre", "mix_pre")
            dve.wait_ge(lb_exp, 2)
            after(link(V.reciprocal(lb[:, 2], lb[:, 1])))
            after(link(V.tensor_tensor(lb[:, 3], lb[:, 1], lb[:, 2], ALU.mult)))
            after(link(V.tensor_tensor(lb[:, 4], lb[:, 3], lb[:, 3], ALU.subtract)))
            after(link(V.tensor_scalar(lb[:, 4], lb[:, 4], 0.0, 1.0, ALU.max, ALU.min)))
            V.tensor_scalar(lb[:, 5], lb[:, 4], -1.0, 1.0, ALU.mult, ALU.add).then_inc(lb_ready, 1)

            dve.wait_ge(pad_ready, 1)
            for j in range(4):
                gates[0] += 1
                wait_gate(gates[0])
                V.tensor_tensor(conv_in[:, j, CW - 1:], bank("conv", j)[:, 0], gate_tmp[:, gate_slot("conv", j), 0],
                                ALU.mult).then_inc(freed["dve"], 1)
            root("mem", rstd[:, 0:S])
            for t in range(KT):
                V.scalar_tensor_tensor(out=mem_n[:, t], in0=mem_n[:, t], scalar=col("mem_norm", t),
                                       in1=rstd[:, 0:S], op0=ALU.mult, op1=ALU.mult).then_inc(mem_ready, 1)
            dve.wait_ge(mem_ready, KT)
            dve.wait_ge(freed["dve"], 4)
            seen = [0] * 4
            for w in range(CW):
                for j in range(4):
                    src = conv_in[:, j, w:w + S]
                    tap = col("dw_w", w * 4 + j)
                    if w == 0:
                        seen[j] = link(V.tensor_scalar(conv_y[:, j], src, tap, col("dw_b", j), ALU.mult, ALU.add))
                    else:
                        after(seen[j])
                        ins = V.scalar_tensor_tensor(out=conv_y[:, j], in0=src, scalar=tap, in1=conv_y[:, j],
                                                     op0=ALU.mult, op1=ALU.add)
                        if w < CW - 1 or j < 3:
                            seen[j] = link(ins)
            ins.then_inc(conv_ready, 1)
            dve.wait_ge(load_side, 64)
            for i, t in enumerate((q_raw, k_raw)):
                wait_read(dve, "qk", 2 * i + 1)
                if i:
                    dve.wait_ge(rope_ready, 1)
                V.tensor_tensor(rope_a, t, over(rope[:, 0], 4), ALU.mult)
                for a, b in ((0, 64), (64, 0)):
                    sin = rope[b:b + 64, 1].unsqueeze(1).to_broadcast([64, 4, S])
                    n = link(V.tensor_tensor(rope_b[a:a + 64], t[b:b + 64], sin, ALU.mult))
                after(n)
                V.tensor_tensor(t, rope_a, rope_b, ALU.add).then_inc(rope_ready, 1)
            dve.wait_ge(stat_done, STAT["ln_mean"] + 1)
            V.tensor_copy(rstd[:, S:2 * S], st[:, 0:S]).then_inc(stat_read, 1)
            dve.wait_ge(stat_read, STAT["ln_mean"] + 1)
            V.tensor_tensor(conv_y, conv_y, over(rstd[:, S:2 * S], 4), ALU.subtract).then_inc(conv_ready, 1)
            for hd in range(RET):
                dve.wait_ge(sc_done, SC_RET + hd + 1)
                V.tensor_tensor(s_ret[:, hd], sc[hd][:, 0:384], decay[:, hd], ALU.mult).then_inc(s_ready, 1)
            root("ln_var", rstd[:, 0:S])
            V.tensor_tensor(conv_y, conv_y, over(rstd[:, 0:S], 4), ALU.mult).then_inc(conv_ready, 1)
            dve.wait_ge(conv_ready, 3)
            for g in range(2):
                dve.wait_ge(o_copied, 2 * g + 2)
                root(f"ret{g}", rstd[:], 2 * S)
                o = o_ret[:, 2 * g:2 * g + 2]
                after(link(V.tensor_tensor(o, o, rstd[:].rearrange("p (a b) -> p a b", a=2), ALU.mult)))
                wait_read(dve, "g", 1)
                V.tensor_tensor(mix[:, 4 + 2 * g:6 + 2 * g], o, g_ret[:, 2 * g:2 * g + 2], ALU.mult
                                ).then_inc(mix_ret, 1)
            wait_read(dve, "wout", 3)
            post_norm("mix_post", "mix_post")
            norm_to_h("ffn_pre", "ffn_pre")
            for j in range(22):
                gates[0] += 1
                wait_gate(gates[0])
                V.tensor_tensor(ff[:, j], bank("ff", j)[:, 1], gate_tmp[:, gate_slot("ff", j), 0],
                                ALU.mult).then_inc(freed["dve"], 1)
            wait_read(dve, "down", 3)
            post_norm("ffn_post", "ffn_post")
            for j in range(4):
                gates[0] += 1
                wait_gate(gates[0])
                dve.wait_ge(ple_proj, j + 1)
                V.tensor_tensor(y[:, 2 * j:2 * j + 2], gate_tmp[:, gate_slot("ple", j)], ple_p[:, 2 * j:2 * j + 2],
                                ALU.mult).then_inc(freed["dve"], 1)
            wait_read(dve, "ple", 3)
            post_norm("ple_post", "ple_post")
            norm_to_h("mix2", "norm_mix2")

            wait_read(dve, "hq", 3)
            n = link(V.tensor_scalar(q_s[:], q_s[:], float(P) ** -0.5, None, ALU.mult))
            dve.wait_ge(gates_ready, 8)
            dve.wait_ge(stat_done, STAT["mix2"] + 1)
            after(n)
            V.tensor_tensor(ksum[:], k_f, k_b, ALU.add)
            V.tensor_tensor(q_f, q_s[:], f_f, ALU.mult)
            V.tensor_tensor(q_b, q_s[:], f_b, ALU.mult).then_inc(level_ready, 1)
            dve.wait_ge(level_ready, 1)

            def masks(i):
                for g in range(4):
                    dve.wait_ge(sc_done, SC_LEVEL + 4 + 4 * (i + 1) + g + 1)
                    if i == 0:
                        dve.wait_ge(st_diag, g + 1)
                    m = mat("mask", i).bitcast(I32).unsqueeze(1).to_broadcast([P, 4, P])
                    dst = st_hg[:, 2 * g:2 * g + 2].rearrange("p a (b c) -> p (a b) c", c=P)
                    m2 = mat("mask", i).bitcast(I32).unsqueeze(1).to_broadcast([P, 2, P])
                    for a in range(2):
                        src = sc[g][:, a * 256:a * 256 + 256].rearrange("p (b c) -> p b c", b=2)
                        ins = V.copy_predicated(dst[:, 4 * a:4 * a + 4:3], m2, src)
                    ins.then_inc(st_mask, 1)

            def grow(i):
                b = LEVELS[i]

                def halves(t):
                    v = t.rearrange("p a s -> p (a s)").rearrange("p (n two b) -> p n two b", two=2, b=b)
                    return v[:, :, 0], v[:, :, 1]

                nb = HG * S // (2 * b)
                fa, fb_ = halves(f_f)
                ba, bb_ = halves(f_b)
                bc = lambda t: t[:, :, 0:1].to_broadcast([P, nb, b])
                qf, qb, kf, kb = halves(q_f)[1], halves(q_b)[0], halves(k_f)[0], halves(k_b)[1]
                V.tensor_tensor(qf, qf, bc(fa), ALU.mult)
                V.tensor_tensor(kf, kf, bc(fb_), ALU.mult)
                V.tensor_tensor(qb, qb, bc(bb_), ALU.mult)
                after(link(V.tensor_tensor(kb, kb, bc(ba), ALU.mult)))
                V.tensor_tensor(fa[:, :, 0:1], fa[:, :, 0:1], fb_[:, :, 0:1], ALU.mult)
                V.tensor_tensor(ba[:, :, 0:1], ba[:, :, 0:1], bb_[:, :, 0:1], ALU.mult).then_inc(level_ready, 1)
                dve.wait_ge(level_ready, i + 2)

            for i in range(len(LEVELS)):
                masks(i)
                grow(i)
            for g in range(4):
                root(f"hg{g}", rstd[:], 2 * S)
                dve.wait_ge(o_copied, RET + g + 1)
                wait_read(dve, "hg", 3)
                o = o_hg[:, 2 * g:2 * g + 2]
                after(link(V.scalar_tensor_tensor(out=o, in0=o, scalar=col("gnorm"), in1=gate_hg[:, 2 * g:2 * g + 2],
                                                  op0=ALU.mult, op1=ALU.mult)))
                V.tensor_tensor(o, o, rstd[:].rearrange("p (a b) -> p a b", a=2), ALU.mult).then_inc(hg_out, 1)
                dve.wait_ge(hg_out, g + 1)

            def att_logits(a):
                par = a % 2
                dve.wait_ge(scored, a + 1)
                if a == 0:
                    dve.wait_ge(toep_sel, 2)
                    dve.wait_ge(sc_done, SC_HGO + 8)
                if a >= 2:
                    dve.wait_ge(turned, a - 1)
                if a < NA:
                    for t in range(2):
                        d0 = (3 - 2 * t - 1) * 64
                        rows = lambda v: v.rearrange("p (r c) -> p r c", c=64)
                        n = link(V.scalar_tensor_tensor(out=rows(probs[:, par, t * S:t * S + S]),
                                                        in0=rows(sc[par][:, t * S:t * S + S]), scalar=64.0 ** -0.5,
                                                        in1=rows(toep_t[:, a, d0:d0 + S])[:, :, ::-1],
                                                        op0=ALU.mult, op1=ALU.add))
                    after(n)
                    src, scale = probs[:, par], -1.0
                else:
                    src, scale = sc[par][:], -float(P) ** -0.5
                n = link(V.tensor_reduce(soft[:, par, 0], src.rearrange("p (t j) -> p t j", t=2), AX.X, ALU.max))
                after(n)
                V.tensor_scalar(soft[:, par, 0], soft[:, par, 0], scale, None, ALU.mult).then_inc(logits_ready, 1)

            def att_norm(a):
                par = a % 2
                dve.wait_ge(exp_ready, a + 1)
                after(link(V.reciprocal(soft[:, par, 2], soft[:, par, 1])))
                for t in range(2):
                    ins = V.tensor_scalar(probs[:, par, t * S:t * S + S], probs[:, par, t * S:t * S + S],
                                          soft[:, par, 2, t:t + 1], None, ALU.mult)
                ins.then_inc(p_ready, 1)

            def att_slot(i):
                if i < NA + CA:
                    att_logits(i)
                    att_norm(i)

            att_slot(0)
            att_slot(1)
            added = {}
            for i, (name, j) in enumerate(MERGE_FILLS):
                gates[0] += 1
                wait_gate(gates[0])
                yv = bank(name, j)[:, 1]
                gv = gate_tmp[:, gate_slot(name, j), 0]
                if name == "mhg":
                    V.tensor_tensor(merged[:, j], yv, gv, ALU.mult).then_inc(freed["dve"], 1)
                else:
                    if i - 2 >= 16:
                        dve.wait_ge(merge_ready, i - 2 - 16 + 1)
                    elif i - 2 >= 8:
                        after(added[i - 2])
                    V.tensor_tensor(prod_tmp[:, i % 2], yv, gv, ALU.mult).then_inc(freed["dve"], 1)
                    wait_read(dve, name, j)
                    if name == "mca":
                        after(added[i - 8])
                    ins = V.tensor_tensor(merged[:, j], merged[:, j], prod_tmp[:, i % 2], ALU.add)
                    if name == "mca":
                        ins.then_inc(merge_ready, 1)
                    else:
                        added[i] = link(ins)
                att_slot(i + 2)

            for j in range(4):
                dve.wait_ge(fill_done, fi("wout2", j) + 1)
                V.tensor_tensor(x[:, 2 * j:2 * j + 2], x[:, 2 * j:2 * j + 2], bank("wout2", j)[:], ALU.add
                                ).then_inc(freed["dve"], 1)
            norm_to_h("ffn2", "norm_ffn2")
            for j in range(23):
                if j < 22:
                    dve.wait_ge(up_lin, j + 1)
                    b = bank("up", j)
                    for i in range(2):
                        t = gate_tmp[:, j % 2, i]
                        ct = 22 * i + j
                        n = link(V.scalar_tensor_tensor(out=t[:, 1:S], in0=b[:, i, 0:S - 1], scalar=col("conv_w", ct),
                                                        in1=t[:, 1:S], op0=ALU.mult, op1=ALU.add))
                    for i in range(2):
                        t = gate_tmp[:, j % 2, i]
                        ct = 22 * i + j
                        if i == 0:
                            after(n)
                        ins = V.scalar_tensor_tensor(out=t[:, 0:S - 1], in0=b[:, i, 1:S], scalar=col("conv_w", 88 + ct),
                                                     in1=t[:, 0:S - 1], op0=ALU.mult, op1=ALU.add)
                    ins.then_inc(freed["dve"], 1)
                if j >= 1:
                    i = j - 1
                    dve.wait_ge(gelu_done, i + 1)
                    V.tensor_tensor(ff[:, i], gate_tmp[:, i % 2, 0], gate_tmp[:, i % 2, 1], ALU.mult
                                    ).then_inc(ff_ready, 1)
            for j in range(4):
                dve.wait_ge(fill_done, fi("down2", j) + 1)
                V.tensor_tensor(x[:, 2 * j:2 * j + 2], x[:, 2 * j:2 * j + 2], bank("down2", j)[:], ALU.add
                                ).then_inc(freed["dve"], 1)
            root("final", rstd[:, 0:S])
            for t in range(KT):
                ins = V.scalar_tensor_tensor(out=y[:, t], in0=x[:, t], scalar=col("norm_final", t), in1=rstd[:, 0:S],
                                             op0=ALU.mult, op1=ALU.mult)
                if t % 4 == 3:
                    ins.then_inc(out_ready, 1)

        @block.tensor
        def _(pe):
            mm = nc.tensor.matmul
            at_block = [0]

            def weight():
                b = at_block[0]
                at_block[0] += 1
                slot = b // 16
                if b % 16 == 0:
                    pe.wait_ge(slot_ready[slot % RING], 16 * (slot // RING + 1))
                return ring[:, slot % RING, b % 16]

            def open_fill(name, j):
                n = fi(name, j)
                if n >= PJ:
                    who = FILLS[n - PJ][3]
                    pe.wait_ge(freed[who], freed_count(n - PJ, who))
                assert at_block[0] == FIRST_BLOCK[n]
                return pj[n % PJ]

            def tile_out(dst, src, kts=KT, ready=None):
                for kt in range(kts):
                    w = weight()
                    if ready is not None:
                        pe.wait_ge(ready[0], ready[1] + kt + 1)
                    last = mm(dst, w, src[:, kt], start=kt == 0, stop=kt == kts - 1)
                return last

            def pair(name, j, src, kts=KT, ready=None):
                b = open_fill(name, j)
                tile_out(b[:, 0], src, kts, ready if j == 0 else None)
                tile_out(b[:, 1], src, kts).then_inc(fill_done, 1)

            def token_pair(name, j, src):
                b = open_fill(name, j)
                for u in range(2):
                    ws = [weight() for _ in range(KT)]
                    for tt in range(2):
                        for kt in range(KT):
                            last = mm(b[:, tt, u * P:u * P + P], src[:, kt, tt * P:tt * P + P], ws[kt],
                                      start=kt == 0, stop=kt == KT - 1)
                last.then_inc(fill_done, 1)

            def wait_stat(name):
                if STAT[name]:
                    pe.wait_ge(stat_read, STAT[name])

            def norm_stat(name, chunks, matrix="m1024", src=None):
                wait_stat(name)
                for c in range(chunks):
                    stat_chunk(name, c, chunks, matrix)

            def stat_chunk(name, c, chunks, matrix="m1024"):
                if c == 0:
                    wait_stat(name)
                pe.wait_ge(sq_ready, SQ_BEFORE[name] + c + 1)
                per = KT // chunks
                for t in range(c * per, c * per + per):
                    last = mm(st[:, 0:S], mat(matrix), sq[:, t], start=t == 0, stop=t == KT - 1)
                if c == chunks - 1:
                    last.then_inc(stat_done, 1)

            pe.wait_ge(load_params, 32)
            norm_stat("mix_pre", 2)
            for j in range(4):
                pair("conv", j, h, ready=(h_ready, H_TILES["mix_pre"]))
                if j == 0:
                    norm_stat("mem", 2)
            for j in range(4):
                pair("qk", j, h)
            for j in range(2):
                token_pair("v", j, h)
            for j in range(2):
                pair("g", j, h)
            for j in range(2):
                pair("memk", j, mem_n, ready=(mem_ready, 0))
            for j in range(2):
                token_pair("memv", j, mem_n)
            pe.wait_ge(conv_ready, 1)
            wait_stat("ln_mean")
            for t in range(4):
                last = mm(st[:, 0:S], mat("m512"), conv_y[:, t], start=t == 0, stop=t == 3)
            last.then_inc(stat_done, 1)
            pe.wait_ge(rope_ready, 2)
            for hd in range(RET):
                mm(sc[hd][:, 0:S], k_raw[:, hd, 0:P], q_raw[:, hd, :], start=True, stop=True)
                mm(sc[hd][:, S:S + P], k_raw[:, hd, P:S], q_raw[:, hd, P:S], start=True, stop=True
                   ).then_inc(sc_done, 1)
            pe.wait_ge(conv_ready, 2)
            wait_stat("ln_var")
            pe.wait_ge(sq_ready, SQ_BEFORE["ln_var"] + 1)
            for t in range(4):
                last = mm(st[:, 0:S], mat("m512"), sq[:, t], start=t == 0, stop=t == 3)
            last.then_inc(stat_done, 1)
            for hd in range(RET):
                pe.wait_ge(s_ready, hd + 1)
                mm(sc[hd][:, 0:S], v_ret[:, 0, hd * P:hd * P + P], s_ret[:, hd, 0:S], start=True, stop=False)
                mm(sc[hd][:, P:S], v_ret[:, 1, hd * P:hd * P + P], s_ret[:, hd, S:S + P], start=False, stop=True
                   ).then_inc(sc_done, 1)
            for g in range(2):
                pe.wait_ge(sq_ready, SQ_BEFORE[f"ret{g}"] + 1)
                wait_stat(f"ret{g}")
                for a in range(2):
                    last = mm(st[:, a * S:a * S + S], mat("m128"), sq[:, 4 + 2 * g + a], start=True, stop=True)
                last.then_inc(stat_done, 1)
            pe.wait_ge(mix_conv, 4)
            pe.wait_ge(mix_ret, 2)
            for j in range(4):
                pair("wout", j, mix)
                if j:
                    stat_chunk("mix_post", j - 1, 4)
            stat_chunk("mix_post", 3, 4)
            norm_stat("ffn_pre", 2)
            for j in range(22):
                pair("ff", j, h, ready=(h_ready, H_TILES["ffn_pre"]))
            pe.wait_ge(freed["dve"], freed_count(fi("ff", 21), "dve"))
            for j in range(4):
                pair("down", j, ff, FT)
                if j:
                    stat_chunk("ffn_post", j - 1, 4)
            stat_chunk("ffn_post", 3, 4)
            pe.wait_ge(load_side, 64)
            for j in range(4):
                for i in range(2):
                    for kt in range(2):
                        last = mm(sc[j][:, i * S:i * S + S], w_ple[:, kt, (2 * j + i) * P:(2 * j + i + 1) * P],
                                  p_in[:, kt], start=kt == 0, stop=kt == 1)
                last.then_inc(sc_done, 1)
            pe.wait_ge(x_ready, X_HALF["ffn_post"] + 2)
            for j in range(4):
                pair("ple", j, x)
                if j:
                    stat_chunk("ple_post", j - 1, 4)
            stat_chunk("ple_post", 3, 4)
            norm_stat("mix2", 2)

            for j in range(4):
                pair("hq", j, h, ready=(h_ready, H_TILES["mix2"]))
            for stage in ("hff", "hfb"):
                for j in range(4):
                    pair(stage, j, h)

            def tile(t, hd, tt):
                return t[:, hd, tt * P:tt * P + P]

            def diagonal():
                pe.wait_ge(level_ready, 1)
                pe.wait_ge(ple_proj, 4)
                for g in range(4):
                    for a in range(2):
                        for tt in range(2):
                            c = (2 * a + tt) * P
                            last = mm(sc[g][:, c:c + P], tile(ksum, 2 * g + a, tt), tile(q_s, 2 * g + a, tt),
                                      start=True, stop=True)
                    last.then_inc(sc_done, 1)

            def level(i):
                b = LEVELS[i]
                pe.wait_ge(level_ready, i + 1)
                for g in range(4):
                    if i == 0:
                        pe.wait_ge(st_diag, g + 1)
                    else:
                        pe.wait_ge(st_mask, 4 * (i - 1) + g + 1)
                    for a in range(2):
                        for tt in range(2):
                            c = (2 * a + tt) * P
                            o = sc[g][:, c:c + P].rearrange("p (n two b) -> p n two b", two=2, b=b)
                            for k, q, side in ((k_f, q_f, 1), (k_b, q_b, 0)):
                                r = tile(q, 2 * g + a, tt).rearrange("p (n two b) -> p n two b", two=2, b=b)
                                last = mm(o[:, :, side], tile(k, 2 * g + a, tt), r[:, :, side],
                                          start=True, stop=True)
                    last.then_inc(sc_done, 1)

            def cross():
                pe.wait_ge(level_ready, 1 + len(LEVELS))
                for g in range(4):
                    pe.wait_ge(st_mask, 4 * (len(LEVELS) - 1) + g + 1)
                    for a in range(2):
                        hd = 2 * g + a
                        mm(sc[g][:, a * S:a * S + P], tile(k_f, hd, 0), tile(q_f, hd, 1), start=True, stop=True)
                        last = mm(sc[g][:, a * S + P:a * S + S], tile(k_b, hd, 1), tile(q_b, hd, 0),
                                  start=True, stop=True)
                    last.then_inc(sc_done, 1)

            def hg_values():
                for g in range(4):
                    pe.wait_ge(st_cross, g + 1)
                    for a in range(2):
                        hd = 2 * g + a
                        o = sc[g][:, a * S:a * S + S]
                        mm(o, v_hg[:, 0, hd * P:hd * P + P], st_hg[:, hd, 0:S], start=True, stop=False)
                        last = mm(o, v_hg[:, 1, hd * P:hd * P + P], st_hg[:, hd, S:2 * S], start=False, stop=True)
                    last.then_inc(sc_done, 1)

            for e, (name, j) in enumerate(SIDE_FILLS):
                if name in ("hi", "nv"):
                    token_pair(name, j, h)
                else:
                    pair(name, j, h)
                if e == 0:
                    diagonal()
                if e % 2 == 1 and e // 2 < len(LEVELS):
                    level(e // 2)
            cross()
            wait_read(pe, "hi", 3)
            hg_values()
            for g in range(4):
                pe.wait_ge(sq_ready, SQ_BEFORE[f"hg{g}"] + 1)
                wait_stat(f"hg{g}")
                for a in range(2):
                    last = mm(st[:, a * S:a * S + S], mat("m128"), sq[:, 2 * g + a], start=True, stop=True)
                last.then_inc(stat_done, 1)

            def att_scores(a):
                if a < 2:
                    pe.wait_ge(o_copied, RET + 4)
                    wait_read(pe, "hg", 3)
                elif a < NA + 2:
                    pe.wait_ge(exp_ready, a - 1)
                else:
                    pe.wait_ge(exp_ready, a - 1)
                for t in range(2):
                    o = sc[a % 2][:, t * S:t * S + S]
                    if a < NA:
                        lo = 64 * (a % 2)
                        last = mm(o, q_na[lo:lo + 64, a // 2, t * P:t * P + P], k_na[lo:lo + 64, a // 2, :],
                                  start=True, stop=True)
                    else:
                        last = mm(o, q_ca[:, a - NA, t * P:t * P + P], mem_k[:, a - NA, :], start=True, stop=True)
                last.then_inc(scored, 1)

            def att_transpose(a):
                pe.wait_ge(p_ready, a + 1)
                if a:
                    pe.wait_ge(pt_ready, a)
                for jt in range(2):
                    for t in range(2):
                        last = nc.tensor.transpose(sc[2][:, jt * S + t * P:jt * S + t * P + P],
                                                   probs[:, a % 2, t * S + jt * P:t * S + jt * P + P],
                                                   mat("ident"))
                last.then_inc(turned, 1)

            def att_values(a):
                pe.wait_ge(pt_ready, a + 1)
                if a < NA:
                    if a >= 2 and a % 2 == 0:
                        pe.wait_ge(o_att, a // 2)
                    o = sc[3][64 * (a % 2):64 * (a % 2) + 64, 0:S]
                    v = v_na[:, :, a * 64:a * 64 + 64]
                else:
                    pe.wait_ge(o_att, a - NA + 4)
                    o = sc[3][:, 0:S]
                    v = mem_v[:, :, (a - NA) * P:(a - NA + 1) * P]
                for jt in range(2):
                    last = mm(o, v[:, jt], probs_t[:, a % 2, jt * S:jt * S + S], start=jt == 0, stop=jt == 1)
                last.then_inc(pv_done, 1)

            def att_slot(i):
                if i < NA + CA:
                    att_scores(i)
                if 1 <= i <= NA + CA:
                    att_transpose(i - 1)
                if 2 <= i < NA + CA + 2:
                    att_values(i - 2)

            att_slot(0)
            att_slot(1)
            for i, (name, j) in enumerate(MERGE_FILLS):
                b = open_fill(name, j)
                tile_out(b[:, 0], h)
                if name == "mhg":
                    pe.wait_ge(hg_out, 4)
                    last = tile_out(b[:, 1], o_hg)
                elif name == "mna":
                    pe.wait_ge(o_att, 4)
                    last = tile_out(b[:, 1], o_na, 4)
                else:
                    pe.wait_ge(o_att, 8)
                    last = tile_out(b[:, 1], o_ca, 4)
                last.then_inc(fill_done, 1)
                att_slot(i + 2)
            for j in range(4):
                pair("wout2", j, merged, ready=(merge_ready, 0))
            norm_stat("ffn2", 2)
            for j in range(22):
                pair("up", j, h, ready=(h_ready, H_TILES["ffn2"]))
            pe.wait_ge(ff_ready, 22)
            for j in range(4):
                pair("down2", j, ff, FT)
            norm_stat("final", 2)


def host_layout(inputs):
    f = np.float32

    def blocks(w, cols):
        k = w.shape[0] // P
        return [[w[kt * P:(kt + 1) * P, m * P:(m + 1) * P] for kt in range(k)] for m in cols]

    def vecs(a, tiles):
        return np.asarray(a, f).reshape(-1, tiles, P).transpose(2, 0, 1).reshape(P, -1)

    g = {k: np.asarray(v) for k, v in inputs.items()}
    w_in, w_in2 = g["w_in"][0], g["w_in_2"][0]
    stream = []

    def add(*tiles):
        for t in tiles:
            stream.extend(t)

    a = blocks(w_in, range(24))
    for j in range(4):
        add(a[j], a[4 + j])
    add(*a[8:24])
    add(*blocks(g["w_mem_kv_2"][0], range(8)))
    add(*blocks(g["w_out"][0], range(8)))
    gate, up = blocks(g["w_ffn_gate"][0], range(FT)), blocks(g["w_ffn_up"][0], range(FT))
    for j in range(FT):
        add(gate[j], up[j])
    add(*blocks(g["w_ffn_down"][0], range(8)))
    add(*blocks(g["w_ple_gate"][0], range(8)))
    b = blocks(w_in2, range(80))
    add(*b[0:8], *b[16:24], *b[24:32], *b[8:16], *b[40:56], *b[32:40])
    for base, w in ((56, g["w_hg_o_2"][0]), (64, g["w_na_o_2"][0]), (72, g["w_ca_o_2"][0])):
        o = blocks(w, range(8))
        for j in range(8):
            add(b[base + j], o[j])
    add(*blocks(g["w_out_2"][0], range(8)))
    u = blocks(g["w_up_2"][0], range(2 * FT))
    for j in range(FT):
        add(u[j], u[FT + j])
    add(*blocks(g["w_down_2"][0], range(8)))
    assert len(stream) == NBLOCKS, (len(stream), NBLOCKS)
    wstream = np.empty((NSLOTS, P, 16, P), f)
    for n, blk in enumerate(stream):
        wstream[n // 16, :, n % 16] = blk

    vec = np.concatenate([
        vecs(g["mix_pre_norm"], 8), vecs(g["conv_dw_w"][0], 4), vecs(g["conv_dw_b"], 4), vecs(g["conv_ln_w"], 4),
        vecs(g["conv_ln_b"], 4), vecs(g["mix_post_norm"], 8), vecs(g["ffn_pre_norm"], 8),
        vecs(g["ffn_post_norm"], 8), vecs(g["ple_post_norm"], 8), vecs(g["norm_mix_2"], 8),
        vecs(g["hg_lb_logits_2"][0], 8), vecs(g["hg_gnorm_2"], 1), vecs(g["mem_norm_2"], 8),
        vecs(g["norm_ffn_2"], 8), vecs(g["conv_w_2"][0], 44), vecs(g["conv_b_2"], 44),
        vecs(g["norm_final_2"], 8)], axis=1)
    assert vec.shape == (P, NVEC)

    idx = np.arange(P)
    con = [np.full((P, P), 1.0 / n, f) for n in (1024, 512, 128)] + [np.eye(P, dtype=f)]
    for b_ in LEVELS:
        same = (idx[:, None] // (2 * b_)) == (idx[None, :] // (2 * b_))
        apart = (idx[:, None] // b_) != (idx[None, :] // b_)
        con.append((same & apart).astype(f))
    con = np.concatenate(con, axis=1)
    half = P // 2
    freqs = (10000.0 ** (-np.arange(half, dtype=f) / half)).astype(f)
    ang = (np.arange(S, dtype=f)[None, :] * freqs[:, None]).astype(f).astype(np.float64)
    cos, sin = np.cos(ang).astype(f), np.sin(ang).astype(f)
    rope = np.stack([np.concatenate([cos, cos]), np.concatenate([sin, -sin])], axis=1)
    decay = np.zeros((P, RET, 384), np.float64)
    rel = (np.arange(S)[None, :] - idx[:, None]).astype(np.float64)
    for hd in range(RET):
        lg = np.float64(np.log(f(1.0 - 2.0 ** (-5.0 - hd))))
        d = np.where(rel >= 0, np.exp(lg * np.maximum(rel, 0.0)), 0.0) * float(P) ** -0.5
        decay[:, hd, 0:S] = d
        decay[:, hd, S:] = d[:, 0:P]

    def act_t(a, tiles):
        return np.ascontiguousarray(a.reshape(S, tiles, P).transpose(2, 1, 0))

    return {
        "xt": act_t(g["x"], 8), "memt": act_t(g["mem_2"], 8), "pt": act_t(g["p"], 2),
        "wstream": wstream,
        "wproj": np.ascontiguousarray(g["w_ple_proj"][0].reshape(2, P, D).transpose(1, 0, 2)),
        "vecs": np.ascontiguousarray(vec), "consts": np.ascontiguousarray(con, dtype=f),
        "rope_tab": np.ascontiguousarray(rope, dtype=f), "decay_tab": decay.astype(f),
        "rpb": np.ascontiguousarray(g["na_rpb_2"][0].reshape(NA * 15, 31)[:, ::-1]),
    }


def kernel(**inputs):
    import concourse.bacc as bacc
    from concourse.bass_utils import run_bass_kernel_spmd

    arrays = host_layout(inputs)
    nc = bacc.Bacc("TRN2", target_bir_lowering=False, num_devices=1)
    args = {k: nc.dram_tensor(k, v.shape, F32, kind="ExternalInput").ap() for k, v in arrays.items()}
    out = nc.dram_tensor("out_t", (P, KT, S), F32, kind="ExternalOutput").ap()
    toep = nc.dram_tensor("toep", (NA * 15, P), F32, kind="Internal").ap()
    program(nc, out=out, toep=toep, **args)
    r = run_bass_kernel_spmd(nc, [arrays], core_ids=[0])
    got = r.results[0]["out_t"]
    return np.ascontiguousarray(got.transpose(2, 1, 0)).reshape(1, S, D)
```

```python
from contextlib import ExitStack

import numpy as np
import concourse.bass as bass
from concourse import mybir

P = 128
D = 1024
S = 256
KT = D // P
DC = 512
DFF = 2816
FT = DFF // P
CW = 31
EPS = 1e-6
HG = 8
NA = 8
CA = 4
RET = 4
RAW = 3
UNITS = 4
UB = 8
PJ = 3

ALU = mybir.AluOpType
ACT = mybir.ActivationFunctionType
F32 = mybir.dt.float32
R32 = mybir.dt.float32r
I32 = mybir.dt.int32
AX = mybir.AxisListType

STAGES = [
    ("conv", 4, 16, "dve"), ("qk", 4, 16, "act"), ("v", 2, 16, "act"), ("g", 2, 16, "act"),
    ("memk", 2, 16, "act"), ("memv", 2, 16, "act"), ("wout", 4, 16, "act"),
    ("ff", 22, 16, "dve"), ("down", 4, 2 * FT, "act"), ("ple", 4, 16, "dve"),
    ("hff", 4, 16, "act"), ("hfb", 4, 16, "act"), ("hq", 4, 16, "act"), ("hi", 4, 16, "act"),
    ("nq", 2, 16, "act"), ("nk", 2, 16, "act"), ("nv", 2, 16, "act"), ("cq", 2, 16, "act"),
    ("hg", 4, 16, "act"), ("mhg", 8, 16, "dve"), ("mna", 8, 12, "dve"), ("mca", 8, 12, "dve"),
    ("wout2", 4, 16, "dve"), ("up", 22, 16, "dve"), ("down2", 4, 2 * FT, "dve"),
]
FILLS = [(name, j, nb, who) for name, n, nb, who in STAGES for j in range(n)]
INDEX = {(name, j): n for n, (name, j, _, _) in enumerate(FILLS)}
FIRST_BLOCK = [sum(f[2] for f in FILLS[:n]) for n in range(len(FILLS) + 1)]
NBLOCKS = FIRST_BLOCK[-1]
NSLOTS = NBLOCKS // 16
NUNITS = NBLOCKS // UB
TOKEN_STAGES = ("v", "memv", "hi", "nv")

_ENDS = sorted({FIRST_BLOCK[n + 1] for n in range(len(FILLS))} | {UB * (u + 1) for u in range(NUNITS)})
STEP = {end: n + 1 for n, end in enumerate(_ENDS)}


def fill_step(n):
    return STEP[FIRST_BLOCK[n + 1]]


def unit_step(u):
    return STEP[UB * (u + 1)]


_BUSY = [(INDEX[("qk", 0)], INDEX[("memv", 1)]), (INDEX[("hq", 0)], INDEX[("cq", 1)])]


def _lo_engine(u):
    busy = any(FIRST_BLOCK[a] <= UB * u < FIRST_BLOCK[b + 1] for a, b in _BUSY)
    return "dve" if u % 4 == 0 or (u % 4 == 2 and not busy) else "pool"


LO_ENGINE = [_lo_engine(u) for u in range(NUNITS)]

STATS = [("mix_pre", 2), ("mem", 2), ("ln_mean", 0), ("ln_var", 1), ("ret0", 1), ("ret1", 1),
         ("mix_post", 4), ("ffn_pre", 2), ("ffn_post", 4), ("ple_post", 4), ("mix2", 2),
         ("hg0", 1), ("hg1", 1), ("hg2", 1), ("hg3", 1), ("ffn2", 2), ("final", 2)]
STAT = {name: n for n, (name, _) in enumerate(STATS)}
ROOTS = [name for name, _ in STATS if name != "ln_mean"]
SQ_BEFORE = {name: sum(c for _, c in STATS[:n]) for n, (name, _) in enumerate(STATS)}

VEC_SIZES = [("mix_pre", 8), ("dw_w", 4 * CW), ("dw_b", 4), ("ln_w", 4), ("ln_b", 4), ("mix_post", 8),
             ("ffn_pre", 8), ("ffn_post", 8), ("ple_post", 8), ("norm_mix2", 8), ("lb", 16), ("gnorm", 1),
             ("mem_norm", 8), ("norm_ffn2", 8), ("conv_w", 3 * 44), ("conv_b", 44), ("norm_final", 8)]
VEC = {}
for _n, _c in VEC_SIZES:
    VEC[_n] = sum(c for n, c in VEC_SIZES[:len(VEC)])
NVEC = sum(c for _, c in VEC_SIZES)

CONST = {"m1024": 0, "m512": P, "m128": 2 * P, "ident": 3 * P, "mask": 4 * P}
LEVELS = [1, 2, 4, 8, 16, 32, 64]
NCONST = 4 * P + len(LEVELS) * P


def lo_count(u, who):
    return sum(1 for e in LO_ENGINE[:u + 1] if e == who)


def split_target(n):
    return min(NUNITS, max(FIRST_BLOCK[n] // UB + UNITS, -(-FIRST_BLOCK[n + 1] // UB)))


def behind_target(n):
    return min(NUNITS, FIRST_BLOCK[n + 1] // UB + UNITS)


def freed_count(n, who):
    return sum(1 for f in FILLS[:n + 1] if f[3] == who)


def program(nc, xt, memt, pt, wstream, wproj, vecs, consts, rope_tab, decay_tab, rpb, out, toep):
    ctx = ExitStack()
    with ctx:
        def sb(name, shape):
            return ctx.enter_context(nc.sbuf_tensor(name, [P] + shape, F32))

        def sem(name):
            return ctx.enter_context(nc.semaphore(name))

        base = nc.sbuf_base
        fence = sb("fence", [52800])
        top = [(base + 31) // 32 * 32]

        def place(name, shape, dt=F32, offset=None):
            size = int(np.prod(shape)) * 4
            if offset is None:
                offset = top[0]
                top[0] += (size + 31) // 32 * 32
            assert offset + size <= base + 4 * 52800, (name, offset + size - base)
            return nc.alloc_sbuf_tensor_at(name, [P] + shape, dt, offset=offset)

        raw = place("raw", [RAW, 16, P])
        w_hi = place("w_hi", [UNITS, UB, P], R32)
        w_lo = place("w_lo", [UNITS, UB, P], R32)
        x = place("x", [KT, S])
        y = place("y", [KT, S])
        sq = place("sq", [KT, S])
        h = place("h", [2, KT, S], R32)
        vec = place("vec", [NVEC])
        con = place("con", [NCONST])
        rstd = place("rstd", [2 * S])
        rstd_h = place("rstd_h", [S])
        std = place("std", [2 * S])
        eps = place("eps", [1])
        gate_tmp = place("gate_tmp", [2, 2, S])
        prod_tmp = place("prod_tmp", [2, S])
        mem_k = place("mem_k", [CA, S])
        mem_v = place("mem_v", [2, DC])
        lb = place("lb", [6, 16])
        soft = place("soft", [2, 3, 2])
        arena = top[0]

        def at(kib, name, *shape, dt=F32):
            return place(name, list(shape), dt, offset=arena + int(1024 * kib))

        conv_in = at(0, "conv_in", 4, CW - 1 + S)
        conv_y = at(5, "conv_y", 4, S)
        q_raw = at(9, "q_raw", RET, S)
        k_raw = at(13, "k_raw", RET, S)
        v_ret = at(17, "v_ret", 2, DC)
        g_ret = at(21, "g_ret", RET, S)
        o_ret = at(25, "o_ret", RET, S)
        s_ret = at(29, "s_ret", RET, 384)
        decay = at(35, "decay", RET, 384)
        rope_a = at(41, "rope_a", RET, S)
        rope_b = at(45, "rope_b", RET, S)
        rope = at(49, "rope", 2, S)
        mem_n = at(51, "mem_n", 2, KT, S, dt=R32)
        mix = at(51, "mix", 2, KT, S, dt=R32)
        ff = at(0, "ff", 2, FT, S, dt=R32)
        w_ple = at(44, "w_ple", 2, D)
        p_in = at(52, "p_in", 2, S)
        ple_p = at(54, "ple_p", KT, S)
        x_split = at(62, "x_split", 2, KT, S, dt=R32)
        f_f = at(0, "f_f", HG, S)
        f_b = at(8, "f_b", HG, S)
        k_f = at(16, "k_f", HG, S)
        k_b = at(24, "k_b", HG, S)
        q_f = at(32, "q_f", HG, S)
        q_b = at(40, "q_b", HG, S)
        v_hg = at(48, "v_hg", 2, D)
        st_hg = at(56, "st_hg", HG, 4 * P)
        v_na = at(72, "v_na", 2, DC)
        q_ca = at(76, "q_ca", CA, S)
        toep_t = at(0, "toep_t", NA, 6 * 64)
        o_hg = at(16, "o_hg", HG, S)
        gate_hg = at(24, "gate_hg", HG, S)
        merged = at(24, "merged", KT, S)
        o_hg_s = at(32, "o_hg_s", 2, HG, S, dt=R32)
        merged_s = at(32, "merged_s", 2, KT, S, dt=R32)
        probs = at(48, "probs", 2, 2 * S)
        probs_t = at(52, "probs_t", 2, 2 * S)
        o_na = at(56, "o_na", 2, 4, S, dt=R32)
        o_ca = at(64, "o_ca", 2, 4, S, dt=R32)
        ksum = sq
        q_s = y
        q_na, k_na = y[:, 0:4], y[:, 4:8]
        mem_x = y

        pj = [ctx.enter_context(nc.psum_tensor(f"pj{i}", [P, 2, S], F32)) for i in range(PJ)]
        sc = [ctx.enter_context(nc.psum_tensor(f"sc{i}", [P, 512], F32)) for i in range(4)]
        st = ctx.enter_context(nc.psum_tensor("st", [P, 512], F32))

        load_x = sem("load_x")
        load_params = sem("load_params")
        load_mem = sem("load_mem")
        load_side = sem("load_side")
        slot_ready = [sem(f"slot_ready{i}") for i in range(RAW)]
        hi_ready = sem("hi_ready")
        lo_ready = {"dve": sem("lo_ready_dve"), "pool": sem("lo_ready_pool")}
        pe_step = sem("pe_step")
        load_ple = sem("load_ple")
        h_full = sem("h_full")
        h_hi = sem("h_hi")
        mem_full = sem("mem_full")
        mem_hi = sem("mem_hi")
        mix_full = sem("mix_full")
        mix_hi = sem("mix_hi")
        mix_ready = sem("mix_ready")
        ret_full = sem("ret_full")
        f_hi = sem("f_hi")
        up_full = sem("up_full")
        xs_hi = sem("xs_hi")
        xs_ready = sem("xs_ready")
        hg_hi = sem("hg_hi")
        hg_split = sem("hg_split")
        att_ready = sem("att_ready")
        merge_full = sem("merge_full")
        merge_hi = sem("merge_hi")
        freed = {"act": sem("freed_act"), "dve": sem("freed_dve")}
        gate_done = sem("gate_done")
        sq_ready = sem("sq_ready")
        stat_done = sem("stat_done")
        root_done = sem("root_done")
        eps_ready = sem("eps_ready")
        stat_read = sem("stat_read")
        h_ready = sem("h_ready")
        x_ready = sem("x_ready")
        mem_ready = sem("mem_ready")
        pad_ready = sem("pad_ready")
        conv_ready = sem("conv_ready")
        rope_ready = sem("rope_ready")
        sc_done = sem("sc_done")
        s_ready = sem("s_ready")
        o_copied = sem("o_copied")
        lb_exp = sem("lb_exp")
        lb_ready = sem("lb_ready")
        ple_proj = sem("ple_proj")
        ple_mul = sem("ple_mul")
        ff_ready = sem("ff_ready")
        gates_ready = sem("gates_ready")
        level_ready = sem("level_ready")
        st_diag = sem("st_diag")
        st_mask = sem("st_mask")
        st_cross = sem("st_cross")
        hg_out = sem("hg_out")
        toep_zero = sem("toep_zero")
        toep_row = sem("toep_row")
        toep_load = sem("toep_load")
        toep_sel = sem("toep_sel")
        zero_ready = sem("zero_ready")
        logits_ready = sem("logits_ready")
        exp_ready = sem("exp_ready")
        p_ready = sem("p_ready")
        turned = sem("turned")
        pt_ready = sem("pt_ready")
        scored = sem("scored")
        pv_done = sem("pv_done")
        o_att = sem("o_att")
        merge_ready = sem("merge_ready")
        up_lin = sem("up_lin")
        up_conv = sem("up_conv")
        gelu_done = sem("gelu_done")
        dve_chain = sem("dve_chain")
        act_chain = sem("act_chain")
        pool_chain = sem("pool_chain")
        out_ready = sem("out_ready")
        stored = sem("stored")

        def col(name, i=0):
            c = VEC[name] + i
            return vec[:, c:c + 1]

        def mat(name, i=0):
            c = CONST[name] + i * P
            return con[:, c:c + P]

        def fi(name, j=0):
            return INDEX[(name, j)]

        def bank(name, j):
            return pj[fi(name, j) % PJ]

        def gate_slot(name, j):
            return (freed_count(fi(name, j), "dve") - 1) % 2

        def wait_gate_slot(eng, name, j):
            d = freed_count(fi(name, j), "dve") - 1
            if d >= 2:
                eng.wait_ge(freed["dve"], d - 1)

        def wait_read(eng, name, j):
            n = fi(name, j)
            eng.wait_ge(freed[FILLS[n][3]], freed_count(n, FILLS[n][3]))

        H_PAIRS = {"mix_pre": 0, "ffn_pre": 4, "mix2": 8, "ffn2": 12}
        X_HALF = {"mix_post": 0, "ffn_post": 2, "ple_post": 4}
        SC_RET, SC_RO = 0, RET
        SC_LEVEL = 2 * RET
        SC_CROSS = SC_LEVEL + 4 * (1 + len(LEVELS))
        SC_HGO = SC_CROSS + 4

        def diag_view(g):
            v = st_hg[:, 2 * g:2 * g + 2].rearrange("p a (b c) -> p a b c", c=P)
            return v[:, :, 0:4:3]

        SIDE_FILLS = [(name, j) for name, j, _, _ in FILLS if name in ("hi", "nq", "nk", "nv", "cq")]
        MERGE_FILLS = [(name, j) for name, j, _, _ in FILLS if name in ("mhg", "mna", "mca")]

        def unit_of_raw(u):
            return raw[:, (u // 2) % RAW, UB * (u % 2):UB * (u % 2) + UB]

        def as_f32(v):
            return v.bitcast(F32)

        block = ctx.enter_context(nc.Block())

        @block.sync
        def _(sp):
            sp.dma_start(x[:], xt).then_inc(load_x, 16)
            sp.dma_start(con[:], consts).then_inc(load_params, 16)
            sp.dma_start(vec[:], vecs).then_inc(load_params, 16)
            for n in range(NSLOTS):
                if n >= RAW:
                    for who in ("dve", "pool"):
                        c = lo_count(2 * (n - RAW) + 1, who)
                        if c:
                            sp.wait_ge(lo_ready[who], c)
                sp.dma_start(raw[:, n % RAW], wstream[n]).then_inc(slot_ready[n % RAW], 16)
                if n == 1:
                    sp.dma_start(mem_x[:], memt).then_inc(load_mem, 16)
                if n == 6:
                    sp.dma_start(rope[:], rope_tab).then_inc(load_side, 16)
                    sp.dma_start(decay[:], decay_tab).then_inc(load_side, 16)
                if n == fi("ff", 4):
                    sp.wait_ge(pe_step, fill_step(fi("ff", 0)))
                    sp.dma_start(p_in[:], pt).then_inc(load_ple, 16)
                    sp.dma_start(w_ple[:], wproj).then_inc(load_ple, 16)
            sp.wait_ge(out_ready, 2)
            sp.dma_start(out, y[:]).then_inc(stored, 16)
            sp.wait_ge(stored, 16)

        @block.gpsimd
        def _(pool):
            chain = [0]

            def link(ins):
                chain[0] += 1
                ins.then_inc(pool_chain, 1)
                return chain[0]

            nc.gpsimd.memset(conv_in[:, :, 0:CW - 1], 0.0).then_inc(pad_ready, 1)
            nc.gpsimd.memset(prod_tmp[:, 0, 0:P], 0.0).then_inc(zero_ready, 1)
            pool.wait_ge(zero_ready, 1)
            pool.dma_start(toep, prod_tmp[0:NA * 15, 0, 0:P]).then_inc(toep_zero, 16)
            pool.wait_ge(toep_zero, 16)
            pool.dma_start(toep[:, 48:79], rpb).then_inc(toep_row, 16)
            pool.wait_ge(toep_row, 16)

            fed = [0]

            def feed(target):
                for u in range(fed[0], target):
                    if LO_ENGINE[u] == "pool":
                        pool.wait_ge(hi_ready, u + 1)
                        nc.gpsimd.tensor_tensor(w_lo[:, u % UNITS], unit_of_raw(u), as_f32(w_hi[:, u % UNITS]),
                                                ALU.subtract).then_inc(lo_ready["pool"], 1)
                fed[0] = max(fed[0], target)

            feed(split_target(fi("hg", 1)))
            pool.wait_ge(level_ready, 1 + len(LEVELS))
            for half in range(2):
                for hd in range(NA):
                    off = (hd * 15 + 5 - half) * P
                    src = bass.AP(tensor=toep.tensor, offset=toep.offset + off, ap=[[1, 64], [P, 6], [1, 64]])
                    pool.dma_start(toep_t[64 * half:64 * half + 64, hd].rearrange("p (d c) -> p d c", c=64),
                                   src).then_inc(toep_load, 16)
            feed(split_target(fi("hg", 3)))
            pool.wait_ge(toep_load, 16 * 2 * NA)
            for half in range(2):
                v = toep_t[64 * half:64 * half + 64].rearrange("p a (d c) -> p (a d) c", c=64)
                lo, hi = v[:, :, 16:64], v[:, :, 0:48]
                a = link(nc.gpsimd.affine_select(out=lo, in_=lo, compare_op=ALU.is_ge, fill=-1e30, base=55,
                                                 pattern=[[0, NA * 6], [-1, 48]], channel_multiplier=-1))
                pool.wait_ge(pool_chain, a)
                nc.gpsimd.affine_select(out=hi, in_=hi, compare_op=ALU.is_ge, fill=-1e30, base=-56,
                                        pattern=[[0, NA * 6], [1, 48]], channel_multiplier=1
                                        ).then_inc(toep_sel, 1)
            pool.wait_ge(toep_sel, 2)
            feed(NUNITS)

        @block.scalar
        def _(act):
            A = nc.scalar.activation
            chain = [0]

            fed = [0]

            def feed(target):
                for u in range(fed[0], target):
                    if u % 2 == 0:
                        act.wait_ge(slot_ready[(u // 2) % RAW], 16 * (u // 2 // RAW + 1))
                    if u >= UNITS:
                        act.wait_ge(pe_step, unit_step(u - UNITS))
                    nc.scalar.copy(w_hi[:, u % UNITS], unit_of_raw(u)).then_inc(hi_ready, 1)
                fed[0] = max(fed[0], target)

            def squares_of_x(stage):
                for i in range(2):
                    if stage in X_HALF:
                        act.wait_ge(x_ready, X_HALF[stage] + i + 1)
                    elif stage is not None:
                        wait_read(act, stage, 2 * i + 1)
                    A(sq[:, 4 * i:4 * i + 4], x[:, 4 * i:4 * i + 4], ACT.Square).then_inc(sq_ready, 1)

            def hi_of_h(name):
                for p in range(4):
                    act.wait_ge(h_full, H_PAIRS[name] + p + 1)
                    nc.scalar.copy(h[:, 0, 2 * p:2 * p + 2], sq[:, 2 * p:2 * p + 2]).then_inc(h_hi, 1)

            def root(name, n=S):
                act.wait_ge(stat_done, STAT[name] + 1)
                if STAT[name]:
                    act.wait_ge(stat_read, STAT[name])
                A(std[:, 0:n], st[:, 0:n], ACT.Sqrt, bias=eps[:, 0:1]).then_inc(root_done, 1)

            def wait_fill(name, j):
                n = fi(name, j)
                feed(split_target(n))
                act.wait_ge(pe_step, fill_step(n))
                feed(behind_target(n))

            def post_norm_fill(name, j):
                wait_fill(name, j)
                A(sq[:, 2 * j:2 * j + 2], bank(name, j)[:], ACT.Square).then_inc(sq_ready, 1)
                nc.scalar.copy(y[:, 2 * j:2 * j + 2], bank(name, j)[:]).then_inc(freed["act"], 1)

            def copy_fill(name, j, dst, func=None, view=None):
                wait_fill(name, j)
                src = bank(name, j)[:]
                if func is None:
                    nc.scalar.copy(dst, src).then_inc(freed["act"], 1)
                else:
                    A(dst, src, func).then_inc(freed["act"], 1)

            act.wait_ge(load_x, 16)
            squares_of_x(None)
            feed(split_target(0))
            act.wait_ge(eps_ready, 1)
            root("mix_pre")
            act.wait_ge(lb_exp, 1)
            A(lb[:, 1], lb[:, 0], ACT.Exp).then_inc(lb_exp, 1)
            hi_of_h("mix_pre")
            act.wait_ge(load_mem, 16)
            act.wait_ge(h_ready, H_PAIRS["mix_pre"] + 4)
            for i in range(2):
                A(sq[:, 4 * i:4 * i + 4], mem_x[:, 4 * i:4 * i + 4], ACT.Square).then_inc(sq_ready, 1)
            for j in range(4):
                wait_fill("conv", j)
                wait_gate_slot(act, "conv", j)
                A(gate_tmp[:, gate_slot("conv", j), 0], bank("conv", j)[:, 1], ACT.Sigmoid).then_inc(gate_done, 1)
            root("mem")
            for p in range(4):
                act.wait_ge(mem_full, p + 1)
                nc.scalar.copy(mem_n[:, 0, 2 * p:2 * p + 2], mem_x[:, 2 * p:2 * p + 2]).then_inc(mem_hi, 1)
            for j in range(2):
                copy_fill("qk", j, q_raw[:, 2 * j:2 * j + 2])
            for j in range(2):
                copy_fill("qk", 2 + j, k_raw[:, 2 * j:2 * j + 2])
            for j in range(2):
                copy_fill("v", j, v_ret[:, :, 256 * j:256 * j + 256])
            for j in range(2):
                copy_fill("g", j, g_ret[:, 2 * j:2 * j + 2], ACT.Silu)
            for j in range(2):
                copy_fill("memk", j, mem_k[:, 2 * j:2 * j + 2])
            for j in range(2):
                copy_fill("memv", j, mem_v[:, :, 256 * j:256 * j + 256])
            act.wait_ge(conv_ready, 2)
            A(sq[:, 0:4], conv_y[:], ACT.Square).then_inc(sq_ready, 1)
            root("ln_var")
            for g in range(2):
                for hd in (2 * g, 2 * g + 1):
                    act.wait_ge(sc_done, SC_RO + hd + 1)
                    ins = A(sq[:, 4 + hd], sc[hd][:, 0:S], ACT.Square)
                    if hd % 2:
                        ins.then_inc(sq_ready, 1)
                    nc.scalar.copy(o_ret[:, hd], sc[hd][:, 0:S]).then_inc(o_copied, 1)
            root("ret0", 2 * S)
            root("ret1", 2 * S)
            act.wait_ge(conv_ready, 3)
            for j in range(4):
                A(conv_y[:, j], conv_y[:, j], ACT.Silu, bias=col("ln_b", j), scale=col("ln_w", j)).then_inc(mix_full, 1)
            act.wait_ge(mix_full, 4)
            nc.scalar.copy(mix[:, 0, 0:4], conv_y[:]).then_inc(mix_hi, 1)
            for g in range(2):
                act.wait_ge(ret_full, g + 1)
                nc.scalar.copy(mix[:, 0, 4 + 2 * g:6 + 2 * g], o_ret[:, 2 * g:2 * g + 2]).then_inc(mix_hi, 1)
            for j in range(4):
                post_norm_fill("wout", j)
            root("mix_post")
            squares_of_x("mix_post")
            root("ffn_pre")
            hi_of_h("ffn_pre")
            for j in range(23):
                if j < 22:
                    wait_fill("ff", j)
                    wait_gate_slot(act, "ff", j)
                    A(gate_tmp[:, gate_slot("ff", j), 0], bank("ff", j)[:, 0], ACT.Silu).then_inc(gate_done, 1)
                if j:
                    wait_read(act, "ff", j - 1)
                    nc.scalar.copy(ff[:, 0, j - 1], prod_tmp[:, (j - 1) % 2]).then_inc(f_hi, 1)
            for j in range(4):
                post_norm_fill("down", j)
            root("ffn_post")
            for j in range(4):
                act.wait_ge(sc_done, SC_LEVEL + j + 1)
                nc.scalar.copy(ple_p[:, 2 * j:2 * j + 2], sc[j][:]).then_inc(ple_proj, 1)
            for i in range(2):
                act.wait_ge(x_ready, X_HALF["ffn_post"] + i + 1)
                nc.scalar.copy(x_split[:, 0, 4 * i:4 * i + 4], x[:, 4 * i:4 * i + 4]).then_inc(xs_hi, 1)
            for j in range(4):
                wait_fill("ple", j)
                wait_gate_slot(act, "ple", j)
                A(gate_tmp[:, gate_slot("ple", j)], bank("ple", j)[:], ACT.Sigmoid).then_inc(gate_done, 1)
                wait_read(act, "ple", j)
                A(sq[:, 2 * j:2 * j + 2], y[:, 2 * j:2 * j + 2], ACT.Square).then_inc(sq_ready, 1)
            root("ple_post")
            squares_of_x("ple_post")
            root("mix2")

            hi_of_h("mix2")

            for stage, f, k in (("hff", f_f, k_f), ("hfb", f_b, k_b)):
                for j in range(4):
                    wait_fill(stage, j)
                    A(f[:, 2 * j:2 * j + 2], bank(stage, j)[:], ACT.Sigmoid)
                    A(k[:, 2 * j:2 * j + 2], bank(stage, j)[:], ACT.Sigmoid, scale=-1.0).then_inc(freed["act"], 1)
            for j in range(4):
                copy_fill("hq", j, q_s[:, 2 * j:2 * j + 2], ACT.Silu)

            def diagonal():
                for g in range(4):
                    act.wait_ge(sc_done, SC_LEVEL + 4 + g + 1)
                    nc.scalar.copy(diag_view(g), sc[g][:].rearrange("p (a b c) -> p a b c", a=2, b=2)
                                   ).then_inc(st_diag, 1)

            def cross():
                for g in range(4):
                    act.wait_ge(sc_done, SC_CROSS + 4 + g + 1)
                    nc.scalar.copy(st_hg[:, 2 * g:2 * g + 2, P:3 * P],
                                   sc[g][:].rearrange("p (a b) -> p a b", a=2)).then_inc(st_cross, 1)

            def hg_outputs():
                for g in range(4):
                    act.wait_ge(sc_done, SC_HGO + 4 + g + 1)
                    o = sc[g][:].rearrange("p (a b) -> p a b", a=2)
                    A(sq[:, 2 * g:2 * g + 2], o, ACT.Square).then_inc(sq_ready, 1)
                    nc.scalar.copy(o_hg[:, 2 * g:2 * g + 2], o).then_inc(o_copied, 1)

            for e, (name, j) in enumerate(SIDE_FILLS):
                if name in ("hi", "nv"):
                    dst = (v_hg if name == "hi" else v_na)[:, :, 256 * j:256 * j + 256]
                    copy_fill(name, j, dst)
                else:
                    copy_fill(name, j, {"nq": q_na, "nk": k_na, "cq": q_ca}[name][:, 2 * j:2 * j + 2])
                if e == 0:
                    diagonal()
            feed(split_target(fi("hg", 0)))
            cross()
            hg_outputs()
            for j in range(4):
                copy_fill("hg", j, gate_hg[:, 2 * j:2 * j + 2], ACT.Silu)
                root(f"hg{j}", 2 * S)
            for g in range(4):
                act.wait_ge(hg_out, g + 1)
                nc.scalar.copy(o_hg_s[:, 0, 2 * g:2 * g + 2], o_hg[:, 2 * g:2 * g + 2]).then_inc(hg_hi, 1)

            def att_exp(a):
                act.wait_ge(logits_ready, a + 1)
                for t in range(2):
                    if a < NA:
                        src, scale = probs[:, a % 2, t * S:t * S + S], 1.0
                    else:
                        src, scale = sc[a % 2][:, t * S:t * S + S], float(P) ** -0.5
                    ins = A(probs[:, a % 2, t * S:t * S + S], src, ACT.Exp, bias=soft[:, a % 2, 0, t:t + 1],
                            scale=scale, accum_out=soft[:, a % 2, 1, t:t + 1])
                ins.then_inc(exp_ready, 1)

            def att_turn(a):
                act.wait_ge(turned, a + 1)
                if a >= 2:
                    act.wait_ge(pv_done, a - 1)
                nc.scalar.copy(probs_t[:, a % 2], sc[2][:]).then_inc(pt_ready, 1)

            def att_out(a):
                act.wait_ge(pv_done, a + 1)
                if a < NA:
                    if a % 2:
                        nc.scalar.copy(o_na[:, 0, a // 2], sc[3][:, 0:S]).then_inc(o_att, 1)
                else:
                    nc.scalar.copy(o_ca[:, 0, a - NA], sc[3][:, 0:S]).then_inc(o_att, 1)

            def att_slot(i):
                if i < NA + CA:
                    att_exp(i)
                if 1 <= i <= NA + CA:
                    att_turn(i - 1)
                if 2 <= i < NA + CA + 2:
                    att_out(i - 2)

            def merge_split(j):
                act.wait_ge(merge_full, j + 1)
                nc.scalar.copy(merged_s[:, 0, j], merged[:, j]).then_inc(merge_hi, 1)

            att_slot(0)
            att_slot(1)
            for i, (name, j) in enumerate(MERGE_FILLS):
                wait_fill(name, j)
                wait_gate_slot(act, name, j)
                A(gate_tmp[:, gate_slot(name, j), 0], bank(name, j)[:, 0], ACT.Sigmoid).then_inc(gate_done, 1)
                if i >= 17:
                    merge_split(i - 17)
                att_slot(i + 2)
            merge_split(7)
            for j in range(4):
                wait_fill("wout2", j)
            squares_of_x("wout2")
            root("ffn2")
            hi_of_h("ffn2")
            for j in range(24):
                if j < 22:
                    wait_fill("up", j)
                    if j >= 2:
                        act.wait_ge(up_full, j - 1)
                    for i in range(2):
                        ins = A(gate_tmp[:, j % 2, i], bank("up", j)[:, i], ACT.Identity,
                                bias=col("conv_b", 22 * i + j), scale=col("conv_w", 44 + 22 * i + j))
                    ins.then_inc(up_lin, 1)
                if 1 <= j <= 22:
                    i = j - 1
                    wait_read(act, "up", i)
                    A(gate_tmp[:, i % 2, 0], gate_tmp[:, i % 2, 0], ACT.Gelu_apprx_tanh).then_inc(gelu_done, 1)
                if j >= 2:
                    act.wait_ge(up_full, j - 1)
                    nc.scalar.copy(ff[:, 0, j - 2], prod_tmp[:, j % 2]).then_inc(f_hi, 1)
            for j in range(4):
                wait_fill("down2", j)
            squares_of_x("down2")
            root("final")

        @block.vector
        def _(dve):
            V = nc.vector
            chain = [0]

            def link(ins):
                chain[0] += 1
                ins.then_inc(dve_chain, 1)
                return chain[0]

            def after(n):
                dve.wait_ge(dve_chain, n)

            def over(v, n):
                return v.unsqueeze(1).to_broadcast([P, n, S])

            def root(name, dst, n=S):
                dve.wait_ge(root_done, ROOTS.index(name) + 1)
                V.reciprocal(dst, std[:, 0:n]).then_inc(stat_read, 1)
                dve.wait_ge(stat_read, STAT[name] + 1)

            fed = [0]

            def feed(target):
                for u in range(fed[0], target):
                    if LO_ENGINE[u] == "dve":
                        dve.wait_ge(hi_ready, u + 1)
                        V.tensor_tensor(w_lo[:, u % UNITS], unit_of_raw(u), as_f32(w_hi[:, u % UNITS]),
                                        ALU.subtract).then_inc(lo_ready["dve"], 1)
                fed[0] = max(fed[0], target)

            def feed_fill(name, j):
                feed(split_target(fi(name, j)))

            def feed_behind(name, j):
                feed(behind_target(fi(name, j)))

            def lo_part(split, full, a, b):
                return V.tensor_tensor(split[:, 1, a:b], full, as_f32(split[:, 0, a:b]), ALU.subtract)

            def norm_to_h(name, gain):
                root(name, rstd_h[:])
                base_n = H_PAIRS[name]
                for p in range(5):
                    if p < 4:
                        for t in (2 * p, 2 * p + 1):
                            ins = V.scalar_tensor_tensor(out=sq[:, t], in0=x[:, t], scalar=col(gain, t),
                                                         in1=rstd_h[:], op0=ALU.mult, op1=ALU.mult)
                        ins.then_inc(h_full, 1)
                    if p:
                        dve.wait_ge(h_hi, base_n + p)
                        lo_part(h, sq[:, 2 * p - 2:2 * p], 2 * p - 2, 2 * p).then_inc(h_ready, 1)
                dve.wait_ge(h_ready, base_n + 4)

            def post_norm(name, gain):
                root(name, rstd[:, 0:S])
                for i in range(2):
                    for t in range(4 * i, 4 * i + 4):
                        n = link(V.scalar_tensor_tensor(out=y[:, t], in0=y[:, t], scalar=col(gain, t),
                                                        in1=rstd[:, 0:S], op0=ALU.mult, op1=ALU.mult))
                    after(n)
                    V.tensor_tensor(x[:, 4 * i:4 * i + 4], x[:, 4 * i:4 * i + 4], y[:, 4 * i:4 * i + 4],
                                    ALU.add).then_inc(x_ready, 1)
                dve.wait_ge(x_ready, X_HALF[name] + 2)

            def wait_gate(count):
                dve.wait_ge(gate_done, count)

            gates = [0]

            V.memset(eps[:], EPS).then_inc(eps_ready, 1)
            dve.wait_ge(load_params, 32)
            logits = vec[:, VEC["lb"]:VEC["lb"] + 16]
            V.tensor_tensor(lb[:, 0], logits, logits, ALU.subtract).then_inc(lb_exp, 1)
            feed_fill("conv", 0)
            norm_to_h("mix_pre", "mix_pre")
            dve.wait_ge(lb_exp, 2)
            after(link(V.reciprocal(lb[:, 2], lb[:, 1])))
            after(link(V.tensor_tensor(lb[:, 3], lb[:, 1], lb[:, 2], ALU.mult)))
            after(link(V.tensor_tensor(lb[:, 4], lb[:, 3], lb[:, 3], ALU.subtract)))
            after(link(V.tensor_scalar(lb[:, 4], lb[:, 4], 0.0, 1.0, ALU.max, ALU.min)))
            V.tensor_scalar(lb[:, 5], lb[:, 4], -1.0, 1.0, ALU.mult, ALU.add).then_inc(lb_ready, 1)

            dve.wait_ge(pad_ready, 1)
            for j in range(4):
                gates[0] += 1
                feed_behind("conv", j)
                wait_gate(gates[0])
                V.tensor_tensor(conv_in[:, j, CW - 1:], bank("conv", j)[:, 0], gate_tmp[:, gate_slot("conv", j), 0],
                                ALU.mult).then_inc(freed["dve"], 1)
            root("mem", rstd[:, 0:S])
            for p in range(5):
                if p < 4:
                    for t in (2 * p, 2 * p + 1):
                        ins = V.scalar_tensor_tensor(out=mem_x[:, t], in0=mem_x[:, t], scalar=col("mem_norm", t),
                                                     in1=rstd[:, 0:S], op0=ALU.mult, op1=ALU.mult)
                    ins.then_inc(mem_full, 1)
                if p:
                    dve.wait_ge(mem_hi, p)
                    lo_part(mem_n, mem_x[:, 2 * p - 2:2 * p], 2 * p - 2, 2 * p).then_inc(mem_ready, 1)
            dve.wait_ge(mem_ready, 4)
            dve.wait_ge(freed["dve"], 4)
            seen = [0] * 4
            taps_per_fill = 3
            behind = [(name, j) for name, j, _, _ in FILLS[fi("qk", 0):fi("wout", 0)]]
            for w in range(CW):
                if w % taps_per_fill == taps_per_fill - 1:
                    feed_behind(*behind.pop(0))
                for j in range(4):
                    src = conv_in[:, j, w:w + S]
                    tap = col("dw_w", w * 4 + j)
                    if w == 0:
                        seen[j] = link(V.tensor_scalar(conv_y[:, j], src, tap, col("dw_b", j), ALU.mult, ALU.add))
                    else:
                        after(seen[j])
                        ins = V.scalar_tensor_tensor(out=conv_y[:, j], in0=src, scalar=tap, in1=conv_y[:, j],
                                                     op0=ALU.mult, op1=ALU.add)
                        if w < CW - 1 or j < 3:
                            seen[j] = link(ins)
            ins.then_inc(conv_ready, 1)
            dve.wait_ge(load_side, 32)
            for i, t in enumerate((q_raw, k_raw)):
                feed_fill("qk", 2 * i + 1)
                wait_read(dve, "qk", 2 * i + 1)
                if i:
                    if behind:
                        feed_behind(*behind.pop(0))
                    dve.wait_ge(rope_ready, 1)
                V.tensor_tensor(rope_a[:], t[:], over(rope[:, 0], 4), ALU.mult)
                for a, b in ((0, 64), (64, 0)):
                    sin = rope[b:b + 64, 1].unsqueeze(1).to_broadcast([64, 4, S])
                    n = link(V.tensor_tensor(rope_b[a:a + 64], t[b:b + 64], sin, ALU.mult))
                after(n)
                V.tensor_tensor(t[:], rope_a[:], rope_b[:], ALU.add).then_inc(rope_ready, 1)
            while behind:
                feed_behind(*behind.pop(0))
            dve.wait_ge(stat_done, STAT["ln_mean"] + 1)
            V.tensor_copy(rstd[:, S:2 * S], st[:, 0:S]).then_inc(stat_read, 1)
            dve.wait_ge(stat_read, STAT["ln_mean"] + 1)
            V.tensor_tensor(conv_y[:], conv_y[:], over(rstd[:, S:2 * S], 4), ALU.subtract).then_inc(conv_ready, 1)
            for hd in range(RET):
                dve.wait_ge(sc_done, SC_RET + hd + 1)
                V.tensor_tensor(s_ret[:, hd], sc[hd][:, 0:384], decay[:, hd], ALU.mult).then_inc(s_ready, 1)
            root("ln_var", rstd[:, 0:S])
            V.tensor_tensor(conv_y[:], conv_y[:], over(rstd[:, 0:S], 4), ALU.mult).then_inc(conv_ready, 1)
            dve.wait_ge(conv_ready, 3)
            for g in range(2):
                dve.wait_ge(o_copied, 2 * g + 2)
                root(f"ret{g}", rstd[:], 2 * S)
                o = o_ret[:, 2 * g:2 * g + 2]
                after(link(V.tensor_tensor(o, o, rstd[:].rearrange("p (a b) -> p a b", a=2), ALU.mult)))
                wait_read(dve, "g", 1)
                V.tensor_tensor(o, o, g_ret[:, 2 * g:2 * g + 2], ALU.mult).then_inc(ret_full, 1)
                if g == 0:
                    dve.wait_ge(ret_full, 1)
            dve.wait_ge(mix_hi, 1)
            lo_part(mix, conv_y[:], 0, 4).then_inc(mix_ready, 1)
            for g in range(2):
                dve.wait_ge(mix_hi, g + 2)
                lo_part(mix, o_ret[:, 2 * g:2 * g + 2], 4 + 2 * g, 6 + 2 * g).then_inc(mix_ready, 1)
            for j in range(4):
                feed_fill("wout", j)
                feed_behind("wout", j)
            wait_read(dve, "wout", 3)
            post_norm("mix_post", "mix_post")
            norm_to_h("ffn_pre", "ffn_pre")
            def ff_lo(j):
                ff_lo.count += 1
                dve.wait_ge(f_hi, ff_lo.count)
                V.tensor_tensor(ff[:, 1, j], prod_tmp[:, j % 2], as_f32(ff[:, 0, j]), ALU.subtract).then_inc(ff_ready, 1)

            ff_lo.count = 0
            for j in range(23):
                if j < 22:
                    gates[0] += 1
                    feed_behind("ff", j)
                    wait_gate(gates[0])
                    if j >= 2:
                        dve.wait_ge(ff_ready, j - 1)
                    V.tensor_tensor(prod_tmp[:, j % 2], bank("ff", j)[:, 1], gate_tmp[:, gate_slot("ff", j), 0],
                                    ALU.mult).then_inc(freed["dve"], 1)
                if j:
                    ff_lo(j - 1)
            for j in range(4):
                feed_fill("down", j)
                feed_behind("down", j)
            wait_read(dve, "down", 3)
            post_norm("ffn_post", "ffn_post")
            for i in range(2):
                dve.wait_ge(xs_hi, i + 1)
                lo_part(x_split, x[:, 4 * i:4 * i + 4], 4 * i, 4 * i + 4).then_inc(xs_ready, 1)
            for j in range(4):
                gates[0] += 1
                feed_behind("ple", j)
                wait_gate(gates[0])
                dve.wait_ge(ple_proj, j + 1)
                V.tensor_tensor(y[:, 2 * j:2 * j + 2], gate_tmp[:, gate_slot("ple", j)], ple_p[:, 2 * j:2 * j + 2],
                                ALU.mult).then_inc(freed["dve"], 1)
            wait_read(dve, "ple", 3)
            post_norm("ple_post", "ple_post")
            norm_to_h("mix2", "norm_mix2")

            for d, (stage, f, k) in enumerate((("hff", f_f, k_f), ("hfb", f_b, k_b))):
                for j in range(4):
                    feed_fill(stage, j)
                    wait_read(dve, stage, j)
                    feed_behind(stage, j)
                    for t in (2 * j, 2 * j + 1):
                        c = d * 8 + t
                        V.tensor_scalar(k[:, t], k[:, t], lb[:, 5, c:c + 1], None, ALU.mult)
                        last = link(V.tensor_scalar(f[:, t], f[:, t], lb[:, 5, c:c + 1],
                                                    lb[:, 4, c:c + 1], ALU.mult, ALU.add))
                    after(last)
                    last = link(V.tensor_scalar(f[:, 2 * j:2 * j + 2], f[:, 2 * j:2 * j + 2], 1e-12, None, ALU.max))
            for j in range(4):
                feed_behind("hq", j)
            wait_read(dve, "hq", 3)
            after(link(V.tensor_scalar(q_s[:], q_s[:], float(P) ** -0.5, None, ALU.mult)))
            V.tensor_tensor(ksum[:], k_f[:], k_b[:], ALU.add)
            V.tensor_tensor(q_f[:], q_s[:], f_f[:], ALU.mult)
            V.tensor_tensor(q_b[:], q_s[:], f_b[:], ALU.mult).then_inc(level_ready, 1)
            dve.wait_ge(level_ready, 1)

            def masks(i):
                for g in range(4):
                    dve.wait_ge(sc_done, SC_LEVEL + 4 + 4 * (i + 1) + g + 1)
                    if i == 0:
                        dve.wait_ge(st_diag, g + 1)
                    m = mat("mask", i).bitcast(I32).unsqueeze(1).to_broadcast([P, 4, P])
                    dst = st_hg[:, 2 * g:2 * g + 2].rearrange("p a (b c) -> p (a b) c", c=P)
                    m2 = mat("mask", i).bitcast(I32).unsqueeze(1).to_broadcast([P, 2, P])
                    for a in range(2):
                        src = sc[g][:, a * 256:a * 256 + 256].rearrange("p (b c) -> p b c", b=2)
                        ins = V.copy_predicated(dst[:, 4 * a:4 * a + 4:3], m2, src)
                    ins.then_inc(st_mask, 1)

            def grow(i):
                b = LEVELS[i]

                def halves(t):
                    v = t[:].rearrange("p a s -> p (a s)").rearrange("p (n two b) -> p n two b", two=2, b=b)
                    return v[:, :, 0], v[:, :, 1]

                nb = HG * S // (2 * b)
                fa, fb_ = halves(f_f)
                ba, bb_ = halves(f_b)
                bc = lambda t: t[:, :, 0:1].to_broadcast([P, nb, b])
                qf, qb, kf, kb = halves(q_f)[1], halves(q_b)[0], halves(k_f)[0], halves(k_b)[1]
                V.tensor_tensor(qf, qf, bc(fa), ALU.mult)
                V.tensor_tensor(kf, kf, bc(fb_), ALU.mult)
                V.tensor_tensor(qb, qb, bc(bb_), ALU.mult)
                after(link(V.tensor_tensor(kb, kb, bc(ba), ALU.mult)))
                V.tensor_tensor(fa[:, :, 0:1], fa[:, :, 0:1], fb_[:, :, 0:1], ALU.mult)
                V.tensor_tensor(ba[:, :, 0:1], ba[:, :, 0:1], bb_[:, :, 0:1], ALU.mult).then_inc(level_ready, 1)
                dve.wait_ge(level_ready, i + 2)

            side = list(SIDE_FILLS)
            for i in range(len(LEVELS)):
                for _ in range(2 if i < len(LEVELS) - 1 else 0):
                    feed_behind(*side.pop(0))
                masks(i)
                grow(i)
            for g in range(4):
                feed_fill("hg", g)
                wait_read(dve, "hg", g)
                feed_behind("hg", g)
                root(f"hg{g}", rstd[:], 2 * S)
                dve.wait_ge(o_copied, RET + g + 1)
                o = o_hg[:, 2 * g:2 * g + 2]
                after(link(V.scalar_tensor_tensor(out=o, in0=o, scalar=col("gnorm"), in1=gate_hg[:, 2 * g:2 * g + 2],
                                                  op0=ALU.mult, op1=ALU.mult)))
                V.tensor_tensor(o, o, rstd[:].rearrange("p (a b) -> p a b", a=2), ALU.mult).then_inc(hg_out, 1)
                dve.wait_ge(hg_out, g + 1)
            for g in range(4):
                dve.wait_ge(hg_hi, g + 1)
                lo_part(o_hg_s, o_hg[:, 2 * g:2 * g + 2], 2 * g, 2 * g + 2).then_inc(hg_split, 1)

            def att_logits(a):
                par = a % 2
                dve.wait_ge(scored, a + 1)
                if a == 0:
                    dve.wait_ge(toep_sel, 2)
                    dve.wait_ge(sc_done, SC_HGO + 8)
                if a >= 2:
                    dve.wait_ge(turned, a - 1)
                if a < NA:
                    for t in range(2):
                        d0 = (3 - 2 * t - 1) * 64
                        rows = lambda v: v.rearrange("p (r c) -> p r c", c=64)
                        n = link(V.scalar_tensor_tensor(out=rows(probs[:, par, t * S:t * S + S]),
                                                        in0=rows(sc[par][:, t * S:t * S + S]), scalar=64.0 ** -0.5,
                                                        in1=rows(toep_t[:, a, d0:d0 + S])[:, :, ::-1],
                                                        op0=ALU.mult, op1=ALU.add))
                    after(n)
                    src, scale = probs[:, par], -1.0
                else:
                    src, scale = sc[par][:], -float(P) ** -0.5
                n = link(V.tensor_reduce(soft[:, par, 0], src.rearrange("p (t j) -> p t j", t=2), AX.X, ALU.max))
                after(n)
                V.tensor_scalar(soft[:, par, 0], soft[:, par, 0], scale, None, ALU.mult).then_inc(logits_ready, 1)

            def att_norm(a):
                par = a % 2
                dve.wait_ge(exp_ready, a + 1)
                after(link(V.reciprocal(soft[:, par, 2], soft[:, par, 1])))
                for t in range(2):
                    ins = V.tensor_scalar(probs[:, par, t * S:t * S + S], probs[:, par, t * S:t * S + S],
                                          soft[:, par, 2, t:t + 1], None, ALU.mult)
                ins.then_inc(p_ready, 1)

            def att_lo(a):
                if a < NA and a % 2 == 0:
                    return
                o, t = (o_na, a // 2) if a < NA else (o_ca, a - NA)
                dve.wait_ge(o_att, a // 2 + 1 if a < NA else a - NA + 5)
                V.tensor_tensor(o[:, 1, t], sc[3][:, 0:S], as_f32(o[:, 0, t]), ALU.subtract).then_inc(att_ready, 1)

            def att_slot(i):
                if i < NA + CA:
                    att_logits(i)
                    att_norm(i)
                if 2 <= i < NA + CA + 2:
                    att_lo(i - 2)

            att_slot(0)
            att_slot(1)
            def merge_lo(j):
                dve.wait_ge(merge_hi, j + 1)
                V.tensor_tensor(merged_s[:, 1, j], merged[:, j], as_f32(merged_s[:, 0, j]), ALU.subtract
                                ).then_inc(merge_ready, 1)

            added = {}
            for i, (name, j) in enumerate(MERGE_FILLS):
                gates[0] += 1
                feed_behind(name, j)
                wait_gate(gates[0])
                yv = bank(name, j)[:, 1]
                gv = gate_tmp[:, gate_slot(name, j), 0]
                if name == "mhg":
                    V.tensor_tensor(merged[:, j], yv, gv, ALU.mult).then_inc(freed["dve"], 1)
                else:
                    if i - 2 >= 16:
                        dve.wait_ge(merge_full, i - 2 - 16 + 1)
                    elif i - 2 >= 8:
                        after(added[i - 2])
                    V.tensor_tensor(prod_tmp[:, i % 2], yv, gv, ALU.mult).then_inc(freed["dve"], 1)
                    wait_read(dve, name, j)
                    if name == "mca":
                        after(added[i - 8])
                    ins = V.tensor_tensor(merged[:, j], merged[:, j], prod_tmp[:, i % 2], ALU.add)
                    if name == "mca":
                        ins.then_inc(merge_full, 1)
                    else:
                        added[i] = link(ins)
                if i >= 17:
                    merge_lo(i - 17)
                att_slot(i + 2)
            merge_lo(7)

            for j in range(4):
                feed_fill("wout2", j)
                dve.wait_ge(pe_step, fill_step(fi("wout2", j)))
                feed_behind("wout2", j)
                V.tensor_tensor(x[:, 2 * j:2 * j + 2], x[:, 2 * j:2 * j + 2], bank("wout2", j)[:], ALU.add
                                ).then_inc(freed["dve"], 1)
            norm_to_h("ffn2", "norm_ffn2")
            for j in range(24):
                if j < 22:
                    feed_behind("up", j)
                    dve.wait_ge(up_lin, j + 1)
                    b = bank("up", j)
                    for i in range(2):
                        t = gate_tmp[:, j % 2, i]
                        ct = 22 * i + j
                        n = link(V.scalar_tensor_tensor(out=t[:, 1:S], in0=b[:, i, 0:S - 1], scalar=col("conv_w", ct),
                                                        in1=t[:, 1:S], op0=ALU.mult, op1=ALU.add))
                    for i in range(2):
                        t = gate_tmp[:, j % 2, i]
                        ct = 22 * i + j
                        if i == 0:
                            after(n)
                        ins = V.scalar_tensor_tensor(out=t[:, 0:S - 1], in0=b[:, i, 1:S], scalar=col("conv_w", 88 + ct),
                                                     in1=t[:, 0:S - 1], op0=ALU.mult, op1=ALU.add)
                    ins.then_inc(freed["dve"], 1)
                if j >= 2:
                    ff_lo(j - 2)
                if 1 <= j <= 22:
                    i = j - 1
                    dve.wait_ge(gelu_done, i + 1)
                    if i >= 2:
                        dve.wait_ge(ff_ready, 22 + i - 1)
                    V.tensor_tensor(prod_tmp[:, i % 2], gate_tmp[:, i % 2, 0], gate_tmp[:, i % 2, 1], ALU.mult
                                    ).then_inc(up_full, 1)
            for j in range(4):
                feed_fill("down2", j)
                dve.wait_ge(pe_step, fill_step(fi("down2", j)))
                feed_behind("down2", j)
                V.tensor_tensor(x[:, 2 * j:2 * j + 2], x[:, 2 * j:2 * j + 2], bank("down2", j)[:], ALU.add
                                ).then_inc(freed["dve"], 1)
            root("final", rstd[:, 0:S])
            for t in range(KT):
                ins = V.scalar_tensor_tensor(out=y[:, t], in0=x[:, t], scalar=col("norm_final", t), in1=rstd[:, 0:S],
                                             op0=ALU.mult, op1=ALU.mult)
                if t % 4 == 3:
                    ins.then_inc(out_ready, 1)

        @block.tensor
        def _(pe):
            mm = nc.tensor.matmul
            at_block = [0]

            PASSES = ((0, 0), (0, 1), (1, 0))

            def take(count=1):
                b = at_block[0]
                at_block[0] += count
                u = b // UB
                if b % UB == 0:
                    pe.wait_ge(lo_ready[LO_ENGINE[u]], lo_count(u, LO_ENGINE[u]))
                if count == 1:
                    return [w[:, u % UNITS, b % UB] for w in (w_hi, w_lo)]
                return [w[:, u % UNITS, b % UB:b % UB + count].rearrange("p a b -> p (a b)") for w in (w_hi, w_lo)]

            def step(ins, end):
                if end in STEP:
                    ins.then_inc(pe_step, 1)

            def open_fill(name, j):
                n = fi(name, j)
                if n >= PJ:
                    who = FILLS[n - PJ][3]
                    pe.wait_ge(freed[who], freed_count(n - PJ, who))
                assert at_block[0] == FIRST_BLOCK[n]
                return pj[n % PJ]

            def tile_out(dst, src, kts=KT, ready=None):
                for kt in range(kts):
                    w = take()
                    if ready is not None:
                        ready(kt)
                    for i, (a, b) in enumerate(PASSES):
                        last = mm(dst, w[a], src[:, b, kt], start=kt == 0 and i == 0, stop=kt == kts - 1 and i == 2)
                    step(last, at_block[0])

            def pair(name, j, src, kts=KT, ready=None):
                b = open_fill(name, j)
                tile_out(b[:, 0], src, kts, ready if j == 0 else None)
                tile_out(b[:, 1], src, kts)

            def token_pair(name, j, src):
                b = open_fill(name, j)
                start = at_block[0]
                ws = [take(2) for _ in range(KT)]
                for tt in range(2):
                    for kt in range(KT):
                        for i, (wa, xa) in enumerate(PASSES):
                            last = mm(b[:, tt], src[:, xa, kt, tt * P:tt * P + P], ws[kt][wa],
                                      start=kt == 0 and i == 0, stop=kt == KT - 1 and i == 2)
                        if tt == 1:
                            step(last, start + 2 * kt + 2)

            def h_pairs(name):
                def ready(kt):
                    if kt % 2 == 0:
                        pe.wait_ge(h_ready, H_PAIRS[name] + kt // 2 + 1)
                return ready

            def wait_stat(name):
                if STAT[name]:
                    pe.wait_ge(stat_read, STAT[name])

            def norm_stat(name, chunks, matrix="m1024", src=None):
                wait_stat(name)
                for c in range(chunks):
                    stat_chunk(name, c, chunks, matrix)

            def stat_chunk(name, c, chunks, matrix="m1024"):
                if c == 0:
                    wait_stat(name)
                pe.wait_ge(sq_ready, SQ_BEFORE[name] + c + 1)
                per = KT // chunks
                for t in range(c * per, c * per + per):
                    last = mm(st[:, 0:S], mat(matrix), sq[:, t], start=t == 0, stop=t == KT - 1)
                if c == chunks - 1:
                    last.then_inc(stat_done, 1)

            pe.wait_ge(load_params, 32)
            norm_stat("mix_pre", 2)
            for j in range(4):
                pair("conv", j, h, ready=h_pairs("mix_pre"))
                if j == 0:
                    norm_stat("mem", 2)
            for j in range(4):
                pair("qk", j, h)
            for j in range(2):
                token_pair("v", j, h)
            for j in range(2):
                pair("g", j, h)
            for j in range(2):
                pe.wait_ge(mem_ready, 4)
                pair("memk", j, mem_n)
            for j in range(2):
                token_pair("memv", j, mem_n)
            pe.wait_ge(conv_ready, 1)
            wait_stat("ln_mean")
            for t in range(4):
                last = mm(st[:, 0:S], mat("m512"), conv_y[:, t], start=t == 0, stop=t == 3)
            last.then_inc(stat_done, 1)
            pe.wait_ge(rope_ready, 2)
            for hd in range(RET):
                mm(sc[hd][:, 0:S], k_raw[:, hd, 0:P], q_raw[:, hd, :], start=True, stop=True)
                mm(sc[hd][:, S:S + P], k_raw[:, hd, P:S], q_raw[:, hd, P:S], start=True, stop=True
                   ).then_inc(sc_done, 1)
            pe.wait_ge(conv_ready, 2)
            wait_stat("ln_var")
            pe.wait_ge(sq_ready, SQ_BEFORE["ln_var"] + 1)
            for t in range(4):
                last = mm(st[:, 0:S], mat("m512"), sq[:, t], start=t == 0, stop=t == 3)
            last.then_inc(stat_done, 1)
            for hd in range(RET):
                pe.wait_ge(s_ready, hd + 1)
                mm(sc[hd][:, 0:S], v_ret[:, 0, hd * P:hd * P + P], s_ret[:, hd, 0:S], start=True, stop=False)
                mm(sc[hd][:, P:S], v_ret[:, 1, hd * P:hd * P + P], s_ret[:, hd, S:S + P], start=False, stop=True
                   ).then_inc(sc_done, 1)
            for g in range(2):
                pe.wait_ge(sq_ready, SQ_BEFORE[f"ret{g}"] + 1)
                wait_stat(f"ret{g}")
                for a in range(2):
                    last = mm(st[:, a * S:a * S + S], mat("m128"), sq[:, 4 + 2 * g + a], start=True, stop=True)
                last.then_inc(stat_done, 1)
            pe.wait_ge(mix_ready, 3)
            for j in range(4):
                pair("wout", j, mix)
                if j:
                    stat_chunk("mix_post", j - 1, 4)
            stat_chunk("mix_post", 3, 4)
            norm_stat("ffn_pre", 2)
            for j in range(22):
                pair("ff", j, h, ready=h_pairs("ffn_pre"))
            pe.wait_ge(ff_ready, 22)
            for j in range(4):
                pair("down", j, ff, FT)
                if j:
                    stat_chunk("ffn_post", j - 1, 4)
            stat_chunk("ffn_post", 3, 4)
            pe.wait_ge(load_ple, 32)
            for j in range(4):
                for i in range(2):
                    for kt in range(2):
                        last = mm(sc[j][:, i * S:i * S + S], w_ple[:, kt, (2 * j + i) * P:(2 * j + i + 1) * P],
                                  p_in[:, kt], start=kt == 0, stop=kt == 1)
                last.then_inc(sc_done, 1)
            pe.wait_ge(xs_ready, 2)
            for j in range(4):
                pair("ple", j, x_split)
                if j:
                    stat_chunk("ple_post", j - 1, 4)
            stat_chunk("ple_post", 3, 4)
            norm_stat("mix2", 2)

            for stage in ("hff", "hfb", "hq"):
                for j in range(4):
                    pair(stage, j, h, ready=h_pairs("mix2") if stage == "hff" else None)

            def tile(t, hd, tt):
                return t[:, hd, tt * P:tt * P + P]

            def diagonal():
                pe.wait_ge(level_ready, 1)
                pe.wait_ge(ple_proj, 4)
                for g in range(4):
                    for a in range(2):
                        for tt in range(2):
                            c = (2 * a + tt) * P
                            last = mm(sc[g][:, c:c + P], tile(ksum, 2 * g + a, tt), tile(q_s, 2 * g + a, tt),
                                      start=True, stop=True)
                    last.then_inc(sc_done, 1)

            def level(i):
                b = LEVELS[i]
                pe.wait_ge(level_ready, i + 1)
                for g in range(4):
                    if i == 0:
                        pe.wait_ge(st_diag, g + 1)
                    else:
                        pe.wait_ge(st_mask, 4 * (i - 1) + g + 1)
                    for a in range(2):
                        for tt in range(2):
                            c = (2 * a + tt) * P
                            o = sc[g][:, c:c + P].rearrange("p (n two b) -> p n two b", two=2, b=b)
                            for k, q, side in ((k_f, q_f, 1), (k_b, q_b, 0)):
                                r = tile(q, 2 * g + a, tt).rearrange("p (n two b) -> p n two b", two=2, b=b)
                                last = mm(o[:, :, side], tile(k, 2 * g + a, tt), r[:, :, side],
                                          start=True, stop=True)
                    last.then_inc(sc_done, 1)

            def cross():
                pe.wait_ge(level_ready, 1 + len(LEVELS))
                for g in range(4):
                    pe.wait_ge(st_mask, 4 * (len(LEVELS) - 1) + g + 1)
                    for a in range(2):
                        hd = 2 * g + a
                        mm(sc[g][:, a * S:a * S + P], tile(k_f, hd, 0), tile(q_f, hd, 1), start=True, stop=True)
                        last = mm(sc[g][:, a * S + P:a * S + S], tile(k_b, hd, 1), tile(q_b, hd, 0),
                                  start=True, stop=True)
                    last.then_inc(sc_done, 1)

            def hg_values():
                for g in range(4):
                    pe.wait_ge(st_cross, g + 1)
                    for a in range(2):
                        hd = 2 * g + a
                        o = sc[g][:, a * S:a * S + S]
                        mm(o, v_hg[:, 0, hd * P:hd * P + P], st_hg[:, hd, 0:S], start=True, stop=False)
                        last = mm(o, v_hg[:, 1, hd * P:hd * P + P], st_hg[:, hd, S:2 * S], start=False, stop=True)
                    last.then_inc(sc_done, 1)

            for e, (name, j) in enumerate(SIDE_FILLS):
                if name in ("hi", "nv"):
                    token_pair(name, j, h)
                else:
                    pair(name, j, h)
                if e == 0:
                    diagonal()
                if e % 2 == 1 and e // 2 < len(LEVELS) - 1:
                    level(e // 2)
            level(len(LEVELS) - 1)
            cross()
            wait_read(pe, "hi", 3)
            hg_values()
            for g in range(4):
                pair("hg", g, h)
                pe.wait_ge(sq_ready, SQ_BEFORE[f"hg{g}"] + 1)
                wait_stat(f"hg{g}")
                for a in range(2):
                    last = mm(st[:, a * S:a * S + S], mat("m128"), sq[:, 2 * g + a], start=True, stop=True)
                last.then_inc(stat_done, 1)

            def att_scores(a):
                if a < 2:
                    pe.wait_ge(o_copied, RET + 4)
                    wait_read(pe, "cq", 1)
                elif a < NA + 2:
                    pe.wait_ge(exp_ready, a - 1)
                else:
                    pe.wait_ge(exp_ready, a - 1)
                for t in range(2):
                    o = sc[a % 2][:, t * S:t * S + S]
                    if a < NA:
                        lo = 64 * (a % 2)
                        last = mm(o, q_na[lo:lo + 64, a // 2, t * P:t * P + P], k_na[lo:lo + 64, a // 2, :],
                                  start=True, stop=True)
                    else:
                        last = mm(o, q_ca[:, a - NA, t * P:t * P + P], mem_k[:, a - NA, :], start=True, stop=True)
                last.then_inc(scored, 1)

            def att_transpose(a):
                pe.wait_ge(p_ready, a + 1)
                if a:
                    pe.wait_ge(pt_ready, a)
                for jt in range(2):
                    for t in range(2):
                        last = nc.tensor.transpose(sc[2][:, jt * S + t * P:jt * S + t * P + P],
                                                   probs[:, a % 2, t * S + jt * P:t * S + jt * P + P],
                                                   mat("ident"))
                last.then_inc(turned, 1)

            def att_values(a):
                pe.wait_ge(pt_ready, a + 1)
                if a < NA:
                    if a >= 2 and a % 2 == 0:
                        pe.wait_ge(att_ready, a // 2)
                    o = sc[3][64 * (a % 2):64 * (a % 2) + 64, 0:S]
                    v = v_na[:, :, a * 64:a * 64 + 64]
                else:
                    pe.wait_ge(att_ready, a - NA + 4)
                    o = sc[3][:, 0:S]
                    v = mem_v[:, :, (a - NA) * P:(a - NA + 1) * P]
                for jt in range(2):
                    last = mm(o, v[:, jt], probs_t[:, a % 2, jt * S:jt * S + S], start=jt == 0, stop=jt == 1)
                last.then_inc(pv_done, 1)

            def att_slot(i):
                if i < NA + CA:
                    att_scores(i)
                if 1 <= i <= NA + CA:
                    att_transpose(i - 1)
                if 2 <= i < NA + CA + 2:
                    att_values(i - 2)

            att_slot(0)
            att_slot(1)
            for i, (name, j) in enumerate(MERGE_FILLS):
                b = open_fill(name, j)
                tile_out(b[:, 0], h)
                if name == "mhg":
                    pe.wait_ge(hg_split, 4)
                    tile_out(b[:, 1], o_hg_s)
                elif name == "mna":
                    pe.wait_ge(att_ready, 4)
                    tile_out(b[:, 1], o_na, 4)
                else:
                    pe.wait_ge(att_ready, 8)
                    tile_out(b[:, 1], o_ca, 4)
                att_slot(i + 2)
            for j in range(4):
                pair("wout2", j, merged_s, ready=lambda kt: pe.wait_ge(merge_ready, kt + 1))
            norm_stat("ffn2", 2)
            for j in range(22):
                pair("up", j, h, ready=h_pairs("ffn2"))
            pe.wait_ge(ff_ready, 44)
            for j in range(4):
                pair("down2", j, ff, FT)
            norm_stat("final", 2)


def host_layout(inputs):
    f = np.float32

    def blocks(w, cols):
        k = w.shape[0] // P
        return [[w[kt * P:(kt + 1) * P, m * P:(m + 1) * P] for kt in range(k)] for m in cols]

    def token_blocks(w, pairs):
        k = w.shape[0] // P
        return [[w[kt * P:(kt + 1) * P, m * P:(m + 1) * P] for kt in range(k) for m in (2 * q, 2 * q + 1)]
                for q in pairs]

    def vecs(a, tiles):
        return np.asarray(a, f).reshape(-1, tiles, P).transpose(2, 0, 1).reshape(P, -1)

    g = {k: np.asarray(v) for k, v in inputs.items()}
    w_in, w_in2 = g["w_in"][0], g["w_in_2"][0]
    stream = []

    def add(*tiles):
        for t in tiles:
            stream.extend(t)

    a = blocks(w_in, range(24))
    for j in range(4):
        add(a[j], a[4 + j])
    add(*a[8:16], *token_blocks(w_in, (8, 9)), *a[20:24])
    w_kv = g["w_mem_kv_2"][0]
    add(*blocks(w_kv, range(4)), *token_blocks(w_kv, (2, 3)))
    add(*blocks(g["w_out"][0], range(8)))
    gate, up = blocks(g["w_ffn_gate"][0], range(FT)), blocks(g["w_ffn_up"][0], range(FT))
    for j in range(FT):
        add(gate[j], up[j])
    add(*blocks(g["w_ffn_down"][0], range(8)))
    add(*blocks(g["w_ple_gate"][0], range(8)))
    b = blocks(w_in2, range(80))
    add(*b[16:32], *b[0:8], *token_blocks(w_in2, range(4, 8)), *b[40:48], *token_blocks(w_in2, (24, 25)),
        *b[52:56], *b[32:40])
    for base, w in ((56, g["w_hg_o_2"][0]), (64, g["w_na_o_2"][0]), (72, g["w_ca_o_2"][0])):
        o = blocks(w, range(8))
        for j in range(8):
            add(b[base + j], o[j])
    add(*blocks(g["w_out_2"][0], range(8)))
    u = blocks(g["w_up_2"][0], range(2 * FT))
    for j in range(FT):
        add(u[j], u[FT + j])
    add(*blocks(g["w_down_2"][0], range(8)))
    assert len(stream) == NBLOCKS, (len(stream), NBLOCKS)
    wstream = np.empty((NSLOTS, P, 16, P), f)
    for n, blk in enumerate(stream):
        wstream[n // 16, :, n % 16] = blk

    vec = np.concatenate([
        vecs(g["mix_pre_norm"], 8), vecs(g["conv_dw_w"][0], 4), vecs(g["conv_dw_b"], 4), vecs(g["conv_ln_w"], 4),
        vecs(g["conv_ln_b"], 4), vecs(g["mix_post_norm"], 8), vecs(g["ffn_pre_norm"], 8),
        vecs(g["ffn_post_norm"], 8), vecs(g["ple_post_norm"], 8), vecs(g["norm_mix_2"], 8),
        vecs(g["hg_lb_logits_2"][0], 8), vecs(g["hg_gnorm_2"], 1), vecs(g["mem_norm_2"], 8),
        vecs(g["norm_ffn_2"], 8), vecs(g["conv_w_2"][0], 44), vecs(g["conv_b_2"], 44),
        vecs(g["norm_final_2"], 8)], axis=1)
    assert vec.shape == (P, NVEC)

    idx = np.arange(P)
    con = [np.full((P, P), 1.0 / n, f) for n in (1024, 512, 128)] + [np.eye(P, dtype=f)]
    for b_ in LEVELS:
        same = (idx[:, None] // (2 * b_)) == (idx[None, :] // (2 * b_))
        apart = (idx[:, None] // b_) != (idx[None, :] // b_)
        con.append((same & apart).astype(f))
    con = np.concatenate(con, axis=1)
    half = P // 2
    freqs = (10000.0 ** (-np.arange(half, dtype=f) / half)).astype(f)
    ang = (np.arange(S, dtype=f)[None, :] * freqs[:, None]).astype(f).astype(np.float64)
    cos, sin = np.cos(ang).astype(f), np.sin(ang).astype(f)
    rope = np.stack([np.concatenate([cos, cos]), np.concatenate([sin, -sin])], axis=1)
    decay = np.zeros((P, RET, 384), np.float64)
    rel = (np.arange(S)[None, :] - idx[:, None]).astype(np.float64)
    for hd in range(RET):
        lg = np.float64(np.log(f(1.0 - 2.0 ** (-5.0 - hd))))
        d = np.where(rel >= 0, np.exp(lg * np.maximum(rel, 0.0)), 0.0) * float(P) ** -0.5
        decay[:, hd, 0:S] = d
        decay[:, hd, S:] = d[:, 0:P]

    def act_t(a, tiles):
        return np.ascontiguousarray(a.reshape(S, tiles, P).transpose(2, 1, 0))

    return {
        "xt": act_t(g["x"], 8), "memt": act_t(g["mem_2"], 8), "pt": act_t(g["p"], 2),
        "wstream": wstream,
        "wproj": np.ascontiguousarray(g["w_ple_proj"][0].reshape(2, P, D).transpose(1, 0, 2)),
        "vecs": np.ascontiguousarray(vec), "consts": np.ascontiguousarray(con, dtype=f),
        "rope_tab": np.ascontiguousarray(rope, dtype=f), "decay_tab": decay.astype(f),
        "rpb": np.ascontiguousarray(g["na_rpb_2"][0].reshape(NA * 15, 31)[:, ::-1]),
    }


def kernel(**inputs):
    import concourse.bacc as bacc
    from concourse.bass_utils import run_bass_kernel_spmd

    arrays = host_layout(inputs)
    nc = bacc.Bacc("TRN2", target_bir_lowering=False, num_devices=1)
    args = {k: nc.dram_tensor(k, v.shape, F32, kind="ExternalInput").ap() for k, v in arrays.items()}
    out = nc.dram_tensor("out_t", (P, KT, S), F32, kind="ExternalOutput").ap()
    toep = nc.dram_tensor("toep", (NA * 15, P), F32, kind="Internal").ap()
    program(nc, out=out, toep=toep, **args)
    r = run_bass_kernel_spmd(nc, [arrays], core_ids=[0])
    got = r.results[0]["out_t"]
    return np.ascontiguousarray(got.transpose(2, 1, 0)).reshape(1, S, D)
```

```python
from contextlib import ExitStack

import numpy as np
import concourse.bass as bass
from concourse import mybir

P = 128
D = 1024
S = 256
KT = D // P
DC = 512
DFF = 2816
FT = DFF // P
CW = 31
EPS = 1e-6
HG = 8
NA = 8
CA = 4
RET = 4
RAW = 3
UNITS = 4
UB = 8
SBUF_WORDS = 52912
PJ = 3

ALU = mybir.AluOpType
ACT = mybir.ActivationFunctionType
F32 = mybir.dt.float32
R32 = mybir.dt.float32r
I32 = mybir.dt.int32
AX = mybir.AxisListType

STAGES = [
    ("conv", 4, 16, "dve"), ("qk", 4, 16, "act"), ("v", 2, 16, "act"), ("g", 2, 16, "act"),
    ("memk", 2, 16, "act"), ("wout", 4, 16, "act"), ("memv", 2, 16, "act"),
    ("ff", 22, 16, "dve"), ("down", 4, 2 * FT, "act"), ("ple", 4, 16, "dve"),
    ("hff", 4, 16, "act"), ("hfb", 4, 16, "act"), ("hq", 4, 16, "act"), ("hi", 4, 16, "act"),
    ("hg", 4, 16, "act"), ("nq", 2, 16, "act"), ("nk", 2, 16, "act"), ("nv", 2, 16, "act"), ("cq", 2, 16, "act"),
    ("mhg", 8, 16, "dve"), ("mca", 8, 12, "dve"), ("mna", 8, 12, "dve"),
    ("wout2", 4, 16, "dve"), ("up", 22, 16, "dve"), ("down2", 4, 2 * FT, "dve"),
]
FILLS = [(name, j, nb, who) for name, n, nb, who in STAGES for j in range(n)]
INDEX = {(name, j): n for n, (name, j, _, _) in enumerate(FILLS)}
FIRST_BLOCK = [sum(f[2] for f in FILLS[:n]) for n in range(len(FILLS) + 1)]
NBLOCKS = FIRST_BLOCK[-1]
NSLOTS = NBLOCKS // 16
NUNITS = NBLOCKS // UB
TOKEN_STAGES = ("v", "memv", "hi", "nv")

_ENDS = sorted({FIRST_BLOCK[n + 1] for n in range(len(FILLS))} | {UB * (u + 1) for u in range(NUNITS)})
STEP = {end: n + 1 for n, end in enumerate(_ENDS)}


def fill_step(n):
    return STEP[FIRST_BLOCK[n + 1]]


def unit_step(u):
    return STEP[UB * (u + 1)]


_BUSY = [(INDEX[("hq", 0)], INDEX[("cq", 1)])]
_POOL_ONLY = [(INDEX[("conv", 2)], INDEX[("wout", 0)]), (INDEX[("mhg", 0)], INDEX[("mhg", 1)]),
              (INDEX[("mca", 0)], INDEX[("mna", 7)])]


def _within(u, ranges):
    return any(FIRST_BLOCK[a] <= UB * u < FIRST_BLOCK[b + 1] for a, b in ranges)


def _lo_engine(u):
    if _within(u, _POOL_ONLY):
        return "pool"
    busy = _within(u, _BUSY)
    return "dve" if u % 4 == 0 or (u % 4 == 2 and not busy) else "pool"


LO_ENGINE = [_lo_engine(u) for u in range(NUNITS)]

STATS = [("mix_pre", 2), ("mem", 2), ("ln_mean", 0), ("ln_var", 1),
         ("mix_post", 4), ("ffn_pre", 4), ("ffn_post", 4), ("ple_post", 4), ("mix2", 4),
         ("ffn2", 4), ("final", 4)]
STAT = {name: n for n, (name, _) in enumerate(STATS)}
ROOTS = [name for name, _ in STATS if name != "ln_mean"]
SQ_BEFORE = {name: sum(c for _, c in STATS[:n]) for n, (name, _) in enumerate(STATS)}

VEC_SIZES = [("mix_pre", 8), ("dw_w", 4 * CW), ("dw_b", 4), ("ln_w", 4), ("ln_b", 4), ("mix_post", 8),
             ("ffn_pre", 8), ("ffn_post", 8), ("ple_post", 8), ("norm_mix2", 8), ("lb", 16), ("gnorm", 1),
             ("mem_norm", 8), ("norm_ffn2", 8), ("conv_w", 3 * 44), ("conv_b", 44), ("norm_final", 8)]
VEC = {}
for _n, _c in VEC_SIZES:
    VEC[_n] = sum(c for n, c in VEC_SIZES[:len(VEC)])
NVEC = sum(c for _, c in VEC_SIZES)

CONST = {"m1024": 0, "m512": P, "m128": 2 * P, "ident": 3 * P, "mask": 4 * P}
LEVELS = [1, 2, 4, 8, 16, 32, 64]
NCONST = 4 * P + len(LEVELS) * P


def lo_count(u, who):
    return sum(1 for e in LO_ENGINE[:u + 1] if e == who)


def ahead_target(n):
    return min(NUNITS, FIRST_BLOCK[n] // UB + UNITS)


def split_target(n):
    return min(NUNITS, (FIRST_BLOCK[n + 1] - 1) // UB + UNITS)


def behind_target(n):
    return min(NUNITS, FIRST_BLOCK[n + 1] // UB + UNITS)


def freed_count(n, who):
    return sum(1 for f in FILLS[:n + 1] if f[3] == who)


def program(nc, xt, memt, pt, wstream, wproj, vecs, consts, rope_tab, decay_tab, rpb, out, toep):
    ctx = ExitStack()
    with ctx:
        def sb(name, shape):
            return ctx.enter_context(nc.sbuf_tensor(name, [P] + shape, F32))

        def sem(name):
            return ctx.enter_context(nc.semaphore(name))

        base = nc.sbuf_base
        fence = sb("fence", [SBUF_WORDS])
        top = [(base + 31) // 32 * 32]

        def place(name, shape, dt=F32, offset=None):
            size = int(np.prod(shape)) * 4
            if offset is None:
                offset = top[0]
                top[0] += (size + 31) // 32 * 32
            assert offset + size <= base + 4 * SBUF_WORDS, (name, offset + size - base)
            return nc.alloc_sbuf_tensor_at(name, [P] + shape, dt, offset=offset)

        raw = place("raw", [RAW, 16, P])
        w_hi = place("w_hi", [UNITS, UB, P], R32)
        w_lo = place("w_lo", [UNITS, UB, P], R32)
        x = place("x", [KT, S])
        y = place("y", [KT, S])
        sq = place("sq", [KT, S])
        h = place("h", [2, KT, S], R32)
        vec = place("vec", [NVEC])
        con = place("con", [NCONST])
        rstd = place("rstd", [2 * S])
        rstd_h = place("rstd_h", [S])
        std = place("std", [2 * S])
        eps = place("eps", [1])
        spare = place("spare", [16])
        gate_tmp = place("gate_tmp", [2, 2, S])
        prod_tmp = place("prod_tmp", [2, S])
        mem_k = place("mem_k", [CA, S])
        mem_v = place("mem_v", [2, DC])
        lb = place("lb", [6, 16])
        soft = place("soft", [2, 3, 2])
        arena = top[0]

        def at(kib, name, *shape, dt=F32):
            return place(name, list(shape), dt, offset=arena + int(1024 * kib))

        conv_in = at(0, "conv_in", 4, CW - 1 + S)
        conv_y = at(5, "conv_y", 4, S)
        q_raw = at(9, "q_raw", RET, S)
        k_raw = at(13, "k_raw", RET, S)
        v_ret = at(17, "v_ret", 2, DC)
        g_ret = at(21, "g_ret", RET, S)
        o_ret = at(25, "o_ret", RET, S)
        s_ret = at(29, "s_ret", RET, 384)
        ret_inv = at(29, "ret_inv", RET, S)
        decay = at(35, "decay", RET, 384)
        rope_a = at(41, "rope_a", RET, S)
        rope_b = at(45, "rope_b", RET, S)
        rope = at(49, "rope", 2, S)
        mem_n = at(51, "mem_n", 2, KT, S, dt=R32)
        mix = at(35, "mix", 2, KT, S, dt=R32)
        ff = at(0, "ff", 2, FT, S, dt=R32)
        w_ple = at(44, "w_ple", 2, D)
        p_in = at(52, "p_in", 2, S)
        ple_p = at(54, "ple_p", KT, S)
        x_split = at(62, "x_split", 2, KT, S, dt=R32)
        f_f = at(0, "f_f", HG, S)
        f_b = at(8, "f_b", HG, S)
        k_fb = at(16, "k_fb", 2, HG, S)
        q_bf = at(32, "q_bf", 2, HG, S)
        k_f, k_b, q_b, q_f = k_fb[:, 0], k_fb[:, 1], q_bf[:, 0], q_bf[:, 1]
        v_hg = at(48, "v_hg", 2, D)
        st_hg = at(56, "st_hg", HG, 4 * P)
        k_mix = [gate_tmp[:].rearrange("p a b s -> p (a b) s"),
                 at(80, "k_mix", 4, S)[:]]
        v_na = at(72, "v_na", 2, DC)
        q_ca = at(76, "q_ca", CA, S)
        toep_t = at(0, "toep_t", NA, 6 * 64)
        o_hg = at(16, "o_hg", HG, S)
        hg_sq = at(24, "hg_sq", HG, S)
        merged = at(24, "merged", KT, S)
        o_hg_s = at(32, "o_hg_s", 2, HG, S, dt=R32)
        merged_s = at(32, "merged_s", 2, KT, S, dt=R32)
        probs = at(48, "probs", 2, 2 * S)
        probs_t = at(52, "probs_t", 2, 2 * S)
        o_na = at(56, "o_na", 2, 4, S, dt=R32)
        o_ca = at(64, "o_ca", 2, 4, S, dt=R32)
        ksum = sq
        gate_hg = sq
        q_s = y
        q_na, k_na = y[:, 0:4], y[:, 4:8]
        mem_x = y

        pj = [ctx.enter_context(nc.psum_tensor(f"pj{i}", [P, 2, S], F32)) for i in range(PJ)]
        sc = [ctx.enter_context(nc.psum_tensor(f"sc{i}", [P, 512], F32)) for i in range(4)]
        st = ctx.enter_context(nc.psum_tensor("st", [P, 512], F32))

        mix_keys = sem("mix_keys")
        load_x = [sem(f"load_x{i}") for i in range(2)]
        load_mean = sem("load_mean")
        load_params = sem("load_params")
        load_mem = sem("load_mem")
        load_side = sem("load_side")
        slot_ready = [sem(f"slot_ready{i}") for i in range(RAW)]
        hi_ready = sem("hi_ready")
        lo_ready = {"dve": sem("lo_ready_dve"), "pool": sem("lo_ready_pool")}
        pe_step = sem("pe_step")
        load_ple = sem("load_ple")
        h_full = sem("h_full")
        h_hi = sem("h_hi")
        mem_full = sem("mem_full")
        mem_hi = sem("mem_hi")
        mix_full = sem("mix_full")
        mix_hi = sem("mix_hi")
        mix_ready = sem("mix_ready")
        ret_full = sem("ret_full")
        ret_squares = sem("ret_squares")
        ret_stat = sem("ret_stat")
        ret_root = sem("ret_root")
        f_hi = sem("f_hi")
        up_full = sem("up_full")
        xs_hi = sem("xs_hi")
        xs_ready = sem("xs_ready")
        hg_hi = sem("hg_hi")
        hg_split = sem("hg_split")
        att_ready = sem("att_ready")
        merge_full = sem("merge_full")
        merge_hi = sem("merge_hi")
        freed = {"act": sem("freed_act"), "dve": sem("freed_dve")}
        gate_done = sem("gate_done")
        sq_ready = sem("sq_ready")
        stat_done = sem("stat_done")
        root_done = sem("root_done")
        eps_ready = sem("eps_ready")
        stat_read = sem("stat_read")
        h_ready = sem("h_ready")
        x_ready = sem("x_ready")
        mem_ready = sem("mem_ready")
        pad_ready = sem("pad_ready")
        conv_ready = sem("conv_ready")
        rope_ready = sem("rope_ready")
        sc_done = sem("sc_done")
        s_ready = sem("s_ready")
        o_copied = sem("o_copied")
        lb_exp = sem("lb_exp")
        lb_ready = sem("lb_ready")
        ple_proj = sem("ple_proj")
        ple_mul = sem("ple_mul")
        ff_ready = sem("ff_ready")
        gates_ready = sem("gates_ready")
        level_ready = sem("level_ready")
        st_diag = sem("st_diag")
        st_mask = sem("st_mask")
        st_cross = sem("st_cross")
        hg_squares = sem("hg_squares")
        hg_stat = sem("hg_stat")
        hg_root = sem("hg_root")
        hg_inv = sem("hg_inv")
        hg_out = sem("hg_out")
        toep_zero = sem("toep_zero")
        toep_row = sem("toep_row")
        toep_load = sem("toep_load")
        toep_sel = sem("toep_sel")
        zero_ready = sem("zero_ready")
        logits_ready = sem("logits_ready")
        exp_ready = sem("exp_ready")
        p_ready = sem("p_ready")
        turned = sem("turned")
        pt_ready = sem("pt_ready")
        scored = sem("scored")
        pv_done = sem("pv_done")
        o_att = sem("o_att")
        merge_ready = sem("merge_ready")
        up_lin = sem("up_lin")
        up_conv = sem("up_conv")
        gelu_done = sem("gelu_done")
        dve_chain = sem("dve_chain")
        act_chain = sem("act_chain")
        pool_chain = sem("pool_chain")
        out_ready = sem("out_ready")
        stored = sem("stored")

        def col(name, i=0):
            c = VEC[name] + i
            return vec[:, c:c + 1]

        def mat(name, i=0):
            c = CONST[name] + i * P
            return con[:, c:c + P]

        def fi(name, j=0):
            return INDEX[(name, j)]

        def bank(name, j):
            return pj[fi(name, j) % PJ]

        def gate_slot(name, j):
            return (freed_count(fi(name, j), "dve") - 1) % 2

        def wait_gate_slot(eng, name, j):
            d = freed_count(fi(name, j), "dve") - 1
            if d >= 2:
                eng.wait_ge(freed["dve"], d - 1)

        def wait_read(eng, name, j):
            n = fi(name, j)
            eng.wait_ge(freed[FILLS[n][3]], freed_count(n, FILLS[n][3]))

        H_PAIRS = {"mix_pre": 0, "ffn_pre": 4, "mix2": 8, "ffn2": 12}
        X_PAIRS = {"mix_post": 0, "ffn_post": 4, "ple_post": 8}
        SC_RET, SC_RO = 0, RET
        SC_LEVEL = 2 * RET
        SC_CROSS = SC_LEVEL + 4 * (1 + len(LEVELS))
        SC_HGO = SC_CROSS + 4

        def diag_view(g):
            v = st_hg[:, 2 * g:2 * g + 2].rearrange("p a (b c) -> p a b c", c=P)
            return v[:, :, 0:4:3]

        SIDE_FILLS = [(name, j) for name, j, _, _ in FILLS if name in ("hi", "hg", "nq", "nk", "nv", "cq")]
        LEVEL_AFTER = {1: 0, 3: 1, 5: 2, 7: 3, 9: 4, 11: 5, 12: 6}
        DIAGONAL_AFTER, CROSS_AFTER = 1, 13
        HEADS = [("ca", i) for i in range(CA)] + [("na", i) for i in range(NA)]
        NHEADS = len(HEADS)
        MERGE_FILLS = [(name, j) for name, j, _, _ in FILLS if name in ("mhg", "mna", "mca")]

        def unit_of_raw(u):
            return raw[:, (u // 2) % RAW, UB * (u % 2):UB * (u % 2) + UB]

        def as_f32(v):
            return v.bitcast(F32)

        def partners(first, b):
            n = first.shape[-1] * (first.shape[1] if len(first.shape) == 3 else 1)
            return bass.AP(tensor=first.tensor, offset=first.offset,
                           ap=[first.ap[0], [2 * b, n // (2 * b)], [HG * S + b, 2], [1, b]])

        block = ctx.enter_context(nc.Block())

        @block.sync
        def _(sp):
            sp.dma_start(con[:, 0:P], consts[:, 0:P]).then_inc(load_mean, 16)
            sp.dma_start(x[:, 0:4], xt[:, 0:4]).then_inc(load_x[0], 16)
            sp.dma_start(x[:, 4:8], xt[:, 4:8]).then_inc(load_x[1], 16)
            sp.dma_start(vec[:], vecs).then_inc(load_params, 16)
            sp.dma_start(con[:, P:4 * P], consts[:, P:4 * P]).then_inc(load_params, 16)
            for n in range(NSLOTS):
                if n >= RAW:
                    for who in ("dve", "pool"):
                        c = lo_count(2 * (n - RAW) + 1, who)
                        if c:
                            sp.wait_ge(lo_ready[who], c)
                if n == FIRST_BLOCK[fi("mhg", 1)] // 16:
                    sp.wait_ge(toep_row, 16)
                    sp.wait_ge(level_ready, 1 + len(LEVELS))
                    for half in range(2):
                        for hd in range(NA):
                            off = (hd * 15 + 5 - half) * P
                            src = bass.AP(tensor=toep.tensor, offset=toep.offset + off, ap=[[1, 64], [P, 6], [1, 64]])
                            sp.dma_start(toep_t[64 * half:64 * half + 64, hd].rearrange("p (d c) -> p d c", c=64),
                                         src).then_inc(toep_load, 16)
                sp.dma_start(raw[:, n % RAW], wstream[n]).then_inc(slot_ready[n % RAW], 16)
                if n == 1:
                    sp.dma_start(mem_x[:], memt).then_inc(load_mem, 16)
                if n == 6:
                    sp.dma_start(rope[:], rope_tab).then_inc(load_side, 16)
                    sp.dma_start(decay[:], decay_tab).then_inc(load_side, 16)
                    sp.dma_start(con[:, 4 * P:], consts[:, 4 * P:]).then_inc(load_side, 16)
                if n == fi("ff", 4):
                    sp.wait_ge(pe_step, fill_step(fi("ff", 0)))
                    sp.dma_start(p_in[:], pt).then_inc(load_ple, 16)
                    sp.dma_start(w_ple[:], wproj).then_inc(load_ple, 16)
            for p in range(4):
                sp.wait_ge(out_ready, p + 1)
                sp.dma_start(out[:, 2 * p:2 * p + 2], y[:, 2 * p:2 * p + 2]).then_inc(stored, 16)
            sp.wait_ge(stored, 64)

        @block.gpsimd
        def _(pool):
            chain = [0]

            def link(ins):
                chain[0] += 1
                ins.then_inc(pool_chain, 1)
                return chain[0]

            nc.gpsimd.memset(conv_in[:, :, 0:CW - 1], 0.0).then_inc(pad_ready, 1)
            nc.gpsimd.memset(prod_tmp[:, 0, 0:P], 0.0).then_inc(zero_ready, 1)
            pool.wait_ge(zero_ready, 1)
            pool.dma_start(toep, prod_tmp[0:NA * 15, 0, 0:P]).then_inc(toep_zero, 16)
            pool.wait_ge(toep_zero, 16)
            pool.dma_start(toep[:, 48:79], rpb).then_inc(toep_row, 16)
            pool.wait_ge(toep_row, 16)

            fed = [0]

            def feed(target):
                for u in range(fed[0], target):
                    if LO_ENGINE[u] == "pool":
                        pool.wait_ge(hi_ready, u + 1)
                        nc.gpsimd.tensor_tensor(w_lo[:, u % UNITS], unit_of_raw(u), as_f32(w_hi[:, u % UNITS]),
                                                ALU.subtract).then_inc(lo_ready["pool"], 1)
                fed[0] = max(fed[0], target)

            feed(ahead_target(fi("ple", 0)))
            for i in range(4):
                pool.wait_ge(xs_hi, i + 1)
                nc.gpsimd.tensor_tensor(x_split[:, 1, 2 * i:2 * i + 2], x[:, 2 * i:2 * i + 2],
                                        as_f32(x_split[:, 0, 2 * i:2 * i + 2]), ALU.subtract).then_inc(xs_ready, 1)
            feed(ahead_target(fi("mhg", 1)))
            pool.wait_ge(toep_load, 16 * 2 * NA)
            for half in range(2):
                feed(ahead_target(fi("mhg", 1 + 2 * half)))
                pool.wait_ge(lo_ready["pool"], lo_count(fed[0] - 1, "pool"))
                v = toep_t[64 * half:64 * half + 64].rearrange("p a (d c) -> p (a d) c", c=64)
                lo, hi = v[:, :, 16:64], v[:, :, 0:48]
                a = link(nc.gpsimd.affine_select(out=lo, in_=lo, compare_op=ALU.is_ge, fill=-1e30, base=55,
                                                 pattern=[[0, NA * 6], [-1, 48]], channel_multiplier=-1))
                pool.wait_ge(pool_chain, a)
                nc.gpsimd.affine_select(out=hi, in_=hi, compare_op=ALU.is_ge, fill=-1e30, base=-56,
                                        pattern=[[0, NA * 6], [1, 48]], channel_multiplier=1
                                        ).then_inc(toep_sel, 1)
                pool.wait_ge(toep_sel, half + 1)
            feed(NUNITS)

        @block.scalar
        def _(act):
            A = nc.scalar.activation
            chain = [0]

            fed = [0]

            def feed(target):
                for u in range(fed[0], target):
                    if u % 2 == 0:
                        act.wait_ge(slot_ready[(u // 2) % RAW], 16 * (u // 2 // RAW + 1))
                    if u >= UNITS:
                        act.wait_ge(pe_step, unit_step(u - UNITS))
                    nc.scalar.copy(w_hi[:, u % UNITS], unit_of_raw(u)).then_inc(hi_ready, 1)
                fed[0] = max(fed[0], target)

            def squares_of_x(stage):
                for i in range(4):
                    if stage in X_PAIRS:
                        act.wait_ge(x_ready, X_PAIRS[stage] + i + 1)
                    else:
                        wait_read(act, stage, i)
                    A(sq[:, 2 * i:2 * i + 2], x[:, 2 * i:2 * i + 2], ACT.Square).then_inc(sq_ready, 1)

            def hi_of_h(name):
                for p in range(4):
                    act.wait_ge(h_full, H_PAIRS[name] + p + 1)
                    nc.scalar.copy(h[:, 0, 2 * p:2 * p + 2], sq[:, 2 * p:2 * p + 2]).then_inc(h_hi, 1)

            def root(name, n=S):
                act.wait_ge(stat_done, STAT[name] + 1)
                if STAT[name]:
                    act.wait_ge(stat_read, STAT[name])
                A(std[:, 0:n], st[:, 0:n], ACT.Sqrt, bias=eps[:, 0:1]).then_inc(root_done, 1)

            def prime(func):
                prime.count += 1
                A(spare[:, prime.count:prime.count + 1], spare[:, 0:1], func)

            prime.count = 0

            def level_keys(i):
                b = LEVELS[i]
                act.wait_ge(level_ready, i + 1)
                for half in range(2):
                    dst = k_mix[half].rearrange("p a s -> p (a s)").rearrange("p (n two b) -> p n two b", two=2, b=b)
                    nc.scalar.copy(dst, partners(k_f[:, 4 * half:4 * half + 4], b)).then_inc(mix_keys, 1)

            def wait_fill(name, j, behind=True):
                n = fi(name, j)
                feed(split_target(n))
                side = n - fi("hi", 0)
                if side in LEVEL_AFTER:
                    level_keys(LEVEL_AFTER[side])
                act.wait_ge(pe_step, fill_step(n))
                if behind:
                    feed(behind_target(n))

            def post_norm_fill(name, j):
                wait_fill(name, j, behind=j < 3)
                A(sq[:, 2 * j:2 * j + 2], bank(name, j)[:], ACT.Square).then_inc(sq_ready, 1)
                nc.scalar.copy(y[:, 2 * j:2 * j + 2], bank(name, j)[:]).then_inc(freed["act"], 1)
                feed(behind_target(fi(name, j)))

            def copy_fill(name, j, dst, func=None, view=None):
                wait_fill(name, j)
                src = bank(name, j)[:]
                if func is None:
                    nc.scalar.copy(dst, src).then_inc(freed["act"], 1)
                else:
                    A(dst, src, func).then_inc(freed["act"], 1)

            act.wait_ge(eps_ready, 2)
            prime(ACT.Sqrt)
            for i in range(2):
                act.wait_ge(load_x[i], 16)
                A(sq[:, 4 * i:4 * i + 4], x[:, 4 * i:4 * i + 4], ACT.Square).then_inc(sq_ready, 1)
            feed(ahead_target(0))
            root("mix_pre")
            act.wait_ge(lb_exp, 1)
            A(lb[:, 1], lb[:, 0], ACT.Exp).then_inc(lb_exp, 1)
            hi_of_h("mix_pre")
            act.wait_ge(load_mem, 16)
            act.wait_ge(h_ready, H_PAIRS["mix_pre"] + 4)
            for i in range(2):
                A(sq[:, 4 * i:4 * i + 4], mem_x[:, 4 * i:4 * i + 4], ACT.Square).then_inc(sq_ready, 1)
            for j in range(4):
                wait_fill("conv", j)
                wait_gate_slot(act, "conv", j)
                A(gate_tmp[:, gate_slot("conv", j), 0], bank("conv", j)[:, 1], ACT.Sigmoid).then_inc(gate_done, 1)
            root("mem")
            for p in range(4):
                if p == 2:
                    feed(split_target(fi("qk", 0)))
                act.wait_ge(mem_full, p + 1)
                nc.scalar.copy(mem_n[:, 0, 2 * p:2 * p + 2], mem_x[:, 2 * p:2 * p + 2]).then_inc(mem_hi, 1)
            for j in range(2):
                copy_fill("qk", j, q_raw[:, 2 * j:2 * j + 2])
            for j in range(2):
                copy_fill("qk", 2 + j, k_raw[:, 2 * j:2 * j + 2])
            for j in range(2):
                copy_fill("v", j, v_ret[:, :, 256 * j:256 * j + 256])
            for j in range(2):
                copy_fill("g", j, g_ret[:, 2 * j:2 * j + 2], ACT.Silu)
            for j in range(2):
                copy_fill("memk", j, mem_k[:, 2 * j:2 * j + 2])
            prime(ACT.Sqrt)
            for hd in range(RET):
                act.wait_ge(sc_done, SC_RO + hd + 1)
                A(sq[:, 4 + hd], sc[hd][:, 0:S], ACT.Square).then_inc(ret_squares, 1)
                nc.scalar.copy(o_ret[:, hd], sc[hd][:, 0:S]).then_inc(o_copied, 1)
            for hd in range(RET):
                act.wait_ge(ret_stat, hd + 1)
                A(ret_inv[:, hd], sc[hd][:, 0:S], ACT.Sqrt, bias=eps[:, 0:1]).then_inc(ret_root, 1)
            act.wait_ge(conv_ready, 2)
            A(sq[:, 0:4], conv_y[:], ACT.Square).then_inc(sq_ready, 1)
            root("ln_var")
            prime(ACT.Silu)
            act.wait_ge(conv_ready, 3)
            for j in range(4):
                A(conv_y[:, j], conv_y[:, j], ACT.Silu, bias=col("ln_b", j), scale=col("ln_w", j)).then_inc(mix_full, 1)
                if j % 2:
                    act.wait_ge(mix_full, j + 1)
                    nc.scalar.copy(mix[:, 0, j - 1:j + 1], conv_y[:, j - 1:j + 1]).then_inc(mix_hi, 1)
            for g in range(2):
                act.wait_ge(ret_full, g + 1)
                nc.scalar.copy(mix[:, 0, 4 + 2 * g:6 + 2 * g], o_ret[:, 2 * g:2 * g + 2]).then_inc(mix_hi, 1)
            prime(ACT.Sqrt)
            for j in range(4):
                post_norm_fill("wout", j)
            root("mix_post")
            squares_of_x("mix_post")
            copy_fill("memv", 0, mem_v[:, :, 0:256])
            root("ffn_pre")
            hi_of_h("ffn_pre")
            copy_fill("memv", 1, mem_v[:, :, 256:512])
            for j in range(23):
                if j < 22:
                    wait_fill("ff", j)
                    wait_gate_slot(act, "ff", j)
                    A(gate_tmp[:, gate_slot("ff", j), 0], bank("ff", j)[:, 0], ACT.Silu).then_inc(gate_done, 1)
                if j:
                    wait_read(act, "ff", j - 1)
                    nc.scalar.copy(ff[:, 0, j - 1], prod_tmp[:, (j - 1) % 2]).then_inc(f_hi, 1)
            prime(ACT.Sqrt)
            for j in range(4):
                post_norm_fill("down", j)
            root("ffn_post")
            for j in range(4):
                act.wait_ge(sc_done, SC_LEVEL + j + 1)
                nc.scalar.copy(ple_p[:, 2 * j:2 * j + 2], sc[j][:]).then_inc(ple_proj, 1)
                act.wait_ge(x_ready, X_PAIRS["ffn_post"] + j + 1)
                nc.scalar.copy(x_split[:, 0, 2 * j:2 * j + 2], x[:, 2 * j:2 * j + 2]).then_inc(xs_hi, 1)
            for j in range(4):
                wait_fill("ple", j, behind=j < 3)
                wait_gate_slot(act, "ple", j)
                A(gate_tmp[:, gate_slot("ple", j)], bank("ple", j)[:], ACT.Sigmoid).then_inc(gate_done, 1)
                if j == 3:
                    prime(ACT.Sqrt)
                wait_read(act, "ple", j)
                A(sq[:, 2 * j:2 * j + 2], y[:, 2 * j:2 * j + 2], ACT.Square).then_inc(sq_ready, 1)
                feed(behind_target(fi("ple", j)))
            root("ple_post")
            squares_of_x("ple_post")
            root("mix2")

            hi_of_h("mix2")

            for stage, f, k in (("hff", f_f, k_f), ("hfb", f_b, k_b)):
                for j in range(4):
                    wait_fill(stage, j)
                    A(f[:, 2 * j:2 * j + 2], bank(stage, j)[:], ACT.Sigmoid)
                    A(k[:, 2 * j:2 * j + 2], bank(stage, j)[:], ACT.Sigmoid, scale=-1.0).then_inc(freed["act"], 1)
            for j in range(4):
                copy_fill("hq", j, q_s[:, 2 * j:2 * j + 2], ACT.Silu)

            def diagonal():
                for g in range(4):
                    act.wait_ge(sc_done, SC_LEVEL + 4 + g + 1)
                    nc.scalar.copy(diag_view(g), sc[g][:].rearrange("p (a b c) -> p a b c", a=2, b=2)
                                   ).then_inc(st_diag, 1)

            def cross():
                prime(ACT.Sqrt)
                for g in range(4):
                    act.wait_ge(sc_done, SC_CROSS + 4 + g + 1)
                    nc.scalar.copy(st_hg[:, 2 * g:2 * g + 2, P:3 * P],
                                   sc[g][:].rearrange("p (a b) -> p a b", a=2)).then_inc(st_cross, 1)

            def hg_outputs():
                for g in range(5):
                    if g < 4:
                        act.wait_ge(sc_done, SC_HGO + 4 + g + 1)
                        o = sc[g][:].rearrange("p (a b) -> p a b", a=2)
                        A(hg_sq[:, 2 * g:2 * g + 2], o, ACT.Square).then_inc(hg_squares, 1)
                        nc.scalar.copy(o_hg[:, 2 * g:2 * g + 2], o).then_inc(o_copied, 1)
                    if g:
                        act.wait_ge(hg_stat, g)
                        A(hg_sq[:, 2 * g - 2:2 * g], sc[g - 1][:].rearrange("p (a b) -> p a b", a=2), ACT.Sqrt,
                          bias=eps[:, 0:1]).then_inc(hg_root, 1)

            def hg_hi_part(g):
                act.wait_ge(hg_out, g + 1)
                nc.scalar.copy(o_hg_s[:, 0, 2 * g:2 * g + 2], o_hg[:, 2 * g:2 * g + 2]).then_inc(hg_hi, 1)

            for e, (name, j) in enumerate(SIDE_FILLS):
                if name in ("hi", "nv"):
                    dst = (v_hg if name == "hi" else v_na)[:, :, 256 * j:256 * j + 256]
                    copy_fill(name, j, dst)
                elif name == "hg":
                    copy_fill(name, j, gate_hg[:, 2 * j:2 * j + 2], ACT.Silu)
                else:
                    copy_fill(name, j, {"nq": q_na, "nk": k_na, "cq": q_ca}[name][:, 2 * j:2 * j + 2])
                if e == DIAGONAL_AFTER:
                    diagonal()
                if e == CROSS_AFTER:
                    cross()
                    hg_outputs()
                if e >= CROSS_AFTER:
                    hg_hi_part(e - CROSS_AFTER)
            hg_hi_part(3)

            def att_exp(a):
                act.wait_ge(logits_ready, a + 1)
                for t in range(2):
                    if HEADS[a][0] == "na":
                        src, scale = probs[:, a % 2, t * S:t * S + S], 1.0
                    else:
                        src, scale = sc[a % 2][:, t * S:t * S + S], float(P) ** -0.5
                    ins = A(probs[:, a % 2, t * S:t * S + S], src, ACT.Exp, bias=soft[:, a % 2, 0, t:t + 1],
                            scale=scale, accum_out=soft[:, a % 2, 1, t:t + 1])
                ins.then_inc(exp_ready, 1)

            def att_turn(a):
                act.wait_ge(turned, a + 1)
                if a >= 2:
                    act.wait_ge(pv_done, a - 1)
                nc.scalar.copy(probs_t[:, a % 2], sc[2][:]).then_inc(pt_ready, 1)

            def att_out(a):
                act.wait_ge(pv_done, a + 1)
                kind, i = HEADS[a]
                if kind == "ca":
                    nc.scalar.copy(o_ca[:, 0, i], sc[3][:, 0:S]).then_inc(o_att, 1)
                elif i % 2:
                    nc.scalar.copy(o_na[:, 0, i // 2], sc[3][:, 0:S]).then_inc(o_att, 1)

            def att_slot(i):
                if i < NHEADS:
                    att_exp(i)
                if 1 <= i <= NHEADS:
                    att_turn(i - 1)
                if 2 <= i < NHEADS + 2:
                    att_out(i - 2)

            def merge_split(j):
                act.wait_ge(merge_full, j + 1)
                nc.scalar.copy(merged_s[:, 0, j], merged[:, j]).then_inc(merge_hi, 1)

            att_slot(0)
            for i, (name, j) in enumerate(MERGE_FILLS):
                wait_fill(name, j)
                wait_gate_slot(act, name, j)
                A(gate_tmp[:, gate_slot(name, j), 0], bank(name, j)[:, 0], ACT.Tanh, scale=0.5).then_inc(gate_done, 1)
                if i >= 17:
                    merge_split(i - 17)
                att_slot(i + 1)
            merge_split(7)
            prime(ACT.Sqrt)
            for j in range(4):
                wait_fill("wout2", j, behind=j < 3)
            squares_of_x("wout2")
            feed(behind_target(fi("wout2", 3)))
            root("ffn2")
            hi_of_h("ffn2")
            for j in range(24):
                if j < 22:
                    wait_fill("up", j)
                    if j >= 2:
                        act.wait_ge(up_full, j - 1)
                    for i in range(2):
                        ins = A(gate_tmp[:, j % 2, i], bank("up", j)[:, i], ACT.Identity,
                                bias=col("conv_b", 22 * i + j), scale=col("conv_w", 44 + 22 * i + j))
                    ins.then_inc(up_lin, 1)
                if 1 <= j <= 22:
                    i = j - 1
                    wait_read(act, "up", i)
                    A(gate_tmp[:, i % 2, 0], gate_tmp[:, i % 2, 0], ACT.Gelu_apprx_tanh).then_inc(gelu_done, 1)
                if j >= 2:
                    act.wait_ge(up_full, j - 1)
                    nc.scalar.copy(ff[:, 0, j - 2], prod_tmp[:, j % 2]).then_inc(f_hi, 1)
            prime(ACT.Sqrt)
            for j in range(4):
                wait_fill("down2", j)
            squares_of_x("down2")
            root("final")

        @block.vector
        def _(dve):
            V = nc.vector
            chain = [0]

            def link(ins):
                chain[0] += 1
                ins.then_inc(dve_chain, 1)
                return chain[0]

            def after(n):
                dve.wait_ge(dve_chain, n)

            def over(v, n):
                return v.unsqueeze(1).to_broadcast([P, n, S])

            def root(name, dst, n=S):
                dve.wait_ge(root_done, ROOTS.index(name) + 1)
                V.reciprocal(dst, std[:, 0:n]).then_inc(stat_read, 1)
                dve.wait_ge(stat_read, STAT[name] + 1)

            fed = [0]

            def feed(target):
                for u in range(fed[0], target):
                    if LO_ENGINE[u] == "dve":
                        dve.wait_ge(hi_ready, u + 1)
                        V.tensor_tensor(w_lo[:, u % UNITS], unit_of_raw(u), as_f32(w_hi[:, u % UNITS]),
                                        ALU.subtract).then_inc(lo_ready["dve"], 1)
                fed[0] = max(fed[0], target)

            def feed_fill(name, j):
                feed(split_target(fi(name, j)))

            def feed_behind(name, j):
                feed(behind_target(fi(name, j)))

            def lo_part(split, full, a, b):
                return V.tensor_tensor(split[:, 1, a:b], full, as_f32(split[:, 0, a:b]), ALU.subtract)

            def norm_to_h(name, gain):
                root(name, rstd_h[:])
                base_n = H_PAIRS[name]
                for p in range(5):
                    if p < 4:
                        for t in (2 * p, 2 * p + 1):
                            ins = V.scalar_tensor_tensor(out=sq[:, t], in0=x[:, t], scalar=col(gain, t),
                                                         in1=rstd_h[:], op0=ALU.mult, op1=ALU.mult)
                        ins.then_inc(h_full, 1)
                    if p:
                        dve.wait_ge(h_hi, base_n + p)
                        lo_part(h, sq[:, 2 * p - 2:2 * p], 2 * p - 2, 2 * p).then_inc(h_ready, 1)
                dve.wait_ge(h_ready, base_n + 4)

            def post_norm(name, gain):
                root(name, rstd[:, 0:S])
                for i in range(4):
                    for t in (2 * i, 2 * i + 1):
                        n = link(V.scalar_tensor_tensor(out=y[:, t], in0=y[:, t], scalar=col(gain, t),
                                                        in1=rstd[:, 0:S], op0=ALU.mult, op1=ALU.mult))
                    after(n)
                    V.tensor_tensor(x[:, 2 * i:2 * i + 2], x[:, 2 * i:2 * i + 2], y[:, 2 * i:2 * i + 2],
                                    ALU.add).then_inc(x_ready, 1)
                dve.wait_ge(x_ready, X_PAIRS[name] + 4)

            def wait_gate(count):
                dve.wait_ge(gate_done, count)

            gates = [0]

            V.memset(spare[:, 0:1], 1.0).then_inc(eps_ready, 1)
            V.memset(eps[:], EPS).then_inc(eps_ready, 1)
            dve.wait_ge(load_params, 32)
            for i in range(2):
                dve.wait_ge(load_x[i], 16)
            logits = vec[:, VEC["lb"]:VEC["lb"] + 16]
            V.tensor_tensor(lb[:, 0], logits, logits, ALU.subtract).then_inc(lb_exp, 1)
            feed(ahead_target(0))
            norm_to_h("mix_pre", "mix_pre")
            dve.wait_ge(lb_exp, 2)
            after(link(V.reciprocal(lb[:, 2], lb[:, 1])))
            after(link(V.tensor_tensor(lb[:, 3], lb[:, 1], lb[:, 2], ALU.mult)))
            after(link(V.tensor_tensor(lb[:, 4], lb[:, 3], lb[:, 3], ALU.subtract)))
            after(link(V.tensor_scalar(lb[:, 4], lb[:, 4], 0.0, 1.0, ALU.max, ALU.min)))
            V.tensor_scalar(lb[:, 5], lb[:, 4], -1.0, 1.0, ALU.mult, ALU.add).then_inc(lb_ready, 1)

            seen, tap_of = [0] * 4, [0] * 4

            def taps(tiles, until):
                for w in range(min(tap_of[j] for j in tiles), until):
                    for j in tiles:
                        if w < tap_of[j]:
                            continue
                        tap_of[j] = w + 1
                        src = conv_in[:, j, w:w + S]
                        tap = col("dw_w", w * 4 + j)
                        if w == 0:
                            seen[j] = link(V.tensor_scalar(conv_y[:, j], src, tap, col("dw_b", j), ALU.mult, ALU.add))
                            continue
                        after(seen[j])
                        ins = V.scalar_tensor_tensor(out=conv_y[:, j], in0=src, scalar=tap, in1=conv_y[:, j],
                                                     op0=ALU.mult, op1=ALU.add)
                        if min(tap_of) == CW:
                            ins.then_inc(conv_ready, 1)
                        else:
                            seen[j] = link(ins)

            dve.wait_ge(pad_ready, 1)
            for j in range(4):
                gates[0] += 1
                feed_behind("conv", j)
                wait_gate(gates[0])
                V.tensor_tensor(conv_in[:, j, CW - 1:], bank("conv", j)[:, 0], gate_tmp[:, gate_slot("conv", j), 0],
                                ALU.mult).then_inc(freed["dve"], 1)
                if j in (1, 2):
                    dve.wait_ge(freed["dve"], 2)
                    taps((0, 1), 5 * j)
            root("mem", rstd[:, 0:S])
            for p in range(5):
                if p < 4:
                    for t in (2 * p, 2 * p + 1):
                        ins = V.scalar_tensor_tensor(out=mem_x[:, t], in0=mem_x[:, t], scalar=col("mem_norm", t),
                                                     in1=rstd[:, 0:S], op0=ALU.mult, op1=ALU.mult)
                    ins.then_inc(mem_full, 1)
                if p:
                    dve.wait_ge(mem_hi, p)
                    lo_part(mem_n, mem_x[:, 2 * p - 2:2 * p], 2 * p - 2, 2 * p).then_inc(mem_ready, 1)
            dve.wait_ge(mem_ready, 4)
            dve.wait_ge(freed["dve"], 4)
            taps((2, 3), 10)
            taps((0, 1, 2, 3), 18)
            dve.wait_ge(load_side, 48)
            for i, t in enumerate((q_raw, k_raw)):
                wait_read(dve, "qk", 2 * i + 1)
                if i:
                    dve.wait_ge(rope_ready, 1)
                V.tensor_tensor(rope_a[:], t[:], over(rope[:, 0], 4), ALU.mult)
                for a, b in ((0, 64), (64, 0)):
                    sin = rope[b:b + 64, 1].unsqueeze(1).to_broadcast([64, 4, S])
                    n = link(V.tensor_tensor(rope_b[a:a + 64], t[b:b + 64], sin, ALU.mult))
                after(n)
                V.tensor_tensor(t[:], rope_a[:], rope_b[:], ALU.add).then_inc(rope_ready, 1)
            taps((0, 1, 2, 3), 26)
            for hd in range(RET):
                dve.wait_ge(sc_done, SC_RET + hd + 1)
                V.tensor_tensor(s_ret[:, hd], sc[hd][:, 0:384], decay[:, hd], ALU.mult).then_inc(s_ready, 1)
            taps((0, 1, 2, 3), CW)
            def ret_norm(hd):
                dve.wait_ge(ret_root, hd + 1)
                after(link(V.reciprocal(ret_inv[:, hd], ret_inv[:, hd])))
                ret_norm.done = link(V.tensor_tensor(o_ret[:, hd], o_ret[:, hd], ret_inv[:, hd], ALU.mult))

            dve.wait_ge(stat_done, STAT["ln_mean"] + 1)
            V.tensor_copy(rstd[:, S:2 * S], st[:, 0:S]).then_inc(stat_read, 1)
            dve.wait_ge(stat_read, STAT["ln_mean"] + 1)
            V.tensor_tensor(conv_y[:], conv_y[:], over(rstd[:, S:2 * S], 4), ALU.subtract).then_inc(conv_ready, 1)
            ret_norm(0)
            ret_norm(1)
            root("ln_var", rstd[:, 0:S])
            V.tensor_tensor(conv_y[:], conv_y[:], over(rstd[:, 0:S], 4), ALU.mult).then_inc(conv_ready, 1)
            feed_behind("memk", 1)

            def ret_gate(g):
                after(ret_norm.done)
                o = o_ret[:, 2 * g:2 * g + 2]
                V.tensor_tensor(o, o, g_ret[:, 2 * g:2 * g + 2], ALU.mult).then_inc(ret_full, 1)

            def mix_lo(p):
                dve.wait_ge(mix_hi, p + 1)
                full = conv_y[:, 2 * p:2 * p + 2] if p < 2 else o_ret[:, 2 * p - 4:2 * p - 2]
                lo_part(mix, full, 2 * p, 2 * p + 2).then_inc(mix_ready, 1)

            wait_read(dve, "g", 1)
            ret_gate(0)
            ret_norm(2)
            mix_lo(0)
            ret_norm(3)
            mix_lo(1)
            dve.wait_ge(conv_ready, 3)
            ret_gate(1)
            mix_lo(2)
            mix_lo(3)
            for j in range(4):
                feed_fill("wout", j)
                feed_behind("wout", j)
            wait_read(dve, "wout", 3)
            post_norm("mix_post", "mix_post")
            feed_behind("memv", 0)
            norm_to_h("ffn_pre", "ffn_pre")
            feed_behind("memv", 1)
            def ff_lo(j):
                ff_lo.count += 1
                dve.wait_ge(f_hi, ff_lo.count)
                V.tensor_tensor(ff[:, 1, j], prod_tmp[:, j % 2], as_f32(ff[:, 0, j]), ALU.subtract).then_inc(ff_ready, 1)

            ff_lo.count = 0
            for j in range(23):
                if j < 22:
                    gates[0] += 1
                    feed_behind("ff", j)
                    wait_gate(gates[0])
                    if j >= 2:
                        dve.wait_ge(ff_ready, j - 1)
                    V.tensor_tensor(prod_tmp[:, j % 2], bank("ff", j)[:, 1], gate_tmp[:, gate_slot("ff", j), 0],
                                    ALU.mult).then_inc(freed["dve"], 1)
                if j:
                    ff_lo(j - 1)
            for j in range(4):
                feed_fill("down", j)
                feed_behind("down", j)
            wait_read(dve, "down", 3)
            post_norm("ffn_post", "ffn_post")
            for j in range(4):
                gates[0] += 1
                if j < 3:
                    feed_behind("ple", j)
                wait_gate(gates[0])
                dve.wait_ge(ple_proj, j + 1)
                V.tensor_tensor(y[:, 2 * j:2 * j + 2], gate_tmp[:, gate_slot("ple", j)], ple_p[:, 2 * j:2 * j + 2],
                                ALU.mult).then_inc(freed["dve"], 1)
            feed_behind("ple", 3)
            wait_read(dve, "ple", 3)
            dve.wait_ge(xs_ready, 4)
            post_norm("ple_post", "ple_post")
            norm_to_h("mix2", "norm_mix2")

            for d, (stage, f, k) in enumerate((("hff", f_f, k_f), ("hfb", f_b, k_b))):
                for j in range(4):
                    feed_fill(stage, j)
                    wait_read(dve, stage, j)
                    feed_behind(stage, j)
                    for t in (2 * j, 2 * j + 1):
                        c = d * 8 + t
                        V.tensor_scalar(k[:, t], k[:, t], lb[:, 5, c:c + 1], None, ALU.mult)
                        last = link(V.tensor_scalar(f[:, t], f[:, t], lb[:, 5, c:c + 1],
                                                    lb[:, 4, c:c + 1], ALU.mult, ALU.add))
                    after(last)
                    last = link(V.tensor_scalar(f[:, 2 * j:2 * j + 2], f[:, 2 * j:2 * j + 2], 1e-12, None, ALU.max))
            for j in range(4):
                feed_behind("hq", j)
            wait_read(dve, "hq", 3)
            after(link(V.tensor_scalar(q_s[:], q_s[:], float(P) ** -0.5, None, ALU.mult)))
            V.tensor_tensor(ksum[:], k_f, k_b, ALU.add)
            V.tensor_tensor(q_f, q_s[:], f_f[:], ALU.mult)
            V.tensor_tensor(q_b, q_s[:], f_b[:], ALU.mult).then_inc(level_ready, 1)
            dve.wait_ge(level_ready, 1)

            def masks(i):
                for g in range(4):
                    dve.wait_ge(sc_done, SC_LEVEL + 4 + 4 * (i + 1) + g + 1)
                    if i == 0:
                        dve.wait_ge(st_diag, g + 1)
                    m = mat("mask", i).bitcast(I32).unsqueeze(1).to_broadcast([P, 4, P])
                    dst = st_hg[:, 2 * g:2 * g + 2].rearrange("p a (b c) -> p (a b) c", c=P)
                    m2 = mat("mask", i).bitcast(I32).unsqueeze(1).to_broadcast([P, 2, P])
                    for a in range(2):
                        src = sc[g][:, a * 256:a * 256 + 256].rearrange("p (b c) -> p b c", b=2)
                        ins = V.copy_predicated(dst[:, 4 * a:4 * a + 4:3], m2, src)
                    ins.then_inc(st_mask, 1)

            def grow(i):
                b = LEVELS[i]

                def halves(t):
                    v = t.rearrange("p a s -> p (a s)").rearrange("p (n two b) -> p n two b", two=2, b=b)
                    return v[:, :, 0], v[:, :, 1]

                nb = HG * S // (2 * b)
                fa, fb_ = halves(f_f[:])
                ba, bb_ = halves(f_b[:])
                bc = lambda t: t[:, :, 0:1].to_broadcast([P, nb, b])
                qf, qb, kf, kb = halves(q_f)[1], halves(q_b)[0], halves(k_f)[0], halves(k_b)[1]
                V.tensor_tensor(qf, qf, bc(fa), ALU.mult)
                V.tensor_tensor(kf, kf, bc(fb_), ALU.mult)
                V.tensor_tensor(qb, qb, bc(bb_), ALU.mult)
                after(link(V.tensor_tensor(kb, kb, bc(ba), ALU.mult)))
                V.tensor_tensor(fa[:, :, 0:1], fa[:, :, 0:1], fb_[:, :, 0:1], ALU.mult)
                V.tensor_tensor(ba[:, :, 0:1], ba[:, :, 0:1], bb_[:, :, 0:1], ALU.mult).then_inc(level_ready, 1)
                dve.wait_ge(level_ready, i + 2)

            for e, (name, j) in enumerate(SIDE_FILLS):
                feed_behind(name, j)
                if e in LEVEL_AFTER:
                    masks(LEVEL_AFTER[e])
                    grow(LEVEL_AFTER[e])
                if e == CROSS_AFTER:
                    gated = []
                    for g in range(6):
                        if g < 4:
                            dve.wait_ge(o_copied, RET + g + 1)
                            o = o_hg[:, 2 * g:2 * g + 2]
                            gated.append(link(V.scalar_tensor_tensor(out=o, in0=o, scalar=col("gnorm"),
                                                                     in1=gate_hg[:, 2 * g:2 * g + 2],
                                                                     op0=ALU.mult, op1=ALU.mult)))
                        if 1 <= g < 5:
                            dve.wait_ge(hg_root, g)
                            root_g = hg_sq[:, 2 * g - 2:2 * g]
                            V.reciprocal(root_g, root_g).then_inc(hg_inv, 1)
                            dve.wait_ge(hg_inv, g)
                            after(gated[g - 1])
                            o = o_hg[:, 2 * g - 2:2 * g]
                            V.tensor_tensor(o, o, root_g, ALU.mult).then_inc(hg_out, 1)
                        if g >= 2:
                            dve.wait_ge(hg_hi, g - 1)
                            lo_part(o_hg_s, o_hg[:, 2 * g - 4:2 * g - 2], 2 * g - 4, 2 * g - 2).then_inc(hg_split, 1)

            def att_logits(a):
                par = a % 2
                dve.wait_ge(scored, a + 1)
                if a == CA:
                    dve.wait_ge(toep_sel, 2)
                if a >= 2:
                    dve.wait_ge(turned, a - 1)
                if HEADS[a][0] == "na":
                    for t in range(2):
                        d0 = (3 - 2 * t - 1) * 64
                        rows = lambda v: v.rearrange("p (r c) -> p r c", c=64)
                        n = link(V.scalar_tensor_tensor(out=rows(probs[:, par, t * S:t * S + S]),
                                                        in0=rows(sc[par][:, t * S:t * S + S]), scalar=64.0 ** -0.5,
                                                        in1=rows(toep_t[:, HEADS[a][1], d0:d0 + S])[:, :, ::-1],
                                                        op0=ALU.mult, op1=ALU.add))
                    after(n)
                    src, scale = probs[:, par], -1.0
                else:
                    src, scale = sc[par][:], -float(P) ** -0.5
                n = link(V.tensor_reduce(soft[:, par, 0], src.rearrange("p (t j) -> p t j", t=2), AX.X, ALU.max))
                after(n)
                V.tensor_scalar(soft[:, par, 0], soft[:, par, 0], scale, None, ALU.mult).then_inc(logits_ready, 1)

            def att_norm(a):
                par = a % 2
                dve.wait_ge(exp_ready, a + 1)
                after(link(V.reciprocal(soft[:, par, 2], soft[:, par, 1])))
                for t in range(2):
                    ins = V.tensor_scalar(probs[:, par, t * S:t * S + S], probs[:, par, t * S:t * S + S],
                                          soft[:, par, 2, t:t + 1], None, ALU.mult)
                ins.then_inc(p_ready, 1)

            def att_lo(a):
                kind, i = HEADS[a]
                if kind == "na" and i % 2 == 0:
                    return
                n = i if kind == "ca" else CA + i // 2
                o, t = (o_ca, i) if kind == "ca" else (o_na, i // 2)
                dve.wait_ge(o_att, n + 1)
                V.tensor_tensor(o[:, 1, t], sc[3][:, 0:S], as_f32(o[:, 0, t]), ALU.subtract).then_inc(att_ready, 1)

            def att_slot(i):
                if i < NHEADS:
                    att_logits(i)
                    att_norm(i)
                if 2 <= i < NHEADS + 2:
                    att_lo(i - 2)

            att_slot(0)

            def merge_lo(j):
                dve.wait_ge(merge_hi, j + 1)
                V.tensor_tensor(merged_s[:, 1, j], merged[:, j], as_f32(merged_s[:, 0, j]), ALU.subtract
                                ).then_inc(merge_ready, 1)

            added = {}
            for i, (name, j) in enumerate(MERGE_FILLS):
                gates[0] += 1
                feed_behind(name, j)
                wait_gate(gates[0])
                yv = bank(name, j)[:, 1]
                gv = gate_tmp[:, gate_slot(name, j), 0]
                if name == "mhg":
                    V.scalar_tensor_tensor(out=merged[:, j], in0=gv, scalar=1.0, in1=yv, op0=ALU.add,
                                           op1=ALU.mult).then_inc(freed["dve"], 1)
                else:
                    if i - 2 >= 16:
                        dve.wait_ge(merge_full, i - 2 - 16 + 1)
                    elif i - 2 >= 8:
                        after(added[i - 2])
                    V.scalar_tensor_tensor(out=prod_tmp[:, i % 2], in0=gv, scalar=1.0, in1=yv, op0=ALU.add,
                                           op1=ALU.mult).then_inc(freed["dve"], 1)
                    wait_read(dve, name, j)
                    if name == "mna":
                        after(added[i - 8])
                    ins = V.tensor_tensor(merged[:, j], merged[:, j], prod_tmp[:, i % 2], ALU.add)
                    if name == "mna":
                        ins.then_inc(merge_full, 1)
                    else:
                        added[i] = link(ins)
                if i >= 17:
                    merge_lo(i - 17)
                att_slot(i + 1)
            merge_lo(7)

            for j in range(4):
                feed_fill("wout2", j)
                dve.wait_ge(pe_step, fill_step(fi("wout2", j)))
                if j < 3:
                    feed_behind("wout2", j)
                xv = x[:, 2 * j:2 * j + 2]
                V.scalar_tensor_tensor(out=xv, in0=bank("wout2", j)[:], scalar=0.5, in1=xv, op0=ALU.mult,
                                       op1=ALU.add).then_inc(freed["dve"], 1)
            feed_behind("wout2", 3)
            norm_to_h("ffn2", "norm_ffn2")
            for j in range(24):
                if j < 22:
                    feed_behind("up", j)
                    dve.wait_ge(up_lin, j + 1)
                    b = bank("up", j)
                    for i in range(2):
                        t = gate_tmp[:, j % 2, i]
                        ct = 22 * i + j
                        n = link(V.scalar_tensor_tensor(out=t[:, 1:S], in0=b[:, i, 0:S - 1], scalar=col("conv_w", ct),
                                                        in1=t[:, 1:S], op0=ALU.mult, op1=ALU.add))
                    for i in range(2):
                        t = gate_tmp[:, j % 2, i]
                        ct = 22 * i + j
                        if i == 0:
                            after(n)
                        ins = V.scalar_tensor_tensor(out=t[:, 0:S - 1], in0=b[:, i, 1:S], scalar=col("conv_w", 88 + ct),
                                                     in1=t[:, 0:S - 1], op0=ALU.mult, op1=ALU.add)
                    ins.then_inc(freed["dve"], 1)
                if j >= 2:
                    ff_lo(j - 2)
                if 1 <= j <= 22:
                    i = j - 1
                    dve.wait_ge(gelu_done, i + 1)
                    if i >= 2:
                        dve.wait_ge(ff_ready, 22 + i - 1)
                    V.tensor_tensor(prod_tmp[:, i % 2], gate_tmp[:, i % 2, 0], gate_tmp[:, i % 2, 1], ALU.mult
                                    ).then_inc(up_full, 1)
            for j in range(4):
                feed_fill("down2", j)
                dve.wait_ge(pe_step, fill_step(fi("down2", j)))
                feed_behind("down2", j)
                V.tensor_tensor(x[:, 2 * j:2 * j + 2], x[:, 2 * j:2 * j + 2], bank("down2", j)[:], ALU.add
                                ).then_inc(freed["dve"], 1)
            root("final", rstd[:, 0:S])
            for t in range(KT):
                ins = V.scalar_tensor_tensor(out=y[:, t], in0=x[:, t], scalar=col("norm_final", t), in1=rstd[:, 0:S],
                                             op0=ALU.mult, op1=ALU.mult)
                if t % 2:
                    ins.then_inc(out_ready, 1)

        @block.tensor
        def _(pe):
            mm = nc.tensor.matmul
            at_block = [0]

            PASSES = ((0, 0), (0, 1), (1, 0))

            def take(count=1):
                b = at_block[0]
                at_block[0] += count
                u = b // UB
                if b % UB == 0:
                    pe.wait_ge(lo_ready[LO_ENGINE[u]], lo_count(u, LO_ENGINE[u]))
                if count == 1:
                    return [w[:, u % UNITS, b % UB] for w in (w_hi, w_lo)]
                return [w[:, u % UNITS, b % UB:b % UB + count].rearrange("p a b -> p (a b)") for w in (w_hi, w_lo)]

            def step(ins, end):
                if end in STEP:
                    ins.then_inc(pe_step, 1)

            def open_fill(name, j):
                n = fi(name, j)
                if n >= PJ:
                    who = FILLS[n - PJ][3]
                    pe.wait_ge(freed[who], freed_count(n - PJ, who))
                assert at_block[0] == FIRST_BLOCK[n]
                return pj[n % PJ]

            def tile_out(dst, src, kts=KT, ready=None):
                for kt in range(kts):
                    w = take()
                    if ready is not None:
                        ready(kt)
                    for i, (a, b) in enumerate(PASSES):
                        last = mm(dst, w[a], src[:, b, kt], start=kt == 0 and i == 0, stop=kt == kts - 1 and i == 2)
                    step(last, at_block[0])

            def pair(name, j, src, kts=KT, ready=None):
                b = open_fill(name, j)
                tile_out(b[:, 0], src, kts, ready if j == 0 else None)
                tile_out(b[:, 1], src, kts)

            def token_pair(name, j, src):
                b = open_fill(name, j)
                start = at_block[0]
                ws = [take(2) for _ in range(KT)]
                for tt in range(2):
                    for kt in range(KT):
                        for i, (wa, xa) in enumerate(PASSES):
                            last = mm(b[:, tt], src[:, xa, kt, tt * P:tt * P + P], ws[kt][wa],
                                      start=kt == 0 and i == 0, stop=kt == KT - 1 and i == 2)
                        if tt == 1:
                            step(last, start + 2 * kt + 2)

            def h_pairs(name):
                def ready(kt):
                    if kt % 2 == 0:
                        pe.wait_ge(h_ready, H_PAIRS[name] + kt // 2 + 1)
                return ready

            def wait_stat(name):
                if STAT[name]:
                    pe.wait_ge(stat_read, STAT[name])

            def norm_stat(name, chunks, matrix="m1024", src=None):
                wait_stat(name)
                for c in range(chunks):
                    stat_chunk(name, c, chunks, matrix)

            def stat_chunk(name, c, chunks, matrix="m1024"):
                if c == 0:
                    wait_stat(name)
                pe.wait_ge(sq_ready, SQ_BEFORE[name] + c + 1)
                per = KT // chunks
                for t in range(c * per, c * per + per):
                    last = mm(st[:, 0:S], mat(matrix), sq[:, t], start=t == 0, stop=t == KT - 1)
                if c == chunks - 1:
                    last.then_inc(stat_done, 1)

            def warm(n):
                for _ in range(4 * n):
                    mm(sc[0][:, 0:P], mat("m1024"), mat("m1024"), start=True, stop=True)

            pe.wait_ge(load_mean, 16)
            warm(1)
            norm_stat("mix_pre", 2)
            warm(4)
            pe.wait_ge(load_params, 32)
            for j in range(4):
                pair("conv", j, h, ready=h_pairs("mix_pre"))
                if j == 0:
                    norm_stat("mem", 2)
            for j in range(4):
                pair("qk", j, h)
            for j in range(2):
                token_pair("v", j, h)
            for j in range(2):
                pair("g", j, h)
            pe.wait_ge(mem_ready, 4)
            pair("memk", 0, mem_n)
            pe.wait_ge(rope_ready, 2)
            for hd in range(RET):
                mm(sc[hd][:, 0:S], k_raw[:, hd, 0:P], q_raw[:, hd, :], start=True, stop=True)
                mm(sc[hd][:, S:S + P], k_raw[:, hd, P:S], q_raw[:, hd, P:S], start=True, stop=True
                   ).then_inc(sc_done, 1)
            pair("memk", 1, mem_n)
            for hd in range(RET):
                pe.wait_ge(s_ready, hd + 1)
                mm(sc[hd][:, 0:S], v_ret[:, 0, hd * P:hd * P + P], s_ret[:, hd, 0:S], start=True, stop=False)
                mm(sc[hd][:, P:S], v_ret[:, 1, hd * P:hd * P + P], s_ret[:, hd, S:S + P], start=False, stop=True
                   ).then_inc(sc_done, 1)
            for hd in range(RET):
                pe.wait_ge(ret_squares, hd + 1)
                pe.wait_ge(o_copied, hd + 1)
                mm(sc[hd][:, 0:S], mat("m128"), sq[:, 4 + hd], start=True, stop=True).then_inc(ret_stat, 1)
            pe.wait_ge(conv_ready, 1)
            wait_stat("ln_mean")
            for t in range(4):
                last = mm(st[:, 0:S], mat("m512"), conv_y[:, t], start=t == 0, stop=t == 3)
            last.then_inc(stat_done, 1)
            pe.wait_ge(ret_root, RET)
            warm(3)
            pe.wait_ge(conv_ready, 2)
            wait_stat("ln_var")
            pe.wait_ge(sq_ready, SQ_BEFORE["ln_var"] + 1)
            for t in range(4):
                last = mm(st[:, 0:S], mat("m512"), sq[:, t], start=t == 0, stop=t == 3)
            last.then_inc(stat_done, 1)
            warm(9)
            for j in range(4):
                pair("wout", j, mix, ready=lambda kt: pe.wait_ge(mix_ready, kt // 2 + 1))
                if j:
                    stat_chunk("mix_post", j - 1, 4)
            stat_chunk("mix_post", 3, 4)
            token_pair("memv", 0, mem_n)
            norm_stat("ffn_pre", 4)
            token_pair("memv", 1, mem_n)
            for j in range(22):
                pair("ff", j, h, ready=h_pairs("ffn_pre"))
            for j in range(4):
                pair("down", j, ff, FT, ready=lambda kt: pe.wait_ge(ff_ready, kt + 1))
                if j:
                    stat_chunk("ffn_post", j - 1, 4)
            stat_chunk("ffn_post", 3, 4)
            pe.wait_ge(load_ple, 32)
            for j in range(4):
                for i in range(2):
                    for kt in range(2):
                        last = mm(sc[j][:, i * S:i * S + S], w_ple[:, kt, (2 * j + i) * P:(2 * j + i + 1) * P],
                                  p_in[:, kt], start=kt == 0, stop=kt == 1)
                last.then_inc(sc_done, 1)
            for j in range(4):
                pair("ple", j, x_split, ready=lambda kt: pe.wait_ge(xs_ready, kt // 2 + 1))
                if j:
                    stat_chunk("ple_post", j - 1, 4)
            stat_chunk("ple_post", 3, 4)
            warm(5)
            norm_stat("mix2", 4)
            warm(4)

            for stage in ("hff", "hfb", "hq"):
                for j in range(4):
                    pair(stage, j, h, ready=h_pairs("mix2") if stage == "hff" else None)

            def tile(t, hd, tt):
                return t[:, hd, tt * P:tt * P + P]

            def diagonal():
                pe.wait_ge(level_ready, 1)
                pe.wait_ge(ple_proj, 4)
                for g in range(4):
                    for a in range(2):
                        for tt in range(2):
                            c = (2 * a + tt) * P
                            last = mm(sc[g][:, c:c + P], tile(ksum, 2 * g + a, tt), tile(q_s, 2 * g + a, tt),
                                      start=True, stop=True)
                    last.then_inc(sc_done, 1)

            def level(i):
                b = LEVELS[i]
                pe.wait_ge(level_ready, i + 1)
                for g in range(4):
                    pe.wait_ge(mix_keys, 2 * i + g // 2 + 1)
                    if i == 0:
                        pe.wait_ge(st_diag, g + 1)
                    else:
                        pe.wait_ge(st_mask, 4 * (i - 1) + g + 1)
                    for a in range(2):
                        for tt in range(2):
                            c = (2 * a + tt) * P
                            q = partners(q_bf[:, 0, 2 * g + a, tt * P:tt * P + P], b)
                            last = mm(sc[g][:, c:c + P], tile(k_mix[g // 2], 2 * (g % 2) + a, tt), q,
                                      start=True, stop=True)
                    last.then_inc(sc_done, 1)

            def cross():
                pe.wait_ge(level_ready, 1 + len(LEVELS))
                for g in range(4):
                    pe.wait_ge(st_mask, 4 * (len(LEVELS) - 1) + g + 1)
                    for a in range(2):
                        hd = 2 * g + a
                        mm(sc[g][:, a * S:a * S + P], tile(k_f, hd, 0), tile(q_f, hd, 1), start=True, stop=True)
                        last = mm(sc[g][:, a * S + P:a * S + S], tile(k_b, hd, 1), tile(q_b, hd, 0),
                                  start=True, stop=True)
                    last.then_inc(sc_done, 1)

            def hg_values():
                for g in range(5):
                    if g < 4:
                        pe.wait_ge(st_cross, g + 1)
                        for a in range(2):
                            hd = 2 * g + a
                            o = sc[g][:, a * S:a * S + S]
                            mm(o, v_hg[:, 0, hd * P:hd * P + P], st_hg[:, hd, 0:S], start=True, stop=False)
                            last = mm(o, v_hg[:, 1, hd * P:hd * P + P], st_hg[:, hd, S:2 * S], start=False, stop=True)
                        last.then_inc(sc_done, 1)
                    if g:
                        pe.wait_ge(hg_squares, g)
                        pe.wait_ge(o_copied, RET + g)
                        for a in range(2):
                            last = mm(sc[g - 1][:, a * S:a * S + S], mat("m128"), hg_sq[:, 2 * (g - 1) + a],
                                      start=True, stop=True)
                        last.then_inc(hg_stat, 1)

            for e, (name, j) in enumerate(SIDE_FILLS):
                if name in ("hi", "nv"):
                    token_pair(name, j, h)
                else:
                    pair(name, j, h)
                if e == DIAGONAL_AFTER:
                    diagonal()
                if e in LEVEL_AFTER:
                    level(LEVEL_AFTER[e])
                if e == CROSS_AFTER:
                    cross()
                    wait_read(pe, "hi", 3)
                    hg_values()

            def att_scores(a):
                kind, i = HEADS[a]
                if a < 2:
                    pe.wait_ge(hg_root, 4)
                    wait_read(pe, "cq", 1)
                else:
                    pe.wait_ge(exp_ready, a - 1)
                for t in range(2):
                    o = sc[a % 2][:, t * S:t * S + S]
                    if kind == "na":
                        lo = 64 * (i % 2)
                        last = mm(o, q_na[lo:lo + 64, i // 2, t * P:t * P + P], k_na[lo:lo + 64, i // 2, :],
                                  start=True, stop=True)
                    else:
                        last = mm(o, q_ca[:, i, t * P:t * P + P], mem_k[:, i, :], start=True, stop=True)
                last.then_inc(scored, 1)

            def att_transpose(a):
                pe.wait_ge(p_ready, a + 1)
                if a:
                    pe.wait_ge(pt_ready, a)
                for jt in range(2):
                    for t in range(2):
                        last = nc.tensor.transpose(sc[2][:, jt * S + t * P:jt * S + t * P + P],
                                                   probs[:, a % 2, t * S + jt * P:t * S + jt * P + P],
                                                   mat("ident"))
                last.then_inc(turned, 1)

            def att_values(a):
                pe.wait_ge(pt_ready, a + 1)
                kind, i = HEADS[a]
                if kind == "na":
                    if i % 2 == 0:
                        pe.wait_ge(att_ready, CA + i // 2)
                    o = sc[3][64 * (i % 2):64 * (i % 2) + 64, 0:S]
                    v = v_na[:, :, i * 64:i * 64 + 64]
                else:
                    if i:
                        pe.wait_ge(att_ready, i)
                    o = sc[3][:, 0:S]
                    v = mem_v[:, :, i * P:(i + 1) * P]
                for jt in range(2):
                    last = mm(o, v[:, jt], probs_t[:, a % 2, jt * S:jt * S + S], start=jt == 0, stop=jt == 1)
                last.then_inc(pv_done, 1)

            def att_slot(i):
                if i < NHEADS:
                    att_scores(i)
                if 1 <= i <= NHEADS:
                    att_transpose(i - 1)
                if 2 <= i < NHEADS + 2:
                    att_values(i - 2)

            att_slot(0)
            for i, (name, j) in enumerate(MERGE_FILLS):
                b = open_fill(name, j)
                tile_out(b[:, 0], h)
                if name == "mhg":
                    tile_out(b[:, 1], o_hg_s, ready=lambda kt: pe.wait_ge(hg_split, kt // 2 + 1))
                elif name == "mca":
                    pe.wait_ge(att_ready, 4)
                    tile_out(b[:, 1], o_ca, 4)
                else:
                    pe.wait_ge(att_ready, 8)
                    tile_out(b[:, 1], o_na, 4)
                att_slot(i + 1)
            for j in range(4):
                pair("wout2", j, merged_s, ready=lambda kt: pe.wait_ge(merge_ready, kt + 1))
            norm_stat("ffn2", 4)
            warm(4)
            for j in range(22):
                pair("up", j, h, ready=h_pairs("ffn2"))
            for j in range(4):
                pair("down2", j, ff, FT, ready=lambda kt: pe.wait_ge(ff_ready, FT + kt + 1))
            norm_stat("final", 4)


def host_layout(inputs):
    f = np.float32

    def blocks(w, cols):
        k = w.shape[0] // P
        return [[w[kt * P:(kt + 1) * P, m * P:(m + 1) * P] for kt in range(k)] for m in cols]

    def token_blocks(w, pairs):
        k = w.shape[0] // P
        return [[w[kt * P:(kt + 1) * P, m * P:(m + 1) * P] for kt in range(k) for m in (2 * q, 2 * q + 1)]
                for q in pairs]

    def vecs(a, tiles):
        return np.asarray(a, f).reshape(-1, tiles, P).transpose(2, 0, 1).reshape(P, -1)

    g = {k: np.asarray(v) for k, v in inputs.items()}
    w_in, w_in2 = g["w_in"][0], g["w_in_2"][0]
    stream = []

    def add(*tiles):
        for t in tiles:
            stream.extend(t)

    a = blocks(w_in, range(24))
    for j in range(4):
        add(a[j], a[4 + j])
    add(*a[8:16], *token_blocks(w_in, (8, 9)), *a[20:24])
    w_kv = g["w_mem_kv_2"][0]
    add(*blocks(w_kv, range(4)))
    add(*blocks(g["w_out"][0], range(8)))
    add(*token_blocks(w_kv, (2, 3)))
    gate, up = blocks(g["w_ffn_gate"][0], range(FT)), blocks(g["w_ffn_up"][0], range(FT))
    for j in range(FT):
        add(gate[j], up[j])
    add(*blocks(g["w_ffn_down"][0], range(8)))
    add(*blocks(g["w_ple_gate"][0], range(8)))
    b = blocks(w_in2, range(80))
    add(*b[16:32], *b[0:8], *token_blocks(w_in2, range(4, 8)), *b[32:40], *b[40:48],
        *token_blocks(w_in2, (24, 25)), *b[52:56])
    for base, w in ((56, g["w_hg_o_2"][0]), (72, g["w_ca_o_2"][0]), (64, g["w_na_o_2"][0])):
        o = blocks(w, range(8))
        for j in range(8):
            add(b[base + j], o[j])
    add(*blocks(g["w_out_2"][0], range(8)))
    u = blocks(g["w_up_2"][0], range(2 * FT))
    for j in range(FT):
        add(u[j], u[FT + j])
    add(*blocks(g["w_down_2"][0], range(8)))
    assert len(stream) == NBLOCKS, (len(stream), NBLOCKS)
    wstream = np.empty((NSLOTS, P, 16, P), f)
    for n, blk in enumerate(stream):
        wstream[n // 16, :, n % 16] = blk

    vec = np.concatenate([
        vecs(g["mix_pre_norm"], 8), vecs(g["conv_dw_w"][0], 4), vecs(g["conv_dw_b"], 4), vecs(g["conv_ln_w"], 4),
        vecs(g["conv_ln_b"], 4), vecs(g["mix_post_norm"], 8), vecs(g["ffn_pre_norm"], 8),
        vecs(g["ffn_post_norm"], 8), vecs(g["ple_post_norm"], 8), vecs(g["norm_mix_2"], 8),
        vecs(g["hg_lb_logits_2"][0], 8), vecs(g["hg_gnorm_2"], 1), vecs(g["mem_norm_2"], 8),
        vecs(g["norm_ffn_2"], 8), vecs(g["conv_w_2"][0], 44), vecs(g["conv_b_2"], 44),
        vecs(g["norm_final_2"], 8)], axis=1)
    assert vec.shape == (P, NVEC)

    idx = np.arange(P)
    con = [np.full((P, P), 1.0 / n, f) for n in (1024, 512, 128)] + [np.eye(P, dtype=f)]
    for b_ in LEVELS:
        same = (idx[:, None] // (2 * b_)) == (idx[None, :] // (2 * b_))
        apart = (idx[:, None] // b_) != (idx[None, :] // b_)
        con.append((same & apart).astype(f))
    con = np.concatenate(con, axis=1)
    half = P // 2
    freqs = (10000.0 ** (-np.arange(half, dtype=f) / half)).astype(f)
    ang = (np.arange(S, dtype=f)[None, :] * freqs[:, None]).astype(f).astype(np.float64)
    cos, sin = np.cos(ang).astype(f), np.sin(ang).astype(f)
    rope = np.stack([np.concatenate([cos, cos]), np.concatenate([sin, -sin])], axis=1)
    decay = np.zeros((P, RET, 384), np.float64)
    rel = (np.arange(S)[None, :] - idx[:, None]).astype(np.float64)
    for hd in range(RET):
        lg = np.float64(np.log(f(1.0 - 2.0 ** (-5.0 - hd))))
        d = np.where(rel >= 0, np.exp(lg * np.maximum(rel, 0.0)), 0.0) * float(P) ** -0.5
        decay[:, hd, 0:S] = d
        decay[:, hd, S:] = d[:, 0:P]

    def act_t(a, tiles):
        return np.ascontiguousarray(a.reshape(S, tiles, P).transpose(2, 1, 0))

    return {
        "xt": act_t(g["x"], 8), "memt": act_t(g["mem_2"], 8), "pt": act_t(g["p"], 2),
        "wstream": wstream,
        "wproj": np.ascontiguousarray(g["w_ple_proj"][0].reshape(2, P, D).transpose(1, 0, 2)),
        "vecs": np.ascontiguousarray(vec), "consts": np.ascontiguousarray(con, dtype=f),
        "rope_tab": np.ascontiguousarray(rope, dtype=f), "decay_tab": decay.astype(f),
        "rpb": np.ascontiguousarray(g["na_rpb_2"][0].reshape(NA * 15, 31)[:, ::-1]),
    }


def kernel(**inputs):
    import concourse.bacc as bacc
    from concourse.bass_utils import run_bass_kernel_spmd

    arrays = host_layout(inputs)
    nc = bacc.Bacc("TRN2", target_bir_lowering=False, num_devices=1)
    args = {k: nc.dram_tensor(k, v.shape, F32, kind="ExternalInput").ap() for k, v in arrays.items()}
    out = nc.dram_tensor("out_t", (P, KT, S), F32, kind="ExternalOutput").ap()
    toep = nc.dram_tensor("toep", (NA * 15, P), F32, kind="Internal").ap()
    program(nc, out=out, toep=toep, **args)
    r = run_bass_kernel_spmd(nc, [arrays], core_ids=[0])
    got = r.results[0]["out_t"]
    return np.ascontiguousarray(got.transpose(2, 1, 0)).reshape(1, S, D)
```
